# Optimizing a Trainium2 kernel written in Bass

```python
import jax, jax.numpy as jnp
from jax import lax
import numpy as np

D_MODEL = 1024
BATCH = 1
SEQ = 1024
DEPTH = 2

HEAD_DIM = 64
N_MLSTM_HEADS = D_MODEL // (2 * HEAD_DIM)
N_SB_HEADS = D_MODEL // (2 * HEAD_DIM)
D_MLSTM = N_MLSTM_HEADS * HEAD_DIM
D_SB = N_SB_HEADS * HEAD_DIM
D_MIX = D_MLSTM + D_SB
D_FF = 4 * D_MODEL
CONV_WIDTH = 4
MLSTM_CHUNK = 64
SB_BLOCK = 128
NORM_EPS = 1e-6
D_IN_PROJ = 4 * D_MLSTM + 2 * N_MLSTM_HEADS + 3 * D_SB

kernel_name = "hymba_mlstm_stickbreaking_trunk"

def _rmsnorm(x, g):
    xf = x.astype(jnp.float32)
    y = xf * lax.rsqrt(jnp.mean(xf * xf, axis=-1, keepdims=True) + NORM_EPS)
    return y * g.astype(jnp.float32)

def _head_rmsnorm(y, g):
    B, S, H, d = y.shape
    return _rmsnorm(y, g.reshape(H, d))

def _causal_depthwise_conv(u, w, b):
    S = u.shape[1]
    up = jnp.pad(u, ((0, 0), (CONV_WIDTH - 1, 0), (0, 0)))
    y = b
    for j in range(CONV_WIDTH):
        y = y + up[:, j:j + S, :] * w[j]
    return y

def _to_heads(a, H):
    B, S, _ = a.shape
    return a.reshape(B, S, H, HEAD_DIM).transpose(0, 2, 1, 3).astype(jnp.float32)

def _mlstm_chunkwise(q, k, v, i_pre, f_pre):
    B, H, S, d = q.shape
    L = MLSTM_CHUNK
    nc = S // L
    q = q * (d ** -0.5)
    logf = jax.nn.log_sigmoid(f_pre)

    def to_chunks(a):
        return jnp.moveaxis(a.reshape(B, H, nc, L, *a.shape[3:]), 2, 0)

    tri = jnp.tril(jnp.ones((L, L), dtype=bool))

    def step(carry, inp):
        C, n, m_prev = carry
        qc, kc, vc, ic, fc = inp
        b = jnp.cumsum(fc, axis=-1)
        Dlog = jnp.where(tri, b[..., :, None] - b[..., None, :] + ic[..., None, :], -jnp.inf)
        m_inter = b + m_prev[..., None]
        m = jnp.maximum(m_inter, jnp.max(Dlog, axis=-1))
        W = jnp.exp(Dlog - m[..., None]) * jnp.einsum('bhtd,bhsd->bhts', qc, kc)
        s_inter = jnp.exp(m_inter - m)
        num = s_inter[..., None] * jnp.einsum('bhtk,bhkv->bhtv', qc, C) + jnp.einsum('bhts,bhsv->bhtv', W, vc)
        den = s_inter * jnp.einsum('bhtk,bhk->bht', qc, n) + jnp.sum(W, axis=-1)
        h = num / jnp.maximum(jnp.abs(den), jnp.exp(-m))[..., None]
        b_last = b[..., -1]
        g = b_last[..., None] - b + ic
        m_new = jnp.maximum(b_last + m_prev, jnp.max(g, axis=-1))
        decay = jnp.exp(b_last + m_prev - m_new)
        w_s = jnp.exp(g - m_new[..., None])
        C_new = decay[..., None, None] * C + jnp.einsum('bhs,bhsk,bhsv->bhkv', w_s, kc, vc)
        n_new = decay[..., None] * n + jnp.einsum('bhs,bhsk->bhk', w_s, kc)
        return (C_new, n_new, m_new), h

    init = (jnp.zeros((B, H, d, d), jnp.float32), jnp.zeros((B, H, d), jnp.float32),
            jnp.zeros((B, H), jnp.float32))
    _, hs = lax.scan(step, init, (to_chunks(q), to_chunks(k), to_chunks(v), to_chunks(i_pre), to_chunks(logf)))
    return jnp.moveaxis(hs, 0, 2).reshape(B, H, S, d)

def _stick_breaking(q, k, v):
    B, H, S, d = q.shape
    scale = d ** -0.5
    outs = []
    for blk in range(S // SB_BLOCK):
        t0 = blk * SB_BLOCK
        t1 = t0 + SB_BLOCK
        qb = q[:, :, t0:t1]
        kb = k[:, :, :t1]
        vb = v[:, :, :t1]
        z = jnp.einsum('bhtd,bhsd->bhts', qb, kb) * scale
        causal = jnp.arange(t1)[None, :] < (t0 + jnp.arange(SB_BLOCK))[:, None]
        log_1m_beta = jnp.where(causal, jax.nn.log_sigmoid(-z), 0.0)
        after = lax.cumsum(log_1m_beta, axis=3, reverse=True) - log_1m_beta
        A = jnp.where(causal, jnp.exp(jax.nn.log_sigmoid(z) + after), 0.0)
        outs.append(jnp.einsum('bhts,bhsv->bhtv', A, vb))
    return jnp.concatenate(outs, axis=2)

def setup_inputs(seed: int = 0) -> dict:
    key = jax.random.key(seed)
    ks = jax.random.split(key, 15)
    f32 = jnp.float32
    x = jax.random.normal(ks[0], (BATCH, SEQ, D_MODEL), f32)
    attn_norm_g = 1.0 + 0.02 * jax.random.normal(ks[1], (DEPTH, D_MODEL), f32)
    w_in = jax.random.normal(ks[2], (DEPTH, D_MODEL, D_IN_PROJ), f32) * D_MODEL ** -0.5
    conv_w = jax.random.normal(ks[3], (DEPTH, CONV_WIDTH, 2 * D_MLSTM), f32) * CONV_WIDTH ** -0.5
    conv_b = 0.02 * jax.random.normal(ks[4], (DEPTH, 2 * D_MLSTM), f32)
    b_igate = 0.1 * jax.random.normal(ks[5], (DEPTH, N_MLSTM_HEADS), f32)
    b_fgate = jnp.linspace(3.0, 6.0, N_MLSTM_HEADS, dtype=f32)[None, :] + 0.1 * jax.random.normal(ks[6], (DEPTH, N_MLSTM_HEADS), f32)
    q_norm_g = 1.0 + 0.02 * jax.random.normal(ks[7], (DEPTH, HEAD_DIM), f32)
    k_norm_g = 1.0 + 0.02 * jax.random.normal(ks[8], (DEPTH, HEAD_DIM), f32)
    out_norm_g = 1.0 + 0.02 * jax.random.normal(ks[9], (DEPTH, D_MIX), f32)
    w_out = jax.random.normal(ks[10], (DEPTH, D_MIX, D_MODEL), f32) * D_MIX ** -0.5
    mlp_norm_g = 1.0 + 0.02 * jax.random.normal(ks[11], (DEPTH, D_MODEL), f32)
    w_up = jax.random.normal(ks[12], (DEPTH, D_MODEL, D_FF), f32) * D_MODEL ** -0.5
    w_down = jax.random.normal(ks[13], (DEPTH, D_FF, D_MODEL), f32) * D_FF ** -0.5
    return {"x": x, "attn_norm_g": attn_norm_g, "w_in": w_in, "conv_w": conv_w, "conv_b": conv_b,
            "b_igate": b_igate, "b_fgate": b_fgate, "q_norm_g": q_norm_g, "k_norm_g": k_norm_g,
            "out_norm_g": out_norm_g, "w_out": w_out, "mlp_norm_g": mlp_norm_g, "w_up": w_up, "w_down": w_down}

def reference(x, attn_norm_g, w_in, conv_w, conv_b, b_igate, b_fgate, q_norm_g, k_norm_g,
              out_norm_g, w_out, mlp_norm_g, w_up, w_down):
    B, S, _ = x.shape
    o_qk, o_v, o_o, o_i, o_f = 0, 2 * D_MLSTM, 3 * D_MLSTM, 4 * D_MLSTM, 4 * D_MLSTM + N_MLSTM_HEADS
    o_sb = 4 * D_MLSTM + 2 * N_MLSTM_HEADS
    for l in range(DEPTH):
        h = _rmsnorm(x, attn_norm_g[l]).astype(x.dtype)
        p = h @ w_in[l]
        qk_m = jax.nn.silu(_causal_depthwise_conv(p[..., o_qk:o_v], conv_w[l], conv_b[l]))
        q_m = _to_heads(qk_m[..., :D_MLSTM], N_MLSTM_HEADS)
        k_m = _to_heads(qk_m[..., D_MLSTM:], N_MLSTM_HEADS)
        v_m = _to_heads(p[..., o_v:o_o], N_MLSTM_HEADS)
        o_gate = jax.nn.sigmoid(p[..., o_o:o_i].astype(jnp.float32))
        i_pre = (p[..., o_i:o_f] + b_igate[l]).astype(jnp.float32).transpose(0, 2, 1)
        f_pre = (p[..., o_f:o_sb] + b_fgate[l]).astype(jnp.float32).transpose(0, 2, 1)
        y_m = _mlstm_chunkwise(q_m, k_m, v_m, i_pre, f_pre).transpose(0, 2, 1, 3)
        y_m = _head_rmsnorm(y_m, out_norm_g[l, :D_MLSTM]).reshape(B, S, D_MLSTM) * o_gate
        q_s = _rmsnorm(_to_heads(p[..., o_sb:o_sb + D_SB], N_SB_HEADS), q_norm_g[l])
        k_s = _rmsnorm(_to_heads(p[..., o_sb + D_SB:o_sb + 2 * D_SB], N_SB_HEADS), k_norm_g[l])
        v_s = _to_heads(p[..., o_sb + 2 * D_SB:], N_SB_HEADS)
        y_s = _stick_breaking(q_s, k_s, v_s).transpose(0, 2, 1, 3)
        y_s = _head_rmsnorm(y_s, out_norm_g[l, D_MLSTM:]).reshape(B, S, D_SB)
        y = jnp.concatenate([y_m, y_s], axis=-1).astype(x.dtype)
        x = x + y @ w_out[l]
        h = _rmsnorm(x, mlp_norm_g[l]).astype(x.dtype)
        x = x + jnp.square(jax.nn.relu(h @ w_up[l])) @ w_down[l]
    return x


_drawn_inputs = setup_inputs


def setup_inputs(seed=0):
    import zlib

    import numpy as np

    out = dict(_drawn_inputs(seed))
    spreads = {}
    factors = {'conv_b': 5.895,
     'b_igate': 64.0,
     'q_norm_g': 8.0,
     'k_norm_g': 7.894,
     'out_norm_g': 3.326,
     'mlp_norm_g': 2.768}
    for name, (base, spread) in spreads.items():
        noise = np.random.default_rng([zlib.crc32(name.encode()), seed]).standard_normal(out[name].shape)
        drawn = base * np.exp(spread * noise) if base else spread * noise
        out[name] = __import__('jax').numpy.asarray(drawn.astype(out[name].dtype))
    for name, factor in factors.items():
        out[name] = (out[name] * factor).astype(out[name].dtype)
    return out
```

```python
from contextlib import ExitStack

import concourse.bass as bass
from concourse import mybir

F32 = mybir.dt.float32
F32R = mybir.dt.float32r
BF16 = mybir.dt.bfloat16
I32 = mybir.dt.int32
ALU = mybir.AluOpType
ACT = mybir.ActivationFunctionType
AX = mybir.AxisListType

P = 128
EPS = 1e-6
NO_SIGN = 0x7FFFFFFF
MASKED = -float(2 ** 100)


def trunk(nc, x, attn_norm_g, w_in, conv_w, conv_b, b_igate, b_fgate, q_norm_g, k_norm_g,
          out_norm_g, w_out, mlp_norm_g, w_up, w_down, out):
    _, SEQ, D = x.shape
    DEPTH = w_in.shape[0]
    HD = q_norm_g.shape[1]
    NH = b_igate.shape[1]
    DH = NH * HD
    FF = w_up.shape[2]
    CW = conv_w.shape[1]
    TT = SEQ // P
    KT = D // P
    NPAIR = NH // 2
    HALF = 512
    SLOTS = 4
    GROUP = 2
    NG = FF // (GROUP * P)
    O_SB = 4 * DH + 2 * NH
    CH = NH * TT
    VW = HD + 1
    QSC = float(HD) ** -0.5
    SBLK = HALF // P
    assert SEQ == 2 * HALF and KT == 8 and TT == 8 and CH == 64 and HD == 64

    OUT_USES = KT // SLOTS
    STICK_SLOTS = 3
    uses_m = [NPAIR] * SLOTS
    uses_s = [NPAIR if s < STICK_SLOTS else 0 for s in range(SLOTS)]
    uses_layer = [uses_m[s] + uses_s[s] + OUT_USES + NG for s in range(SLOTS)]

    resid_d = nc.dram_tensor("resid_scratch", (SEQ, D), F32, kind="Internal").ap()
    rows_d = nc.dram_tensor("rows_scratch", (CH, P + 1), F32, kind="Internal").ap()
    xin_v = x[0].rearrange("(t p) f -> p t f", p=P)
    out_v = out[0].rearrange("(t p) f -> p t f", p=P)
    resid_v = resid_d.rearrange("(t p) f -> p t f", p=P)

    ctx = ExitStack()
    with ctx:
        def sb(stack, name, shape, dt=F32):
            return stack.enter_context(nc.sbuf_tensor(name, shape, dt))

        def sem(name):
            return ctx.enter_context(nc.semaphore(name))

        ident = sb(ctx, "ident", [P, P])
        ident_b = sb(ctx, "ident_b", [P, P], BF16)
        after_mask = sb(ctx, "after_mask", [P, P], BF16)
        tri_f = sb(ctx, "tri_f", [P, P])
        suffix = sb(ctx, "suffix", [P, P], F32R)
        minus_ones = sb(ctx, "minus_ones", [P, P])
        head_ones = sb(ctx, "head_ones", [P, P])
        eps_c = sb(ctx, "eps_c", [P, 2])
        small_rows = sb(ctx, "small_rows", [P, P])
        small_cols = sb(ctx, "small_cols", [P, P])
        gate_bias = sb(ctx, "gate_bias", [P, 2 * NH])
        a_col = sb(ctx, "a_col", [P, CH])
        floor_col = sb(ctx, "floor_col", [P, CH])
        act_t = sb(ctx, "act_t", [P, 2, KT, SEQ], F32R)
        resid = sb(ctx, "resid", [P, TT, D])
        raw = sb(ctx, "raw", [P, SLOTS, KT * P])
        spl = sb(ctx, "spl", [P, SLOTS, 2, KT * P], F32R)
        gain = sb(ctx, "gain", [P, D])
        turned = sb(ctx, "turned", [P, 2, D])
        ssq = sb(ctx, "ssq", [P, 2])
        rst = sb(ctx, "rst", [P, 2])
        psum = [ctx.enter_context(nc.psum_tensor(f"bank{i}", [P, 512], F32)) for i in range(8)]

        with ExitStack() as s:
            wg_raw = sb(s, "wg_raw", [P, KT, 2 * NH])
            wg = sb(s, "wg", [P, 2, KT, 2 * NH], F32R)
            gsb = sb(s, "gsb", [P, TT, 2 * NH])
            glog = sb(s, "glog", [P, TT, NH])
            gabs = sb(s, "gabs", [P, TT, NH])
            gi = sb(s, "gi", [P, TT, NH])
            brow = sb(s, "brow", [CH, P])
            arow = sb(s, "arow", [CH, P])
            cmax = sb(s, "cmax", [CH, 2, P + 64])
            lastv = sb(s, "lastv", [1, 2, CH])
            mprev = sb(s, "mprev", [1, CH])
            mpcol = sb(s, "mpcol", [CH, 1])
            nrow = sb(s, "nrow", [CH, P + 1])
            frow = sb(s, "frow", [CH, P])
        with ExitStack() as s:
            pre = sb(s, "pre", [P, CW - 1 + SEQ])
            qm = sb(s, "qm", [P, SEQ])
            km = sb(s, "km", [P, SEQ])
            sig = sb(s, "sig", [P, SEQ])
            qs = sb(s, "qs", [P, TT, P])
            vm = sb(s, "vm", [P, TT, 2, VW])
            og = sb(s, "og", [P, TT, P])
            nm = sb(s, "nm", [P, TT, 2, P + 1])
            kw = sb(s, "kw", [P, TT, P])
            state = sb(s, "state", [P, 2, 2 * VW])
            dec = sb(s, "dec", [P, TT, 2])
            dd = sb(s, "dd", [P, 2, 2])
            mss = sb(s, "mss", [P, 2 * TT])
        with ExitStack() as s:
            qkt = sb(s, "qkt", [P, 2, SEQ])
            vs = sb(s, "vs", [P, TT, P])
            sq = sb(s, "sq", [P, HALF])
            rs = sb(s, "rs", [P, HALF])
            sp_ = sb(s, "sp", [P, 3, HALF])
            sph = sb(s, "sph", [P, 3, 2, HALF], F32R)
            carry = sb(s, "carry", [P, 3, HALF])
            prob = sb(s, "prob", [P, 3, HALF])
            yss = sb(s, "yss", [P, SBLK])
        with ExitStack() as s:
            wo_more = sb(s, "wo_more", [P, SLOTS, 2, KT * P], F32R)
            rtile = sb(s, "rtile", [P, 2, D])
        with ExitStack() as s:
            hid = sb(s, "hid", [P, 2, 2, GROUP, SEQ], F32R)
            h1 = sb(s, "h1", [P, 2, HALF])
            h2 = sb(s, "h2", [P, 2, HALF])

        const_done = sem("const_done")
        x_loaded = [sem(f"x_loaded{t}") for t in range(TT)]
        raw_loaded = [sem(f"raw_loaded{s}") for s in range(SLOTS)]
        hi_done = [sem(f"hi_done{s}") for s in range(SLOTS)]
        lo_done = [sem(f"lo_done{s}") for s in range(SLOTS)]
        phase_done = {e: sem(f"phase_done_{e}") for e in ("pe", "act", "dve", "pool", "sp")}
        small_loaded = sem("small_loaded")
        gain_loaded = sem("gain_loaded")
        resid_stored = sem("resid_stored")
        out_stored = sem("out_stored")
        rows_stored = sem("rows_stored")
        nm_loaded = sem("nm_loaded")
        wg_loaded = sem("wg_loaded")
        rt_loaded = [sem(f"rt_loaded{i}") for i in range(2)]
        steps = {e.engine: sem(f"steps_{i}") for i, e in enumerate((nc.tensor, nc.scalar, nc.vector, nc.gpsimd, nc.sync))}
        ready = {}

        from_one = [*lo_done, *phase_done.values()]

        def flag(name, per_layer):
            ready[name] = (sem(name), per_layer)
            from_one.append(ready[name][0])

        def level(name, l, n):
            s, per = ready[name]
            return l * per + n + 1

        def raise_(ins, name):
            ins.then_inc(ready[name][0], 1)

        def await_(eng, name, l, n):
            eng.wait_ge(ready[name][0], level(name, l, n))

        NT = 3 * TT
        NU = 2 * (SBLK + 2 * SBLK)
        NH4 = 2 * 2
        flag("tile_ready", NT)
        flag("scale_ready", 2 * TT)
        flag("tile_turned", 2 * NT)
        flag("turn_hi", 2 * NT)
        flag("turn_lo", 2 * NT)
        flag("out_psum", 2 * TT)
        flag("resid_new", TT)
        flag("small_pe", 1)
        flag("wg_hi", 1)
        flag("wg_lo", 1)
        flag("gate_pe", 5)
        flag("gate_dve", 5)
        flag("gate_act", 2)
        flag("m_proj", 8 * NPAIR)
        flag("m_evac", 8 * NPAIR)
        flag("m_conv", 2 * NPAIR)
        flag("m_esig", 2 * NPAIR)
        flag("m_qk", 2 * NPAIR)
        flag("m_args", 2 * NPAIR)
        flag("m_masked", NPAIR)
        flag("m_exp", 2 * NPAIR)
        flag("m_kt", 2 * NPAIR)
        flag("m_kw", NPAIR)
        flag("m_qs", NPAIR)
        flag("m_s", 4 * NPAIR)
        flag("m_w", 4 * NPAIR)
        flag("m_u", (TT - 1) * NPAIR)
        flag("m_state", TT * NPAIR)
        flag("m_num", TT * NPAIR)
        flag("m_y", TT * NPAIR)
        flag("m_ysq", NPAIR)
        flag("m_yms", NPAIR)
        flag("m_yrs", NPAIR)
        flag("s_proj", 6 * NPAIR)
        flag("s_sq", 4 * NPAIR)
        flag("s_sum", 4 * NPAIR)
        flag("s_rs", 4 * NPAIR)
        flag("s_qk", 4 * NPAIR)
        flag("s_v", 2 * NPAIR)
        flag("u_z", NU * NPAIR)
        flag("u_abs", NU * NPAIR)
        flag("u_ln", NU * NPAIR)
        flag("u_sp", NU * NPAIR)
        flag("u_hi", NU * NPAIR)
        flag("u_lo", NU * NPAIR)
        flag("u_carry", NU * NPAIR)
        flag("u_e", NU * NPAIR)
        flag("u_prob", NU * NPAIR)
        flag("u_av", NU * NPAIR)
        flag("y_sq", NH4 * NPAIR)
        flag("y_ms", NH4 * NPAIR)
        flag("y_rs", NH4 * NPAIR)
        flag("y_done", NH4 * NPAIR)
        UPS = 2 * GROUP
        flag("up_psum", UPS * NG)
        flag("relu", UPS * NG)
        flag("square", UPS * NG)
        flag("hid_hi", UPS * NG)
        flag("hid_lo", UPS * NG)
        flag("down_psum", 2 * TT * NG)
        flag("down_add", 2 * TT * NG)

        PHASES = 6

        def part(eng):
            eng.sem_inc(steps[eng.engine], 1)

        def phase_end(eng, name):
            part(eng)
            eng.drain().then_inc(phase_done[name], 1)

        def phase_start(eng, l, n, *others):
            for o in others:
                eng.wait_ge(phase_done[o], l * PHASES + n + 1)
            part(eng)

        def raw_k(s):
            return raw[:, s].rearrange("p (k n) -> p k n", k=KT)

        def spl_k(s, h):
            return spl[:, s, h].rearrange("p (k n) -> p k n", k=KT)

        def use(l, s, n):
            return l * uses_layer[s] + n

        use_m = [0] * SLOTS
        use_s = uses_m
        use_out = [uses_m[s] + uses_s[s] for s in range(SLOTS)]
        use_mlp = [use_out[s] + OUT_USES for s in range(SLOTS)]

        units = [(j, b, k) for j in range(2) for b in range(2) for k in reversed(range(SBLK * (b + 1)))]
        assert len(units) == NU
        E_BANKS = (0, 1, 2, 3, 6, 7)

        def span(n):
            _, b, k = units[n]
            diag = k >= SBLK * b
            c0 = (k - SBLK * b) * P if diag else 0
            return c0, c0 + P if diag else 0, diag

        def top(n):
            _, b, k = units[n]
            return k == SBLK * (b + 1) - 1

        def y_bank(q):
            return psum[4 + q % 2]

        PASSES = ((0, 0), (0, 1), (1, 0))
        ROW_W, ROW_B, ROW_Q, ROW_K = 0, CW * KT, (CW + 1) * KT, (CW + 1) * KT + 1
        N_SMALL = ROW_K + 1
        SMALL_DMAS = 8

        block = ctx.enter_context(nc.Block())

        @block.sync
        def _(sp):
            for t in range(TT):
                sp.dma_start(resid[:, t], xin_v[:, t]).then_inc(x_loaded[t], 16)

            sp.wait_ge(const_done, 1)

            def load(s, l, n, dst, src):
                sp.wait_ge(lo_done[s], use(l, s, n) + 1)
                part(sp)
                sp.dma_start(dst, src).then_inc(raw_loaded[s], 16)

            with sp.Fori(0, DEPTH) as l:
                w_in_v = w_in[l].rearrange("(k p) n -> p k n", p=P)
                w_up_v = w_up[l].rearrange("(k p) n -> p k n", p=P)

                with sp.Fori(0, NPAIR) as hp:
                    for s in range(SLOTS):
                        load(s, l, use_m[s] + hp, raw_k(s), w_in_v[:, :, bass.ds(s * DH + hp * P, P)])
                load(3, l, use_out[3], raw[:, 3], w_out[l, 3 * P:4 * P, :])
                with sp.Fori(0, NPAIR) as hp:
                    for s in range(STICK_SLOTS):
                        load(s, l, use_s[s] + hp, raw_k(s), w_in_v[:, :, bass.ds(O_SB + s * DH + hp * P, P)])
                for s in range(STICK_SLOTS):
                    load(s, l, use_out[s], raw[:, s], w_out[l, s * P:(s + 1) * P, :])
                for s in range(SLOTS):
                    load(s, l, use_out[s] + 1, raw[:, s], w_out[l, (SLOTS + s) * P:(SLOTS + s + 1) * P, :])
                phase_start(sp, l, 4, "pe", "act", "dve", "pool")
                sp.wait_ge(resid_stored, l * 16 + 16)
                for t in range(TT):
                    if t >= 2:
                        await_(sp, "resid_new", l, t - 1)
                    sp.dma_start(rtile[:, t % 2], resid_v[:, t]).then_inc(rt_loaded[t % 2], 16)
                with sp.Fori(0, NG) as g:
                    for s in range(GROUP):
                        load(s, l, use_mlp[s] + g, raw_k(s), w_up_v[:, :, bass.ds((g * GROUP + s) * P, P)])
                    for s in range(GROUP):
                        load(GROUP + s, l, use_mlp[GROUP + s] + g, raw[:, GROUP + s],
                             w_down[l, bass.ds((g * GROUP + s) * P, P), :])
            phase_start(sp, DEPTH - 1, PHASES, "dve")
            sp.dma_start(out_v, resid[:]).then_inc(out_stored, 16)
            sp.wait_ge(out_stored, 16)

        @block.tensor
        def _(pe):
            def turn(l, n):
                await_(pe, "tile_ready", l, n + 1)
                for b in range(2):
                    i = 2 * n + b
                    if i >= 4:
                        await_(pe, "turn_lo", l, i - 3)
                    for k in range(4):
                        ins = pe.transpose(psum[i % 4][:, k * P:(k + 1) * P],
                                           turned[:, n % 2, (4 * b + k) * P:(4 * b + k + 1) * P], ident[:])
                    raise_(ins, "tile_turned")

            def project_f(l, s, n, banks, done):
                pe.wait_ge(lo_done[s], use(l, s, n) + 2)
                for h in range(2):
                    for k in range(KT):
                        for i, (a, b) in enumerate(PASSES):
                            ins = pe.matmul(psum[banks[h]][:], spl_k(s, a)[:, k, :],
                                            act_t[:, b, k, h * HALF:(h + 1) * HALF],
                                            start=(k == 0 and i == 0), stop=(k == KT - 1 and i == 2))
                    raise_(ins, done)

            def project_t(l, slots, n, place, done, per_bank):
                for s in slots:
                    pe.wait_ge(lo_done[s], use(l, s, n) + 2)
                for t in range(TT):
                    for k in range(KT):
                        for i, (a, b) in enumerate(PASSES):
                            rhs = spl[:, slots[0]:slots[-1] + 1, b, k * P:(k + 1) * P]
                            ins = pe.matmul(place(t), act_t[:, a, k, t * P:(t + 1) * P], rhs,
                                            start=(k == 0 and i == 0), stop=(k == KT - 1 and i == 2))
                    if t % per_bank == per_bank - 1:
                        raise_(ins, done)

            def up(l, g, first=False):
                for i in range(UPS):
                    s, h = i // 2, i % 2
                    if h == 0:
                        pe.wait_ge(lo_done[s], use(l, s, use_mlp[s] + g) + 2)
                    if not first:
                        await_(pe, "square", l, UPS * g + i + 1 - UPS)
                    for k in range(KT):
                        for q, (a, b) in enumerate(PASSES):
                            ins = pe.matmul(psum[i][:], spl_k(s, a)[:, k, :], act_t[:, b, k, h * HALF:(h + 1) * HALF],
                                            start=(k == 0 and q == 0), stop=(k == KT - 1 and q == 2))
                    raise_(ins, "up_psum")

            def down(l, g, buf, first=False):
                for s in range(GROUP):
                    pe.wait_ge(lo_done[GROUP + s], use(l, GROUP + s, use_mlp[GROUP + s] + g) + 2)
                for i in range(2 * TT):
                    t, h = i // 2, i % 2
                    if i == 0:
                        await_(pe, "hid_lo", l, UPS * g + UPS)
                    if not (first and i < 4):
                        await_(pe, "down_add", l, 2 * TT * g + i - 3)
                    for k in range(GROUP):
                        for q, (a, b) in enumerate(PASSES):
                            ins = pe.matmul(psum[4 + i % 4][:], hid[:, buf, a, k, t * P:(t + 1) * P],
                                            spl[:, GROUP + k, b, h * HALF:(h + 1) * HALF],
                                            start=(k == 0 and q == 0), stop=(k == GROUP - 1 and q == 2))
                    raise_(ins, "down_psum")

            pe.wait_ge(const_done, 1)
            with pe.Fori(0, DEPTH) as l:
                phase_start(pe, l, 0, "act", "dve")
                pe.wait_ge(small_loaded, (l + 1) * (16 * SMALL_DMAS))
                part(pe)
                raise_(pe.transpose(psum[7][:, 0:N_SMALL], small_rows[0:N_SMALL, :], ident[0:N_SMALL, 0:N_SMALL]), "small_pe")
                for t in range(TT):
                    turn(l, t)
                phase_end(pe, "pe")
                phase_start(pe, l, 1, "act", "dve")
                await_(pe, "wg_lo", l, 1)
                for t in range(TT):
                    for k in range(KT):
                        for i, (a, b) in enumerate(PASSES):
                            ins = pe.matmul(psum[0][:, t * 2 * NH:(t + 1) * 2 * NH],
                                            act_t[:, a, k, t * P:(t + 1) * P], wg[:, b, k, :],
                                            start=(k == 0 and i == 0), stop=(k == KT - 1 and i == 2))
                raise_(ins, "gate_pe")
                await_(pe, "gate_dve", l, 2)
                pe.matmul(psum[1][0:CH, 0:P], glog[:].rearrange("p t h -> p (t h)"), tri_f[:], start=True, stop=True)
                raise_(pe.matmul(psum[2][0:CH, 0:P], gi[:].rearrange("p t h -> p (t h)"), ident[:],
                                 start=True, stop=True), "gate_pe")
                await_(pe, "gate_dve", l, 3)
                part(pe)
                pe.matmul(psum[3][0:1, 0:CH], brow[:, P - 1:P], ident[0:CH, 0:CH], start=True, stop=True)
                raise_(pe.matmul(psum[3][0:1, CH:2 * CH], cmax[:, 1, 64 + P - 1:64 + P], ident[0:CH, 0:CH],
                                 start=True, stop=True), "gate_pe")
                await_(pe, "gate_dve", l, 4)
                part(pe)
                raise_(pe.matmul(psum[4][0:CH, 0:1], mprev[:, :], ident[0:1, 0:1], start=True, stop=True), "gate_pe")
                await_(pe, "gate_dve", l, 5)
                part(pe)
                pe.transpose(psum[5][:, 0:CH], arow[:], ident[0:CH, 0:CH])
                raise_(pe.transpose(psum[5][:, CH:2 * CH], frow[:], ident[0:CH, 0:CH]), "gate_pe")
                phase_end(pe, "pe")
                phase_start(pe, l, 2, "act", "dve")
                with pe.Fori(0, NPAIR) as hp:
                    await_(pe, "m_y", l, hp * TT)
                    project_f(l, 0, use_m[0] + hp, (0, 1), "m_proj")
                    project_f(l, 1, use_m[1] + hp, (2, 3), "m_proj")
                    project_t(l, (2, 3), use_m[2] + hp,
                              lambda t: psum[4 + t // 2][:, (t % 2) * 2 * P:(t % 2 + 1) * 2 * P].rearrange("p (s n) -> p s n", s=2),
                              "m_proj", 2)
                    await_(pe, "m_qk", l, 2 * hp + 2)
                    for b in range(2):
                        for c in range(4):
                            ins = pe.transpose(psum[b][:, c * P:(c + 1) * P], km[:, (4 * b + c) * P:(4 * b + c + 1) * P], ident[:])
                        raise_(ins, "m_kt")
                    for b in range(2):
                        for j in range(2):
                            if b == 1:
                                await_(pe, "m_w", l, 4 * hp + j + 1)
                            for c in range(4):
                                cc = slice((4 * b + c) * P, (4 * b + c + 1) * P)
                                hs = slice(j * HD, (j + 1) * HD)
                                ins = pe.matmul(psum[2 + j][:, c * P:(c + 1) * P], km[hs, cc], qm[hs, cc], start=True, stop=True)
                            raise_(ins, "m_s")
                    await_(pe, "m_kw", l, hp + 1)
                    await_(pe, "m_qs", l, hp + 1)
                    await_(pe, "m_evac", l, 8 * hp + 8)
                    for c in range(TT):
                        if c < TT - 1:
                            if c >= 2:
                                await_(pe, "m_state", l, TT * hp + c)
                            raise_(pe.matmul(psum[6 + c % 2][:, 0:2 * VW], kw[:, c], vm[:, c].rearrange("p j v -> p (j v)"),
                                             start=True, stop=True), "m_u")
                        await_(pe, "m_state", l, TT * hp + c + 1)
                        await_(pe, "m_w", l, 4 * hp + (2 if c < 4 else 4))
                        if c >= 2:
                            await_(pe, "m_y", l, TT * hp + c - 1)
                        dst = psum[4 + c % 2]
                        pe.matmul(dst[:, 0:2 * VW], qs[:, c], state[:, c % 2], start=True, stop=False, skip_group_check=True)
                        for j in range(2):
                            ins = pe.matmul(dst[:, j * VW:(j + 1) * VW], nm[:, c, j, 0:P], vm[:, c, j], start=False, stop=(j == 1),
                                            skip_group_check=True)
                        raise_(ins, "m_num")
                phase_end(pe, "pe")
                phase_start(pe, l, 3, "act", "dve", "pool")
                with pe.Fori(0, NPAIR) as hp:
                    await_(pe, "u_prob", l, hp * NU)
                    project_f(l, 0, use_s[0] + hp, (0, 1), "s_proj")
                    project_f(l, 1, use_s[1] + hp, (2, 3), "s_proj")
                    await_(pe, "y_done", l, hp * NH4)
                    project_t(l, (2,), use_s[2] + hp, lambda t: psum[4 + t // 4][:, (t % 4) * P:(t % 4 + 1) * P], "s_proj", 4)
                    for n in range(4):
                        await_(pe, "s_sq", l, 4 * hp + n + 1)
                        await_(pe, "s_rs", l, 4 * hp + max(n - 1, 0))
                        raise_(pe.matmul(psum[6 + n % 2][:], head_ones[:], sq[:], start=True, stop=True), "s_sum")
                    await_(pe, "s_qk", l, 4 * hp + 4)
                    await_(pe, "s_v", l, 2 * hp + 2)

                    def scores(n):
                        j, b, k = units[n]
                        c0, c1, diag = span(n)
                        hs = slice(j * HD, (j + 1) * HD)
                        await_(pe, "u_prob", l, NU * hp + max(n + 1 - len(E_BANKS), 0))
                        e = psum[E_BANKS[n % len(E_BANKS)]]
                        ins = pe.matmul(e[:, c0:HALF], qkt[hs, 1, k * P:(k + 1) * P], qkt[hs, 0, b * HALF + c0:(b + 1) * HALF],
                                        start=True, stop=False, skip_group_check=True)
                        if diag:
                            ins = pe.matmul(e[:, c0:c1], ident_b[:], after_mask[:], start=False, stop=False, skip_group_check=True)
                        raise_(ins, "u_z")

                    def exponents(n):
                        c0, c1, diag = span(n)
                        e = psum[E_BANKS[n % len(E_BANKS)]]
                        await_(pe, "u_lo", l, NU * hp + n + 1)
                        for h in range(2):
                            ins = pe.matmul(e[:, c0:HALF], suffix[:], sph[:, n % 3, h, c0:HALF], start=False,
                                            stop=(h == 1 and c1 == HALF), skip_group_check=True)
                        if c1 < HALF:
                            await_(pe, "u_carry", l, NU * hp + n)
                            ins = pe.matmul(e[:, c1:HALF], minus_ones[:], carry[:, n % 3, c1:HALF], start=False,
                                            stop=True, skip_group_check=True)
                        raise_(ins, "u_e")

                    def values(n):
                        j, b, k = units[n]
                        c0, c1, diag = span(n)
                        await_(pe, "u_prob", l, NU * hp + n + 1)
                        if top(n) and 2 * j + b >= 2:
                            await_(pe, "y_done", l, NH4 * hp + 2 * j + b - 1)
                        y = y_bank(2 * j + b)
                        for q in range(c0 // P, SBLK):
                            ins = pe.matmul(y[:, q * HD:(q + 1) * HD], prob[:, n % 3, q * P:(q + 1) * P],
                                            vs[:, k, j * HD:(j + 1) * HD], start=top(n), stop=(k == 0), skip_group_check=True)
                        raise_(ins, "u_av")

                    for n in range(NU + 4):
                        if 0 <= n - 3 < NU:
                            exponents(n - 3)
                        if n < NU:
                            scores(n)
                        if 0 <= n - 4 < NU:
                            values(n - 4)
                phase_end(pe, "pe")
                phase_start(pe, l, 4, "act", "dve")
                for t in range(TT):
                    turn(l, TT + t)
                for s in range(SLOTS):
                    pe.wait_ge(lo_done[s], use(l, s, use_out[s]) + 3)
                await_(pe, "turn_lo", l, 4 * TT)
                for t in range(TT):
                    for h in range(2):
                        if t >= 2:
                            await_(pe, "resid_new", l, t - 1)
                        bank = psum[4 + 2 * (t % 2) + h]
                        for k in range(KT):
                            w = spl if k < SLOTS else wo_more
                            for i, (a, b) in enumerate(PASSES):
                                ins = pe.matmul(bank[:], act_t[:, a, k, t * P:(t + 1) * P],
                                                w[:, k % SLOTS, b, h * HALF:(h + 1) * HALF],
                                                start=(k == 0 and i == 0), stop=(k == KT - 1 and i == 2))
                        raise_(ins, "out_psum")
                    if t >= 1:
                        turn(l, 2 * TT + t - 1)
                turn(l, 3 * TT - 1)
                phase_end(pe, "pe")
                phase_start(pe, l, 5, "act", "dve")
                up(l, 0, first=True)
                up(l, 1)
                down(l, 0, 0, first=True)
                with pe.Fori(0, NG // 2 - 1) as m:
                    up(l, 2 * m + 2)
                    down(l, 2 * m + 1, 1)
                    up(l, 2 * m + 3)
                    down(l, 2 * m + 2, 0)
                down(l, NG - 1, 1)
                phase_end(pe, "pe")

        @block.scalar
        def _(act):
            def hi(s, l, n, dst):
                act.wait_ge(raw_loaded[s], (use(l, s, n) + 1) * 16)
                act.activation(dst, raw[:, s], ACT.Copy).then_inc(hi_done[s], 1)

            def turn_hi(l, n):
                t = n % TT
                for b in range(2):
                    await_(act, "tile_turned", l, 2 * n + b + 1)
                    raise_(act.activation(act_t[:, 0, 4 * b:4 * b + 4, t * P:(t + 1) * P],
                                          psum[(2 * n + b) % 4][:].rearrange("p (k n) -> p k n", k=4), ACT.Copy), "turn_hi")

            def tile_scale(l, n, t):
                if n >= 2:
                    await_(act, "tile_turned", l, 2 * (n - 1))
                act.activation(turned[:, n % 2], resid[:, t], ACT.Square, accum_out=ssq[:, n % 2:n % 2 + 1])
                act.drain()
                act.activation(ssq[:, n % 2:n % 2 + 1], ssq[:, n % 2:n % 2 + 1], ACT.Ln, bias=eps_c[:, 0:1], scale=1.0 / D)
                act.drain()
                raise_(act.activation(rst[:, n % 2:n % 2 + 1], ssq[:, n % 2:n % 2 + 1], ACT.Exp, scale=-0.5), "scale_ready")

            act.preload_act_table_set("natural_log_exp_and_others")
            act.wait_ge(const_done, 1)
            with act.Fori(0, DEPTH) as l:
                phase_start(act, l, 0, "pe", "dve")
                act.dma_start(gain[:], attn_norm_g[l].unsqueeze(0).to_broadcast([P, D])).then_inc(gain_loaded, 16)
                act.dma_start(small_rows[ROW_W:ROW_B, :], conv_w[l].rearrange("j (t p) -> (j t) p", p=P)).then_inc(small_loaded, 16)
                act.dma_start(small_rows[ROW_B:ROW_Q, :], conv_b[l].rearrange("(t p) -> t p", p=P)).then_inc(small_loaded, 16)
                for r, g in ((ROW_Q, q_norm_g), (ROW_K, k_norm_g)):
                    for j in range(2):
                        act.dma_start(small_rows[r:r + 1, j * HD:(j + 1) * HD], g[l].unsqueeze(0)).then_inc(small_loaded, 16)
                act.dma_start(gate_bias[:, 0:NH], b_igate[l].unsqueeze(0).to_broadcast([P, NH])).then_inc(small_loaded, 16)
                act.dma_start(gate_bias[:, NH:2 * NH], b_fgate[l].unsqueeze(0).to_broadcast([P, NH])).then_inc(small_loaded, 16)
                act.dma_start(wg_raw[:], w_in[l].rearrange("(k p) n -> p k n", p=P)[:, :, 4 * DH:4 * DH + 2 * NH]).then_inc(wg_loaded, 16)
                for s in range(SLOTS):
                    hi(s, l, use_m[s], spl[:, s, 0])
                for t in range(TT + 1):
                    if t < TT:
                        act.wait_ge(x_loaded[t], 16)
                        tile_scale(l, t, t)
                    if t >= 1:
                        turn_hi(l, t - 1)
                act.dma_start(resid_v, resid[:]).then_inc(resid_stored, 16)
                act.wait_ge(wg_loaded, 16 * (l + 1))
                raise_(act.activation(wg[:, 0], wg_raw[:], ACT.Copy), "wg_hi")
                phase_end(act, "act")
                phase_start(act, l, 1, "dve")
                act.dma_start(gain[:], out_norm_g[l].unsqueeze(0).to_broadcast([P, D])).then_inc(gain_loaded, 16)
                await_(act, "gate_dve", l, 1)
                act.activation(gabs[:], gabs[:], ACT.Exp, scale=-1.0)
                act.drain()
                raise_(act.activation(gabs[:], gabs[:], ACT.Ln, bias=1.0), "gate_act")
                await_(act, "gate_dve", l, 5)
                act.dma_start(rows_d, nrow[:]).then_inc(rows_stored, 16)
                await_(act, "gate_pe", l, 5)
                raise_(act.activation(floor_col[:], psum[5][:, CH:2 * CH], ACT.Exp), "gate_act")
                act.wait_ge(rows_stored, (l + 1) * 16)
                phase_end(act, "act")
                phase_start(act, l, 2, "pe", "dve")
                with act.Fori(0, NPAIR) as hp:
                    await_(act, "m_num", l, hp * TT)
                    act.dma_start(nm[:], rows_d.rearrange("(c h) t -> c h t", c=TT)[:, bass.ds(2 * hp, 2), :].unsqueeze(0)
                                  .to_broadcast([P, TT, 2, P + 1])).then_inc(nm_loaded, 16)
                    pairs = ((0, "q"), (1, "k"))
                    for h in range(2):
                        await_(act, "m_proj", l, 8 * hp + h + 1)
                        if h == 0:
                            await_(act, "m_yms", l, hp)
                        raise_(act.activation(pre[:, CW - 1 + h * HALF:CW - 1 + (h + 1) * HALF], psum[h][:], ACT.Copy), "m_evac")
                    await_(act, "m_args", l, 2 * hp + 1)
                    act.activation(qs[:], qs[:], ACT.Exp)
                    raise_(act.activation(dec[:], dec[:], ACT.Exp), "m_exp")
                    await_(act, "m_masked", l, hp + 1)
                    raise_(act.activation(nm[:, :, :, 0:P], nm[:, :, :, 0:P], ACT.Exp), "m_exp")
                    await_(act, "m_conv", l, 2 * hp + 1)
                    for h in range(2):
                        await_(act, "m_proj", l, 8 * hp + h + 3)
                        raise_(act.activation(pre[:, CW - 1 + h * HALF:CW - 1 + (h + 1) * HALF], psum[2 + h][:], ACT.Copy), "m_evac")
                    raise_(act.activation(sig[:], qm[:], ACT.Exp, scale=-1.0), "m_esig")
                    await_(act, "m_conv", l, 2 * hp + 2)
                    await_(act, "m_qk", l, 2 * hp + 1)
                    raise_(act.activation(sig[:], km[:], ACT.Exp, scale=-1.0), "m_esig")
                    for b in range(4):
                        await_(act, "m_proj", l, 8 * hp + 5 + b)
                        src = psum[4 + b][:].rearrange("p (t s n) -> p t s n", t=2, s=2)
                        for t in range(2):
                            act.activation(vm[:, 2 * b + t, :, 0:HD], src[:, t, 0].rearrange("p (j d) -> p j d", j=2), ACT.Copy)
                        raise_(act.activation(og[:, 2 * b:2 * b + 2], src[:, :, 1], ACT.Exp, scale=-1.0), "m_evac")
                    for s in range(SLOTS):
                        hi(s, l, use_m[s] + hp + 1, spl[:, s, 0])
                    await_(act, "m_y", l, TT * (hp + 1))
                    raise_(act.activation(pre[:, CW - 1:].rearrange("p (t n) -> p t n", t=TT), resid[:, :, bass.ds(hp * P, P)],
                                          ACT.Square), "m_ysq")
                    await_(act, "m_yms", l, hp + 1)
                    act.activation(mss[:], mss[:], ACT.Ln, bias=eps_c[:, 0:1], scale=1.0 / HD)
                    act.drain()
                    raise_(act.activation(mss[:], mss[:], ACT.Exp, scale=-0.5), "m_yrs")
                phase_end(act, "act")
                phase_start(act, l, 3, "pe", "dve")
                with act.Fori(0, NPAIR) as hp:
                    for n in range(4):
                        await_(act, "s_proj", l, 6 * hp + n + 1)
                        await_(act, "s_sum", l, 4 * hp + n)
                        raise_(act.activation(sq[:], psum[n][:], ACT.Square), "s_sq")
                        await_(act, "s_sum", l, 4 * hp + n + 1)
                        await_(act, "s_qk", l, 4 * hp + n)
                        is_q = n < 2
                        act.activation(rs[:], psum[6 + n % 2][:], ACT.Ln, scale=1.0 if is_q else 1.0 / HD,
                                       bias=eps_c[:, 1:2] if is_q else eps_c[:, 0:1])
                        act.drain()
                        raise_(act.activation(rs[:], rs[:], ACT.Exp, scale=-0.5), "s_rs")
                    for b in range(2):
                        await_(act, "s_proj", l, 6 * hp + 5 + b)
                        raise_(act.activation(vs[:, 4 * b:4 * b + 4], psum[4 + b][:].rearrange("p (t n) -> p t n", t=4), ACT.Copy), "s_v")
                    for s in range(STICK_SLOTS):
                        hi(s, l, use_s[s] + hp + 1, spl[:, s, 0])

                    def log_part(n):
                        c0, _, _ = span(n)
                        u = sp_[:, n % 3, c0:HALF]
                        await_(act, "u_abs", l, NU * hp + n + 1)
                        act.activation(u, u, ACT.Exp, scale=-1.0)
                        act.drain()
                        raise_(act.activation(u, u, ACT.Ln, bias=1.0), "u_ln")

                    def hi_part(n):
                        c0, _, _ = span(n)
                        await_(act, "u_sp", l, NU * hp + n + 1)
                        await_(act, "u_e", l, NU * hp + max(n - 2, 0))
                        raise_(act.activation(sph[:, n % 3, 0, c0:HALF], sp_[:, n % 3, c0:HALF], ACT.Copy), "u_hi")

                    def weights(n):
                        c0, _, _ = span(n)
                        await_(act, "u_e", l, NU * hp + n + 1)
                        await_(act, "u_av", l, NU * hp + max(n - 2, 0))
                        raise_(act.activation(prob[:, n % 3, c0:HALF], psum[E_BANKS[n % len(E_BANKS)]][:, c0:HALF], ACT.Exp), "u_prob")

                    def finish(n):
                        j, b, k = units[n]
                        if k:
                            return
                        q = 2 * j + b
                        await_(act, "u_av", l, NU * hp + n + 1)
                        raise_(act.activation(sq[:, 0:SBLK * HD], y_bank(q)[:, 0:SBLK * HD], ACT.Square), "y_sq")
                        await_(act, "y_ms", l, NH4 * hp + q + 1)
                        act.activation(yss[:], yss[:], ACT.Ln, bias=eps_c[:, 0:1], scale=1.0 / HD)
                        act.drain()
                        raise_(act.activation(yss[:], yss[:], ACT.Exp, scale=-0.5), "y_rs")

                    for n in range(NU + 5):
                        if 0 <= n - 1 < NU:
                            hi_part(n - 1)
                        if 0 <= n - 3 < NU:
                            weights(n - 3)
                        if n < NU:
                            log_part(n)
                        if 0 <= n - 5 < NU:
                            finish(n - 5)
                phase_end(act, "act")
                phase_start(act, l, 4, "pe", "dve", "pool")
                for s in range(SLOTS):
                    hi(s, l, use_out[s] + 1, wo_more[:, s, 0])
                for t in range(TT):
                    turn_hi(l, TT + t)
                act.dma_start(gain[:], mlp_norm_g[l].unsqueeze(0).to_broadcast([P, D])).then_inc(gain_loaded, 16)
                for t in range(TT + 1):
                    if t < TT:
                        await_(act, "resid_new", l, t + 1)
                        tile_scale(l, 2 * TT + t, t)
                    if t >= 1:
                        turn_hi(l, 2 * TT + t - 1)
                await_(act, "out_psum", l, 2 * TT)
                for s in range(SLOTS):
                    hi(s, l, use_mlp[s], spl[:, s, 0])
                phase_end(act, "act")
                phase_start(act, l, 5, "pe", "dve")

                def hidden(l, g, buf, more):
                    for i in range(UPS + 1):
                        if i < UPS:
                            await_(act, "up_psum", l, UPS * g + i + 1)
                            if not (more == "first" and i < 2):
                                await_(act, "square", l, UPS * g + i - 1)
                            raise_(act.activation(h1[:, i % 2], psum[i][:], ACT.Relu), "relu")
                        if i >= 1:
                            q = i - 1
                            await_(act, "square", l, UPS * g + q + 1)
                            raise_(act.activation(hid[:, buf, 0, q // 2, (q % 2) * HALF:(q % 2 + 1) * HALF], h2[:, q % 2], ACT.Copy), "hid_hi")
                    if more:
                        for s in range(GROUP):
                            hi(s, l, use_mlp[s] + g + 1, spl[:, s, 0])

                def next_down(l, g):
                    await_(act, "down_psum", l, 2 * TT * (g + 1))
                    for s in range(GROUP, SLOTS):
                        hi(s, l, use_mlp[s] + g + 1, spl[:, s, 0])

                hidden(l, 0, 0, "first")
                hidden(l, 1, 1, "yes")
                next_down(l, 0)
                with act.Fori(0, NG // 2 - 2) as m:
                    hidden(l, 2 * m + 2, 0, "yes")
                    next_down(l, 2 * m + 1)
                    hidden(l, 2 * m + 3, 1, "yes")
                    next_down(l, 2 * m + 2)
                hidden(l, NG - 2, 0, "yes")
                next_down(l, NG - 3)
                hidden(l, NG - 1, 1, None)
                next_down(l, NG - 2)
                phase_end(act, "act")

        @block.gpsimd
        def _(pool):
            def lo(s, l, n, dst):
                pool.wait_ge(hi_done[s], use(l, s, n) + 1)
                pool.tensor_tensor(dst[:, 1], raw[:, s], dst[:, 0].bitcast(F32), ALU.subtract).then_inc(lo_done[s], 1)

            for s in from_one:
                pool.sem_inc(s, 1)

            def select(dst, value, op, step):
                pool.memset(dst, value)
                pool.drain()
                pool.affine_select(out=dst, in_=dst, compare_op=op, fill=0.0, base=0, pattern=[[step, P]],
                                   channel_multiplier=-step)
                pool.drain()

            select(ident[:], 1.0, ALU.is_equal, 1)
            select(tri_f[:], 1.0, ALU.is_ge, 1)
            select(minus_ones[:], -1.0, ALU.is_ge, -1)
            pool.tensor_copy(suffix[:], minus_ones[:])
            pool.drain()
            select(minus_ones[:], MASKED, ALU.is_ge, -1)
            pool.tensor_copy(after_mask[:], minus_ones[:])
            pool.tensor_copy(ident_b[:], ident[:])
            pool.drain()
            pool.memset(minus_ones[:], -1.0)
            pool.memset(head_ones[:], 0.0)
            pool.memset(eps_c[:, 0:1], EPS)
            pool.memset(eps_c[:, 1:2], HD * EPS)
            pool.drain()
            for j in range(2):
                pool.memset(head_ones[j * HD:(j + 1) * HD, j * HD:(j + 1) * HD], 1.0)
            pool.drain().then_inc(const_done, 1)
            with pool.Fori(0, DEPTH) as l:
                for s in range(SLOTS):
                    lo(s, l, use_m[s], spl[:, s])
                await_(pool, "wg_hi", l, 1)
                raise_(pool.tensor_tensor(wg[:, 1], wg_raw[:], wg[:, 0].bitcast(F32), ALU.subtract), "wg_lo")
                phase_end(pool, "pool")
                phase_end(pool, "pool")
                with pool.Fori(0, NPAIR) as hp:
                    await_(pool, "m_args", l, 2 * hp + 2)
                    part(pool)
                    view = nm[:].rearrange("p c j t -> p (c j) t")[:, :, 0:P]
                    raise_(pool.affine_select(out=view, in_=view, compare_op=ALU.is_ge, fill=MASKED, base=0,
                                              pattern=[[0, 2 * TT], [1, P]], channel_multiplier=-1), "m_masked")
                    for s in range(SLOTS):
                        lo(s, l, use_m[s] + hp + 1, spl[:, s])
                phase_end(pool, "pool")
                phase_start(pool, l, 3, "pe", "dve", "act")
                with pool.Fori(0, NPAIR) as hp:
                    for s in range(STICK_SLOTS):
                        lo(s, l, use_s[s] + hp + 1, spl[:, s])
                    for n in range(NU):
                        c0, c1, diag = span(n)
                        await_(pool, "u_sp", l, NU * hp + n + 1)
                        await_(pool, "u_carry", l, NU * hp + n)
                        await_(pool, "u_e", l, NU * hp + max(n - 1, 0))
                        part(pool)
                        dst, src = carry[:, (n + 1) % 3], carry[:, n % 3]
                        if diag:
                            ins = pool.tensor_copy(dst[:, c0:c1], sp_[:, n % 3, c0:c1])
                        if c1 < HALF:
                            ins = pool.tensor_tensor(dst[:, c1:HALF], src[:, c1:HALF], sp_[:, n % 3, c1:HALF], ALU.add)
                        raise_(ins, "u_carry")
                phase_end(pool, "pool")
                for s in range(SLOTS):
                    lo(s, l, use_out[s] + 1, wo_more[:, s])
                for s in range(SLOTS):
                    lo(s, l, use_mlp[s], spl[:, s])
                phase_end(pool, "pool")
                def hid_lo(l, g, buf, more):
                    for q in range(UPS):
                        await_(pool, "hid_hi", l, UPS * g + q + 1)
                        cols = slice((q % 2) * HALF, (q % 2 + 1) * HALF)
                        raise_(pool.tensor_tensor(hid[:, buf, 1, q // 2, cols], h2[:, q % 2], hid[:, buf, 0, q // 2, cols].bitcast(F32),
                                                  ALU.subtract), "hid_lo")
                    if more:
                        for s in range(GROUP):
                            lo(s, l, use_mlp[s] + g + 1, spl[:, s])

                def next_down(l, g):
                    for s in range(GROUP, SLOTS):
                        lo(s, l, use_mlp[s] + g + 1, spl[:, s])

                hid_lo(l, 0, 0, True)
                hid_lo(l, 1, 1, True)
                next_down(l, 0)
                with pool.Fori(0, NG // 2 - 2) as m:
                    hid_lo(l, 2 * m + 2, 0, True)
                    next_down(l, 2 * m + 1)
                    hid_lo(l, 2 * m + 3, 1, True)
                    next_down(l, 2 * m + 2)
                hid_lo(l, NG - 2, 0, True)
                next_down(l, NG - 3)
                hid_lo(l, NG - 1, 1, False)
                next_down(l, NG - 2)
                phase_end(pool, "pool")

        @block.vector
        def _(dve):
            def turn_lo(l, n):
                t = n % TT
                for b in range(2):
                    await_(dve, "turn_hi", l, 2 * n + b + 1)
                    cells = (slice(None), slice(4 * b, 4 * b + 4), slice(t * P, (t + 1) * P))
                    raise_(dve.tensor_tensor(act_t[:, 1][cells], psum[(2 * n + b) % 4][:].rearrange("p (k n) -> p k n", k=4),
                                             act_t[:, 0][cells].bitcast(F32), ALU.subtract), "turn_lo")

            def normed_tile(l, n, t, scale_no):
                await_(dve, "scale_ready", l, scale_no)
                raise_(dve.scalar_tensor_tensor(out=turned[:, n % 2], in0=resid[:, t], scalar=rst[:, n % 2:n % 2 + 1],
                                                in1=gain[:], op0=ALU.mult, op1=ALU.mult), "tile_ready")

            dve.wait_ge(const_done, 1)
            with dve.Fori(0, DEPTH) as l:
                phase_start(dve, l, 0, "pe", "act")
                dve.wait_ge(gain_loaded, (l * 3 + 1) * 16)
                for t in range(TT + 1):
                    if t < TT:
                        normed_tile(l, t, t, t + 1)
                    if t >= 1:
                        turn_lo(l, t - 1)
                await_(dve, "small_pe", l, 1)
                dve.tensor_copy(small_cols[:, 0:N_SMALL], psum[7][:, 0:N_SMALL])
                phase_end(dve, "dve")
                phase_start(dve, l, 1, "act")
                dve.wait_ge(small_loaded, (l + 1) * (16 * SMALL_DMAS))
                for b in range(2):
                    dve.memset(cmax[:, b, 0:64], MASKED)
                await_(dve, "gate_pe", l, 1)
                dve.tensor_tensor(gsb[:], psum[0][:, 0:TT * 2 * NH].rearrange("p (t g) -> p t g", t=TT),
                                  gate_bias[:].unsqueeze(1).to_broadcast([P, TT, 2 * NH]), ALU.add)
                dve.drain()
                gf = gsb[:, :, NH:2 * NH]
                raise_(dve.tensor_scalar(gabs[:].bitcast(I32), gf.bitcast(I32), NO_SIGN, None, ALU.bitwise_and), "gate_dve")
                dve.tensor_copy(gi[:], gsb[:, :, 0:NH])
                await_(dve, "gate_act", l, 1)
                raise_(dve.scalar_tensor_tensor(out=glog[:], in0=gf, scalar=0.0, in1=gabs[:], op0=ALU.min, op1=ALU.subtract), "gate_dve")
                await_(dve, "gate_pe", l, 2)
                dve.tensor_copy(brow[:], psum[1][0:CH, 0:P])
                dve.drain()
                dve.tensor_tensor(arow[:], psum[2][0:CH, 0:P], brow[:], ALU.subtract)
                dve.drain()
                dve.tensor_copy(cmax[:, 0, 64:], arow[:])
                dve.drain()
                for n in range(7):
                    a, b = cmax[:, n % 2], cmax[:, 1 - n % 2]
                    ins = dve.tensor_tensor(b[:, 64:], a[:, 64:], a[:, 64 - 2 ** n:64 + P - 2 ** n], ALU.max)
                    if n < 6:
                        dve.drain()
                raise_(ins, "gate_dve")
                await_(dve, "gate_pe", l, 3)
                dve.tensor_copy(lastv[:].rearrange("p a n -> p (a n)"), psum[3][0:1, 0:2 * CH])
                dve.memset(mprev[:, 0:NH], 0.0)
                dve.drain()
                for c in range(TT - 1):
                    cur, nxt = mprev[:, c * NH:(c + 1) * NH], mprev[:, (c + 1) * NH:(c + 2) * NH]
                    dve.tensor_tensor(nxt, cur, lastv[:, 1, c * NH:(c + 1) * NH], ALU.max)
                    dve.drain()
                    ins = dve.tensor_tensor(nxt, nxt, lastv[:, 0, c * NH:(c + 1) * NH], ALU.add)
                    if c < TT - 2:
                        dve.drain()
                raise_(ins, "gate_dve")
                await_(dve, "gate_pe", l, 4)
                dve.tensor_copy(mpcol[:], psum[4][0:CH, 0:1])
                dve.drain()
                dve.tensor_scalar(nrow[:, 0:P], cmax[:, 1, 64:], mpcol[:, 0:1], -1.0, ALU.max, ALU.mult)
                dve.tensor_copy(nrow[:, P:P + 1], mpcol[:])
                dve.drain()
                raise_(dve.tensor_tensor(frow[:], nrow[:, 0:P], brow[:], ALU.subtract), "gate_dve")
                await_(dve, "gate_pe", l, 5)
                await_(dve, "gate_act", l, 2)
                dve.tensor_copy(a_col[:], psum[5][:, 0:CH])
                phase_end(dve, "dve")
                phase_start(dve, l, 2, "pe", "act")
                dve.wait_ge(resid_stored, (l + 1) * 16)
                dve.memset(pre[:, 0:CW - 1], 0.0)
                dve.memset(vm[:, :, :, HD:VW], 1.0)
                dve.memset(state[:], 0.0)
                dve.drain()
                with dve.Fori(0, NPAIR) as hp:
                    dve.wait_ge(nm_loaded, (l * NPAIR + hp + 1) * 16)
                    for j in range(2):
                        hs = slice(j * HD, (j + 1) * HD)
                        dve.tensor_tensor(qs[hs], nm[hs, :, j, 0:P], nm[hs, :, j, P:P + 1].to_broadcast([HD, TT, P]), ALU.add)
                    raise_(dve.tensor_tensor(dec[:], nm[:, :, :, P - 1], nm[:, :, :, P], ALU.add), "m_args")
                    dve.drain()
                    acol = a_col[:].rearrange("p (c h) -> p c h", c=TT)[:, :, bass.ds(2 * hp, 2)]
                    raise_(dve.tensor_tensor(nm[:, :, :, 0:P], nm[:, :, :, 0:P], acol.unsqueeze(3).to_broadcast([P, TT, 2, P]), ALU.add),
                           "m_args")
                    for w, dst in ((0, qm), (1, km)):
                        await_(dve, "m_evac", l, 8 * hp + 2 * w + 2)

                        def tap(j):
                            return small_cols[:, bass.ds(ROW_W + j * KT + w * NPAIR + hp, 1)]

                        dve.tensor_scalar(dst[:], pre[:, 0:SEQ], tap(0), small_cols[:, bass.ds(ROW_B + w * NPAIR + hp, 1)],
                                          ALU.mult, ALU.add)
                        for j in range(1, CW):
                            dve.drain()
                            ins = dve.scalar_tensor_tensor(out=dst[:], in0=pre[:, j:j + SEQ], scalar=tap(j), in1=dst[:],
                                                           op0=ALU.mult, op1=ALU.add)
                        raise_(ins, "m_conv")
                    for w, dst in ((0, qm), (1, km)):
                        await_(dve, "m_esig", l, 2 * hp + w + 1)
                        dve.tensor_scalar(sig[:], sig[:], 1.0, None, ALU.add)
                        dve.drain()
                        dve.reciprocal(sig[:], sig[:])
                        dve.drain()
                        raise_(dve.scalar_tensor_tensor(out=dst[:], in0=dst[:], scalar=QSC if w == 0 else 1.0, in1=sig[:],
                                                        op0=ALU.mult, op1=ALU.mult), "m_qk")
                    dve.drain()
                    await_(dve, "m_exp", l, 2 * hp + 2)
                    raise_(dve.tensor_tensor(qs[:], qs[:], qm[:].rearrange("p (c t) -> p c t", c=TT), ALU.mult), "m_qs")
                    for b in range(2):
                        await_(dve, "m_kt", l, 2 * hp + b + 1)
                        for j in range(2):
                            ins = dve.tensor_tensor(kw[:, 4 * b:4 * b + 4, j * HD:(j + 1) * HD],
                                                    psum[b][:].rearrange("p (c n) -> p c n", c=4)[:, :, j * HD:(j + 1) * HD],
                                                    nm[:, 4 * b:4 * b + 4, j, P - 1:P].to_broadcast([P, 4, HD]), ALU.mult)
                    raise_(ins, "m_kw")
                    dve.drain()
                    for b in range(2):
                        for j in range(2):
                            await_(dve, "m_s", l, 4 * hp + 2 * b + j + 1)
                            d = nm[:, 4 * b:4 * b + 4, j, 0:P]
                            raise_(dve.tensor_tensor(d, psum[2 + j][:].rearrange("p (c t) -> p c t", c=4), d, ALU.mult), "m_w")
                    await_(dve, "m_evac", l, 8 * hp + 8)
                    dve.tensor_scalar(og[:], og[:], 1.0, None, ALU.add)
                    dve.drain()
                    dve.reciprocal(og[:], og[:])
                    await_(dve, "m_num", l, TT * hp)
                    for j in range(2):
                        ins = dve.memset(state[j * HD:(j + 1) * HD, 0, j * VW:(j + 1) * VW], 0.0)
                    raise_(ins, "m_state")
                    floors = floor_col[:].rearrange("p (c h) -> p c h", c=TT)
                    for c in range(TT):
                        if c < TT - 1:
                            dve.drain()
                            await_(dve, "m_u", l, (TT - 1) * hp + c + 1)
                            if c >= 1:
                                await_(dve, "m_num", l, TT * hp + c)
                            for j in range(2):
                                hs, vsl = slice(j * HD, (j + 1) * HD), slice(j * VW, (j + 1) * VW)
                                ins = dve.scalar_tensor_tensor(out=state[hs, (c + 1) % 2, vsl], in0=state[hs, c % 2, vsl],
                                                               scalar=dec[hs, c, j:j + 1], in1=psum[6 + c % 2][hs, vsl],
                                                               op0=ALU.mult, op1=ALU.add)
                            raise_(ins, "m_state")
                        await_(dve, "m_num", l, TT * hp + c + 1)
                        num = psum[4 + c % 2][:, 0:2 * VW].rearrange("p (j v) -> p j v", j=2)
                        dve.tensor_scalar(dd[:, c % 2].bitcast(I32), num[:, :, HD].bitcast(I32), NO_SIGN, None, ALU.bitwise_and)
                        dve.drain()
                        dve.tensor_tensor(dd[:, c % 2], dd[:, c % 2], floors[:, c, bass.ds(2 * hp, 2)], ALU.max)
                        dve.drain()
                        dve.reciprocal(dd[:, c % 2], dd[:, c % 2])
                        dve.drain()
                        raise_(dve.tensor_tensor(resid[:, c, bass.ds(hp * P, P)].rearrange("p (j d) -> p j d", j=2), num[:, :, 0:HD],
                                                 dd[:, c % 2].unsqueeze(2).to_broadcast([P, 2, HD]), ALU.mult), "m_y")
                    await_(dve, "m_ysq", l, hp + 1)
                    raise_(dve.tensor_reduce(mss[:], pre[:, CW - 1:].rearrange("p (n d) -> p n d", d=HD), AX.X, ALU.add), "m_yms")
                    await_(dve, "m_yrs", l, hp + 1)
                    yv = resid[:, :, bass.ds(hp * P, P)].rearrange("p t (j d) -> p t j d", j=2)
                    dve.tensor_tensor(yv, yv, mss[:].rearrange("p (t j) -> p t j", j=2).unsqueeze(3).to_broadcast([P, TT, 2, HD]), ALU.mult)
                    dve.drain()
                    yw = resid[:, :, bass.ds(hp * P, P)]
                    dve.tensor_tensor(yw, yw, og[:], ALU.mult)
                    dve.drain()
                phase_end(dve, "dve")
                phase_start(dve, l, 3, "pe", "act", "pool")
                with dve.Fori(0, NPAIR) as hp:
                    for n in range(4):
                        await_(dve, "s_rs", l, 4 * hp + n + 1)
                        row = ROW_Q if n < 2 else ROW_K
                        raise_(dve.scalar_tensor_tensor(out=qkt[:, n // 2, (n % 2) * HALF:(n % 2 + 1) * HALF], in0=psum[n][:],
                                                        scalar=small_cols[:, row:row + 1], in1=rs[:], op0=ALU.mult, op1=ALU.mult), "s_qk")

                    def absolute(n):
                        c0, _, _ = span(n)
                        await_(dve, "u_z", l, NU * hp + n + 1)
                        await_(dve, "u_carry", l, NU * hp + max(n - 2, 0))
                        raise_(dve.tensor_scalar(sp_[:, n % 3, c0:HALF].bitcast(I32),
                                                 psum[E_BANKS[n % len(E_BANKS)]][:, c0:HALF].bitcast(I32), NO_SIGN, None,
                                                 ALU.bitwise_and), "u_abs")

                    def softplus(n):
                        c0, _, _ = span(n)
                        await_(dve, "u_ln", l, NU * hp + n + 1)
                        u = sp_[:, n % 3, c0:HALF]
                        raise_(dve.scalar_tensor_tensor(out=u, in0=psum[E_BANKS[n % len(E_BANKS)]][:, c0:HALF], scalar=0.0, in1=u,
                                                        op0=ALU.max, op1=ALU.add), "u_sp")

                    def lo_part(n):
                        c0, _, _ = span(n)
                        await_(dve, "u_hi", l, NU * hp + n + 1)
                        raise_(dve.tensor_tensor(sph[:, n % 3, 1, c0:HALF], sp_[:, n % 3, c0:HALF],
                                                 sph[:, n % 3, 0, c0:HALF].bitcast(F32), ALU.subtract), "u_lo")

                    def finish(n):
                        j, b, k = units[n]
                        if k:
                            return
                        q = 2 * j + b
                        await_(dve, "y_sq", l, NH4 * hp + q + 1)
                        raise_(dve.tensor_reduce(yss[:], sq[:, 0:SBLK * HD].rearrange("p (t d) -> p t d", d=HD), AX.X, ALU.add), "y_ms")
                        await_(dve, "y_rs", l, NH4 * hp + q + 1)
                        raise_(dve.tensor_tensor(resid[:, b * SBLK:(b + 1) * SBLK, bass.ds(DH + hp * P + j * HD, HD)],
                                                 y_bank(q)[:, 0:SBLK * HD].rearrange("p (t d) -> p t d", d=HD),
                                                 yss[:].unsqueeze(2).to_broadcast([P, SBLK, HD]), ALU.mult), "y_done")

                    for n in range(NU + 5):
                        if 0 <= n - 2 < NU:
                            lo_part(n - 2)
                        if 0 <= n - 1 < NU:
                            softplus(n - 1)
                        if n < NU:
                            absolute(n)
                        if 0 <= n - 5 < NU:
                            finish(n - 5)
                phase_end(dve, "dve")
                phase_start(dve, l, 4, "pe", "act")
                dve.wait_ge(gain_loaded, (l * 3 + 2) * 16)
                for t in range(TT + 1):
                    if t < TT:
                        if t >= 2:
                            await_(dve, "tile_turned", l, 2 * (TT + t - 1))
                        raise_(dve.tensor_tensor(turned[:, t % 2], resid[:, t], gain[:], ALU.mult), "tile_ready")
                    if t >= 1:
                        turn_lo(l, TT + t - 1)
                for t in range(TT + 1):
                    if t < TT:
                        dve.wait_ge(rt_loaded[t % 2], (l * (TT // 2) + t // 2 + 1) * 16)
                        for h in range(2):
                            await_(dve, "out_psum", l, 2 * t + h + 1)
                            cols = slice(h * HALF, (h + 1) * HALF)
                            ins = dve.tensor_tensor(resid[:, t, cols], psum[4 + 2 * (t % 2) + h][:], rtile[:, t % 2, cols], ALU.add)
                        raise_(ins, "resid_new")
                        if t == 0:
                            dve.wait_ge(gain_loaded, (l * 3 + 3) * 16)
                        normed_tile(l, 2 * TT + t, t, TT + t + 1)
                    if t >= 1:
                        turn_lo(l, 2 * TT + t - 1)
                phase_end(dve, "dve")
                phase_start(dve, l, 5, "pe", "act", "pool")

                def square(l, g, first):
                    for i in range(UPS):
                        await_(dve, "relu", l, UPS * g + i + 1)
                        if not (first and i < 2):
                            await_(dve, "hid_lo", l, UPS * g + i - 1)
                        raise_(dve.scalar_tensor_tensor(out=h2[:, i % 2], in0=psum[i][:], scalar=0.0, in1=h1[:, i % 2],
                                                        op0=ALU.max, op1=ALU.mult), "square")

                def add(l, g):
                    for i in range(2 * TT):
                        await_(dve, "down_psum", l, 2 * TT * g + i + 1)
                        r = resid[:, i // 2, (i % 2) * HALF:(i % 2 + 1) * HALF]
                        raise_(dve.tensor_tensor(r, psum[4 + i % 4][:], r, ALU.add), "down_add")

                square(l, 0, True)
                square(l, 1, False)
                add(l, 0)
                with dve.Fori(0, NG // 2 - 1) as m:
                    square(l, 2 * m + 2, False)
                    add(l, 2 * m + 1)
                    square(l, 2 * m + 3, False)
                    add(l, 2 * m + 2)
                add(l, NG - 1)
                phase_end(dve, "dve")


_INS = ["x", "attn_norm_g", "w_in", "conv_w", "conv_b", "b_igate", "b_fgate", "q_norm_g", "k_norm_g", "out_norm_g",
        "w_out", "mlp_norm_g", "w_up", "w_down"]


def kernel(**inputs):
    import numpy as np
    import concourse.bacc as bacc
    from concourse.bass_utils import run_bass_kernel_spmd

    nc = bacc.Bacc("TRN2", target_bir_lowering=False, num_devices=1)
    arrays, args = {}, []
    for name in _INS:
        a = np.ascontiguousarray(inputs[name])
        arrays[f"in_{name}"] = a
        args.append(nc.dram_tensor(f"in_{name}", a.shape, mybir.dt.from_np(a.dtype), kind="ExternalInput").ap())
    out = nc.dram_tensor("out_x", inputs["x"].shape, F32, kind="ExternalOutput").ap()
    trunk(nc, *args, out)
    r = run_bass_kernel_spmd(nc, [arrays], core_ids=[0])
    return r.results[0]["out_x"]
```

```python
from contextlib import ExitStack

import concourse.bass as bass
from concourse import mybir

F32 = mybir.dt.float32
F32R = mybir.dt.float32r
BF16 = mybir.dt.bfloat16
I32 = mybir.dt.int32
ALU = mybir.AluOpType
ACT = mybir.ActivationFunctionType
AX = mybir.AxisListType

P = 128
EPS = 1e-6
NO_SIGN = 0x7FFFFFFF
MASKED = -float(2 ** 100)


def trunk(nc, x, attn_norm_g, w_in, conv_w, conv_b, b_igate, b_fgate, q_norm_g, k_norm_g,
          out_norm_g, w_out, mlp_norm_g, w_up, w_down, out):
    _, SEQ, D = x.shape
    DEPTH = w_in.shape[0]
    HD = q_norm_g.shape[1]
    NH = b_igate.shape[1]
    DH = NH * HD
    FF = w_up.shape[2]
    CW = conv_w.shape[1]
    TT = SEQ // P
    KT = D // P
    NPAIR = NH // 2
    HALF = 512
    SLOTS = 4
    GROUP = 2
    NG = FF // (GROUP * P)
    O_SB = 4 * DH + 2 * NH
    CH = NH * TT
    VW = HD + 1
    QSC = float(HD) ** -0.5
    SBLK = HALF // P
    assert SEQ == 2 * HALF and KT == 8 and TT == 8 and CH == 64 and HD == 64

    OUT_USES = KT // SLOTS
    STICK_SLOTS = 3
    uses_m = [NPAIR] * SLOTS
    uses_s = [NPAIR if s < STICK_SLOTS else 0 for s in range(SLOTS)]
    uses_layer = [uses_m[s] + uses_s[s] + OUT_USES + NG for s in range(SLOTS)]

    resid_d = nc.dram_tensor("resid_scratch", (SEQ, D), F32, kind="Internal").ap()
    rows_d = nc.dram_tensor("rows_scratch", (CH, P + 1), F32, kind="Internal").ap()
    xin_v = x[0].rearrange("(t p) f -> p t f", p=P)
    out_v = out[0].rearrange("(t p) f -> p t f", p=P)
    resid_v = resid_d.rearrange("(t p) f -> p t f", p=P)

    ctx = ExitStack()
    with ctx:
        def sb(stack, name, shape, dt=F32):
            return stack.enter_context(nc.sbuf_tensor(name, shape, dt))

        def sem(name):
            return ctx.enter_context(nc.semaphore(name))

        ident = sb(ctx, "ident", [P, P])
        ident_b = sb(ctx, "ident_b", [P, P], BF16)
        after_mask = sb(ctx, "after_mask", [P, P], BF16)
        tri_f = sb(ctx, "tri_f", [P, P])
        suffix = sb(ctx, "suffix", [P, P], F32R)
        minus_ones = sb(ctx, "minus_ones", [P, P])
        head_ones = sb(ctx, "head_ones", [P, P])
        eps_c = sb(ctx, "eps_c", [P, 2])
        small_rows = sb(ctx, "small_rows", [P, P])
        small_cols = sb(ctx, "small_cols", [P, P])
        gate_bias = sb(ctx, "gate_bias", [P, 2 * NH])
        a_col = sb(ctx, "a_col", [P, CH])
        floor_col = sb(ctx, "floor_col", [P, CH])
        act_t = sb(ctx, "act_t", [P, 2, KT, SEQ], F32R)
        resid = sb(ctx, "resid", [P, TT, D])
        raw = sb(ctx, "raw", [P, SLOTS, KT * P])
        spl = sb(ctx, "spl", [P, SLOTS, 2, KT * P], F32R)
        gain = sb(ctx, "gain", [P, D])
        turned = sb(ctx, "turned", [P, 2, D])
        ssq = sb(ctx, "ssq", [P, 2])
        rst = sb(ctx, "rst", [P, 2])
        banks = ctx.enter_context(nc.psum_tensor("banks", [P, 8, 512], F32))
        psum = [banks[:, i] for i in range(8)]

        with ExitStack() as s:
            wg_raw = sb(s, "wg_raw", [P, KT, P])
            wg = sb(s, "wg", [P, 2, KT, P], F32R)
            gt = sb(s, "gt", [2 * NH, SEQ])
            gsb = sb(s, "gsb", [P, TT, 2 * NH])
            glog = sb(s, "glog", [P, TT, NH])
            gabs = sb(s, "gabs", [P, TT, NH])
            gi = sb(s, "gi", [P, TT, NH])
            brow = sb(s, "brow", [CH, P])
            arow = sb(s, "arow", [CH, P])
            cmax = sb(s, "cmax", [CH, 2, P + 64])
            lastv = sb(s, "lastv", [1, 2, CH])
            mprev = sb(s, "mprev", [1, CH])
            mpcol = sb(s, "mpcol", [CH, 1])
            nrow = sb(s, "nrow", [CH, P + 1])
            frow = sb(s, "frow", [CH, P])
        with ExitStack() as s:
            pre = sb(s, "pre", [P, CW - 1 + SEQ])
            qm = sb(s, "qm", [P, SEQ])
            km = sb(s, "km", [P, SEQ])
            sig = sb(s, "sig", [P, SEQ])
            qs = sb(s, "qs", [P, TT, P])
            vm = sb(s, "vm", [P, TT, 2, VW])
            og = sb(s, "og", [P, TT, P])
            nm = sb(s, "nm", [P, TT, 2, P + 1])
            kw = sb(s, "kw", [P, TT, P])
            state = sb(s, "state", [P, TT - 1, 2 * VW])
            dec = sb(s, "dec", [P, TT, 2])
            dd = sb(s, "dd", [P, TT, 2])
            mss = sb(s, "mss", [P, 2 * TT])
        with ExitStack() as s:
            qkt = sb(s, "qkt", [P, 2, SEQ])
            vs = sb(s, "vs", [P, TT, P])
            sp_ = sb(s, "sp", [P, 2, 2, HALF])
            sph = sb(s, "sph", [P, 2, 2, 2, HALF], F32R)
            carry = sb(s, "carry", [P, 2, 2, HALF])
            prob = turned[:].rearrange("p i (j t) -> p i j t", j=2)
            sq = carry[:, 0]
            rs = carry[:, 1]
            vf = sp_[:, 1].rearrange("p j t -> p (j t)")
            ysq = sb(s, "ysq", [P, 2, SBLK * HD])
            yss = sb(s, "yss", [P, 2 * SBLK])
        with ExitStack() as s:
            wo_more = sb(s, "wo_more", [P, SLOTS, 2, KT * P], F32R)
            rtile = sb(s, "rtile", [P, 2, D])
        with ExitStack() as s:
            hid = sb(s, "hid", [P, 2, 2, GROUP, SEQ], F32R)
            h1 = sb(s, "h1", [P, 2, HALF])
            h2 = sb(s, "h2", [P, 2, HALF])

        const_done = sem("const_done")
        x_loaded = [sem(f"x_loaded{t}") for t in range(TT)]
        raw_loaded = [sem(f"raw_loaded{s}") for s in range(SLOTS)]
        hi_done = [sem(f"hi_done{s}") for s in range(SLOTS)]
        lo_done = [sem(f"lo_done{s}") for s in range(SLOTS)]
        phase_done = {e: sem(f"phase_done_{e}") for e in ("pe", "act", "dve", "pool", "sp")}
        small_loaded = sem("small_loaded")
        gain_loaded = sem("gain_loaded")
        resid_stored = sem("resid_stored")
        out_stored = sem("out_stored")
        rows_stored = sem("rows_stored")
        nm_loaded = sem("nm_loaded")
        wg_loaded = sem("wg_loaded")
        rt_loaded = [sem(f"rt_loaded{i}") for i in range(2)]
        steps = {e.engine: sem(f"steps_{i}") for i, e in enumerate((nc.tensor, nc.scalar, nc.vector, nc.gpsimd, nc.sync))}

        from_one = [*lo_done, *phase_done.values()]

        class Flag:

            def __init__(self, name, per_layer, start=1):
                self.sem, self.per_layer, self.start = sem(name), per_layer, start
                from_one.extend([self.sem] * start)

            def at(self, l, n):
                return l * self.per_layer + n + self.start

        NT = 3 * TT
        NU = SBLK + 2 * SBLK
        NC = NU - 2
        tile_ready = Flag("tile_ready", NT)
        scale_ready = Flag("scale_ready", 2 * TT)
        tile_turned = Flag("tile_turned", 2 * NT)
        turned_hi = Flag("turned_hi", 2 * NT)
        turned_lo = Flag("turned_lo", 2 * NT)
        out_psum = Flag("out_psum", 2 * TT)
        resid_new = Flag("resid_new", TT)
        small_pe = Flag("small_pe", 1)
        wg_hi = Flag("wg_hi", 1)
        wg_lo = Flag("wg_lo", 1)
        gate_pe = Flag("gate_pe", 7)
        gate_dve = Flag("gate_dve", 7)
        gate_act = Flag("gate_act", 2)
        m_gated = Flag("m_gated", NPAIR)
        q_proj = Flag("q_proj", 2 * 2 * NPAIR)
        m_proj = Flag("m_proj", 6 * NPAIR)
        m_evac = Flag("m_evac", 8 * NPAIR)
        m_conv = Flag("m_conv", 2 * NPAIR)
        m_abs = Flag("m_abs", 3 * NPAIR)
        m_ln = Flag("m_ln", 3 * NPAIR)
        m_log = Flag("m_log", 3 * NPAIR)
        m_sig = Flag("m_sig", 3 * NPAIR)
        m_qk = Flag("m_qk", 2 * NPAIR)
        m_args = Flag("m_args", NPAIR)
        m_masked = Flag("m_masked", NPAIR)
        m_exp = Flag("m_exp", 2 * NPAIR)
        m_kt = Flag("m_kt", 2 * NPAIR)
        m_kw = Flag("m_kw", NPAIR)
        m_qs = Flag("m_qs", NPAIR)
        m_s = Flag("m_s", 2 * NPAIR)
        m_w = Flag("m_w", 2 * NPAIR)
        m_u = Flag("m_u", 3 * NPAIR)
        m_state = Flag("m_state", (TT - 1) * NPAIR)
        m_num = Flag("m_num", 3 * NPAIR)
        m_y = Flag("m_y", 3 * NPAIR)
        m_ysq = Flag("m_ysq", NPAIR)
        m_yms = Flag("m_yms", NPAIR)
        m_yrs = Flag("m_yrs", NPAIR)
        s_proj = Flag("s_proj", 4 * NPAIR)
        s_sq = Flag("s_sq", 4 * NPAIR)
        s_sum = Flag("s_sum", 4 * NPAIR)
        s_rs = Flag("s_rs", 4 * NPAIR)
        s_qk = Flag("s_qk", 4 * NPAIR)
        s_vf = Flag("s_vf", 2 * NPAIR)
        s_vt = Flag("s_vt", 2 * NPAIR)
        s_v = Flag("s_v", 2 * NPAIR)
        u_z = Flag("u_z", NU * NPAIR)
        u_abs = Flag("u_abs", NU * NPAIR)
        u_ln = Flag("u_ln", NU * NPAIR)
        u_sp = Flag("u_sp", NU * NPAIR)
        u_hi = Flag("u_hi", NU * NPAIR)
        u_lo = Flag("u_lo", NU * NPAIR)
        u_carry = Flag("u_carry", NC * NPAIR)
        u_e = Flag("u_e", NU * NPAIR)
        u_prob = Flag("u_prob", NU * NPAIR)
        u_av = Flag("u_av", NU * NPAIR)
        y_out = Flag("y_out", 2 * NPAIR)
        y_sq = Flag("y_sq", 2 * NPAIR)
        y_ms = Flag("y_ms", 2 * NPAIR)
        y_rs = Flag("y_rs", 2 * NPAIR)
        UPS = 2 * GROUP
        up_psum = Flag("up_psum", UPS * NG)
        relu = Flag("relu", UPS * NG)
        squared = Flag("squared", UPS * NG)
        hid_hi_done = Flag("hid_hi_done", UPS * NG)
        hid_lo_done = Flag("hid_lo_done", UPS * NG)
        down_psum = Flag("down_psum", 2 * TT * NG)
        down_add = Flag("down_add", 2 * TT * NG)

        PHASES = 6

        def part(eng):
            eng.sem_inc(steps[eng.engine], 1)

        def phase_end(eng, name):
            part(eng)
            eng.drain().then_inc(phase_done[name], 1)

        def phase_start(eng, l, n, *others):
            for o in others:
                eng.wait_ge(phase_done[o], l * PHASES + n + 1)
            part(eng)

        def raw_k(s):
            return raw[:, s].rearrange("p (k n) -> p k n", k=KT)

        def spl_k(s, h):
            return spl[:, s, h].rearrange("p (k n) -> p k n", k=KT)

        def use(l, s, n):
            return l * uses_layer[s] + n

        use_m = [0] * SLOTS
        use_s = uses_m
        use_out = [uses_m[s] + uses_s[s] for s in range(SLOTS)]
        use_mlp = [use_out[s] + OUT_USES for s in range(SLOTS)]

        NUM_BANKS = ((0, 3, 4), (3, 6, 5), (6, 8, 6))
        UPD_BANKS = ((0, 3, 6), (3, 6, 7), (6, 7, 2))
        UPD_BANK = {c: (a, bank) for a, e, bank in UPD_BANKS for c in range(a, e)}

        units = [(b, k) for b in range(2) for k in reversed(range(SBLK * (b + 1)))]
        assert len(units) == NU and NU % 3 == 0
        E_BANKS = (0, 2, 6)

        def span(n):
            b, k = units[n]
            diag = k >= SBLK * b
            c0 = (k - SBLK * b) * P if diag else 0
            return c0, c0 + P if diag else 0, diag

        def top(n):
            b, k = units[n]
            return k == SBLK * (b + 1) - 1

        def carries(n):
            return sum(1 for _, k in units[:max(n, 0)] if k)

        def logits(n):
            e = E_BANKS[n % 3]
            return banks[:, e:e + 2, span(n)[0]:HALF]

        def y_store(b, hp):
            return resid[:, b * SBLK:(b + 1) * SBLK, bass.ds(DH + hp * P, P)].rearrange("p t (j d) -> p j t d", j=2)

        PASSES = ((0, 0), (0, 1), (1, 0))
        ROW_W, ROW_B, ROW_Q, ROW_K = 0, CW * KT, (CW + 1) * KT, (CW + 1) * KT + 1
        N_SMALL = ROW_K + 1
        SMALL_DMAS = 8

        block = ctx.enter_context(nc.Block())

        @block.sync
        def _(sp):
            for t in range(TT):
                sp.dma_start(resid[:, t], xin_v[:, t]).then_inc(x_loaded[t], 16)

            sp.wait_ge(const_done, 1)

            def load(s, l, n, dst, src):
                sp.wait_ge(lo_done[s], use(l, s, n) + 1)
                part(sp)
                sp.dma_start(dst, src).then_inc(raw_loaded[s], 16)

            with sp.Fori(0, DEPTH) as l:
                w_in_v = w_in[l].rearrange("(k p) n -> p k n", p=P)
                w_up_v = w_up[l].rearrange("(k p) n -> p k n", p=P)

                with sp.Fori(0, NPAIR) as hp:
                    for s in range(SLOTS):
                        load(s, l, use_m[s] + hp, raw_k(s), w_in_v[:, :, bass.ds(s * DH + hp * P, P)])
                load(3, l, use_out[3], raw[:, 3], w_out[l, 3 * P:4 * P, :])
                with sp.Fori(0, NPAIR) as hp:
                    for s in range(STICK_SLOTS):
                        load(s, l, use_s[s] + hp, raw_k(s), w_in_v[:, :, bass.ds(O_SB + s * DH + hp * P, P)])
                for s in range(STICK_SLOTS):
                    load(s, l, use_out[s], raw[:, s], w_out[l, s * P:(s + 1) * P, :])
                for s in range(SLOTS):
                    load(s, l, use_out[s] + 1, raw[:, s], w_out[l, (SLOTS + s) * P:(SLOTS + s + 1) * P, :])
                phase_start(sp, l, 4, "pe", "act", "dve", "pool")
                sp.wait_ge(resid_stored, l * 16 + 16)
                for t in range(TT):
                    if t >= 2:
                        sp.wait_ge(resid_new.sem, resid_new.at(l, t - 1))
                    sp.dma_start(rtile[:, t % 2], resid_v[:, t]).then_inc(rt_loaded[t % 2], 16)
                with sp.Fori(0, NG) as g:
                    for s in range(GROUP):
                        load(s, l, use_mlp[s] + g, raw_k(s), w_up_v[:, :, bass.ds((g * GROUP + s) * P, P)])
                    for s in range(GROUP):
                        load(GROUP + s, l, use_mlp[GROUP + s] + g, raw[:, GROUP + s],
                             w_down[l, bass.ds((g * GROUP + s) * P, P), :])
            phase_start(sp, DEPTH - 1, PHASES, "dve")
            sp.dma_start(out_v, resid[:]).then_inc(out_stored, 16)
            sp.wait_ge(out_stored, 16)

        @block.tensor
        def _(pe):
            def turn(l, n):
                pe.wait_ge(tile_ready.sem, tile_ready.at(l, n + 1))
                for b in range(2):
                    i = 2 * n + b
                    if i >= 4:
                        pe.wait_ge(turned_lo.sem, turned_lo.at(l, i - 3))
                    for k in range(4):
                        ins = pe.transpose(psum[i % 4][:, k * P:(k + 1) * P],
                                           turned[:, n % 2, (4 * b + k) * P:(4 * b + k + 1) * P], ident[:])
                    ins.then_inc(tile_turned.sem, 1)

            def project_half(l, s, n, h, bank):
                pe.wait_ge(lo_done[s], use(l, s, n) + 2)
                for k in range(KT):
                    for i, (a, b) in enumerate(PASSES):
                        ins = pe.matmul(psum[bank][:], spl_k(s, a)[:, k, :], act_t[:, b, k, h * HALF:(h + 1) * HALF],
                                        start=(k == 0 and i == 0), stop=(k == KT - 1 and i == 2))
                return ins

            def project_t(l, n):
                for s in (2, 3):
                    pe.wait_ge(lo_done[s], use(l, s, n) + 2)
                for t in range(TT):
                    dst = psum[4 + t // 2][:, (t % 2) * 2 * P:(t % 2 + 1) * 2 * P].rearrange("p (s n) -> p s n", s=2)
                    for k in range(KT):
                        for i, (a, b) in enumerate(PASSES):
                            ins = pe.matmul(dst, act_t[:, a, k, t * P:(t + 1) * P], spl[:, 2:4, b, k * P:(k + 1) * P],
                                            start=(k == 0 and i == 0), stop=(k == KT - 1 and i == 2))
                    if t % 2:
                        ins.then_inc(m_proj.sem, 1)

            def up(l, g, first=False):
                for i in range(UPS):
                    s, h = i // 2, i % 2
                    if h == 0:
                        pe.wait_ge(lo_done[s], use(l, s, use_mlp[s] + g) + 2)
                    if not first:
                        pe.wait_ge(squared.sem, squared.at(l, UPS * g + i + 1 - UPS))
                    for k in range(KT):
                        for q, (a, b) in enumerate(PASSES):
                            ins = pe.matmul(psum[i][:], spl_k(s, a)[:, k, :], act_t[:, b, k, h * HALF:(h + 1) * HALF],
                                            start=(k == 0 and q == 0), stop=(k == KT - 1 and q == 2))
                    ins.then_inc(up_psum.sem, 1)

            def down(l, g, buf, first=False):
                for s in range(GROUP):
                    pe.wait_ge(lo_done[GROUP + s], use(l, GROUP + s, use_mlp[GROUP + s] + g) + 2)
                for i in range(2 * TT):
                    t, h = i // 2, i % 2
                    if i == 0:
                        pe.wait_ge(hid_lo_done.sem, hid_lo_done.at(l, UPS * g + UPS))
                    if not (first and i < 4):
                        pe.wait_ge(down_add.sem, down_add.at(l, 2 * TT * g + i - 3))
                    for k in range(GROUP):
                        for q, (a, b) in enumerate(PASSES):
                            ins = pe.matmul(psum[4 + i % 4][:], hid[:, buf, a, k, t * P:(t + 1) * P],
                                            spl[:, GROUP + k, b, h * HALF:(h + 1) * HALF],
                                            start=(k == 0 and q == 0), stop=(k == GROUP - 1 and q == 2))
                    ins.then_inc(down_psum.sem, 1)

            pe.wait_ge(const_done, 1)
            with pe.Fori(0, DEPTH) as l:
                phase_start(pe, l, 0, "act", "dve")
                pe.wait_ge(small_loaded, (l + 1) * (16 * SMALL_DMAS))
                part(pe)
                pe.transpose(psum[7][:, 0:N_SMALL], small_rows[0:N_SMALL, :], ident[0:N_SMALL, 0:N_SMALL]).then_inc(small_pe.sem, 1)
                for t in range(TT):
                    turn(l, t)
                phase_end(pe, "pe")
                phase_start(pe, l, 1, "act", "dve")
                pe.wait_ge(wg_lo.sem, wg_lo.at(l, 1))
                for h in range(2):
                    for k in range(KT):
                        for i, (a, b) in enumerate(PASSES):
                            ins = pe.matmul(psum[6 + h][:], wg[:, a, k, :], act_t[:, b, k, h * HALF:(h + 1) * HALF],
                                            start=(k == 0 and i == 0), stop=(k == KT - 1 and i == 2))
                    ins.then_inc(gate_pe.sem, 1)
                pe.wait_ge(gate_dve.sem, gate_dve.at(l, 2))
                part(pe)
                for t in range(TT):
                    ins = pe.transpose(psum[4][:, t * 2 * NH:(t + 1) * 2 * NH], gt[:, t * P:(t + 1) * P], ident[0:2 * NH, 0:2 * NH])
                ins.then_inc(gate_pe.sem, 1)
                project_half(l, 0, use_m[0], 0, 0).then_inc(q_proj.sem, 1)
                pe.wait_ge(gate_dve.sem, gate_dve.at(l, 4))
                pe.matmul(psum[5][0:CH, 0:P], glog[:].rearrange("p t h -> p (t h)"), tri_f[:], start=True, stop=True)
                pe.matmul(psum[6][0:CH, 0:P], gi[:].rearrange("p t h -> p (t h)"), ident[:],
                          start=True, stop=True).then_inc(gate_pe.sem, 1)
                project_half(l, 0, use_m[0], 1, 1).then_inc(q_proj.sem, 1)
                pe.wait_ge(gate_dve.sem, gate_dve.at(l, 5))
                part(pe)
                pe.matmul(psum[7][0:1, 0:CH], brow[:, P - 1:P], ident[0:CH, 0:CH], start=True, stop=True)
                pe.matmul(psum[7][0:1, CH:2 * CH], cmax[:, 1, 64 + P - 1:64 + P], ident[0:CH, 0:CH],
                          start=True, stop=True).then_inc(gate_pe.sem, 1)
                pe.wait_ge(gate_dve.sem, gate_dve.at(l, 6))
                part(pe)
                pe.matmul(psum[4][0:CH, 0:1], mprev[:, :], ident[0:1, 0:1], start=True, stop=True).then_inc(gate_pe.sem, 1)
                pe.wait_ge(gate_dve.sem, gate_dve.at(l, 7))
                part(pe)
                pe.transpose(psum[5][:, 0:CH], arow[:], ident[0:CH, 0:CH])
                pe.transpose(psum[5][:, CH:2 * CH], frow[:], ident[0:CH, 0:CH]).then_inc(gate_pe.sem, 1)
                phase_end(pe, "pe")
                with pe.Fori(0, NPAIR) as hp:
                    for h in range(2):
                        project_half(l, 1, use_m[1] + hp, h, 2 + h).then_inc(m_proj.sem, 1)
                    pe.wait_ge(m_y.sem, m_y.at(l, 3 * hp))
                    phase_start(pe, l, 2, "act", "dve")
                    project_t(l, use_m[2] + hp)
                    pe.wait_ge(m_qk.sem, m_qk.at(l, 2 * hp + 2))

                    def scores(b):
                        for c in range(4 * b, 4 * b + 4):
                            for j in range(2):
                                cc, hs = slice(c * P, (c + 1) * P), slice(j * HD, (j + 1) * HD)
                                ins = pe.matmul(psum[2 + j][:, (c % 4) * P:(c % 4 + 1) * P], km[hs, cc], qm[hs, cc],
                                                start=True, stop=True)
                        ins.then_inc(m_s.sem, 1)

                    for b in range(2):
                        for c in range(4):
                            ins = pe.transpose(psum[b][:, c * P:(c + 1) * P], km[:, (4 * b + c) * P:(4 * b + c + 1) * P], ident[:])
                        ins.then_inc(m_kt.sem, 1)
                    scores(0)
                    pe.wait_ge(m_kw.sem, m_kw.at(l, hp + 1))
                    project_half(l, 0, use_m[0] + hp + 1, 0, 0).then_inc(q_proj.sem, 1)
                    pe.wait_ge(m_evac.sem, m_evac.at(l, 8 * hp + 8))

                    def updates(a, e, bank):
                        for c in range(a, e):
                            o = (c - a) * 2 * VW
                            ins = pe.matmul(psum[bank][:, o:o + 2 * VW], kw[:, c], vm[:, c].rearrange("p j v -> p (j v)"),
                                            start=True, stop=True)
                        ins.then_inc(m_u.sem, 1)

                    updates(*UPD_BANKS[0])
                    updates(*UPD_BANKS[1])
                    pe.wait_ge(m_w.sem, m_w.at(l, 2 * hp + 1))
                    scores(1)
                    project_half(l, 0, use_m[0] + hp + 1, 1, 1).then_inc(q_proj.sem, 1)
                    pe.wait_ge(m_w.sem, m_w.at(l, 2 * hp + 2))
                    updates(*UPD_BANKS[2])
                    pe.wait_ge(m_qs.sem, m_qs.at(l, hp + 1))
                    for a, e, bank in NUM_BANKS:
                        for c in range(a, e):
                            o = (c - a) * 2 * VW
                            if c:
                                pe.wait_ge(m_state.sem, m_state.at(l, (TT - 1) * hp + c))
                                pe.matmul(psum[bank][:, o:o + 2 * VW], qs[:, c], state[:, c - 1], start=True, stop=False,
                                          skip_group_check=True)
                            for j in range(2):
                                ins = pe.matmul(psum[bank][:, o + j * VW:o + (j + 1) * VW], nm[:, c, j, 0:P], vm[:, c, j],
                                                start=(c == 0), stop=(j == 1 or c == 0), skip_group_check=True)
                        ins.then_inc(m_num.sem, 1)
                phase_end(pe, "pe")
                phase_start(pe, l, 3, "act", "dve", "pool")
                def stick_pair(hp, more):
                    def norm_sum(n):
                        pe.wait_ge(s_sq.sem, s_sq.at(l, 4 * hp + n + 1))
                        pe.wait_ge(s_rs.sem, s_rs.at(l, 4 * hp + max(n - 1, 0)))
                        pe.matmul(psum[6 + n % 2][:], head_ones[:], sq[:, n % 2], start=True, stop=True).then_inc(s_sum.sem, 1)

                    pe.wait_ge(u_prob.sem, u_prob.at(l, hp * NU))
                    norm_sum(0)
                    project_half(l, 1, use_s[1] + hp, 0, 2).then_inc(s_proj.sem, 1)
                    norm_sum(1)
                    project_half(l, 1, use_s[1] + hp, 1, 3).then_inc(s_proj.sem, 1)
                    norm_sum(2)
                    pe.wait_ge(y_out.sem, y_out.at(l, 2 * hp))
                    project_half(l, 2, use_s[2] + hp, 0, 4).then_inc(s_proj.sem, 1)
                    norm_sum(3)
                    project_half(l, 2, use_s[2] + hp, 1, 5).then_inc(s_proj.sem, 1)

                    def scores(n):
                        b, k = units[n]
                        c0, c1, diag = span(n)
                        if n == 0:
                            pe.wait_ge(s_qk.sem, s_qk.at(l, 4 * hp + 4))
                        if n == 2:
                            pe.wait_ge(s_v.sem, s_v.at(l, 2 * hp + 2))
                        pe.wait_ge(u_prob.sem, u_prob.at(l, NU * hp + max(n - 2, 0)))
                        e = E_BANKS[n % 3]
                        for j in range(2):
                            hs = slice(j * HD, (j + 1) * HD)
                            ins = pe.matmul(psum[e + j][:, c0:HALF], qkt[hs, 1, k * P:(k + 1) * P],
                                            qkt[hs, 0, b * HALF + c0:(b + 1) * HALF],
                                            start=True, stop=False, skip_group_check=True)
                        if diag:
                            for j in range(2):
                                ins = pe.matmul(psum[e + j][:, c0:c1], ident_b[:], after_mask[:], start=False, stop=False,
                                                skip_group_check=True)
                        ins.then_inc(u_z.sem, 1)

                    def exponents(n):
                        c0, c1, diag = span(n)
                        e = E_BANKS[n % 3]
                        pe.wait_ge(u_lo.sem, u_lo.at(l, NU * hp + n + 1))
                        for j in range(2):
                            for h in range(2):
                                ins = pe.matmul(psum[e + j][:, c0:HALF], suffix[:], sph[:, n % 2, h, j, c0:HALF], start=False,
                                                stop=(h == 1 and c1 == HALF), skip_group_check=True)
                        if c1 < HALF:
                            pe.wait_ge(u_carry.sem, u_carry.at(l, NC * hp + carries(n)))
                            for j in range(2):
                                ins = pe.matmul(psum[e + j][:, c1:HALF], minus_ones[:], carry[:, n % 2, j, c1:HALF], start=False,
                                                stop=True, skip_group_check=True)
                        ins.then_inc(u_e.sem, 1)

                    def values(n):
                        b, k = units[n]
                        c0, _, _ = span(n)
                        pe.wait_ge(u_prob.sem, u_prob.at(l, NU * hp + n + 1))
                        if top(n) and b == 1:
                            pe.wait_ge(y_out.sem, y_out.at(l, 2 * hp + 1))
                        for j in range(2):
                            for q in range(c0 // P, SBLK):
                                ins = pe.matmul(psum[4 + j][:, q * HD:(q + 1) * HD], prob[:, n % 2, j, q * P:(q + 1) * P],
                                                vs[:, k, j * HD:(j + 1) * HD], start=top(n), stop=(k == 0), skip_group_check=True)
                        ins.then_inc(u_av.sem, 1)

                    for n in range(NU + 3):
                        if more and n > NU:
                            pe.wait_ge(u_prob.sem, u_prob.at(l, NU * hp + NU - 2))
                            h = n - NU - 1
                            project_half(l, 0, use_s[0] + hp + 1, h, h).then_inc(q_proj.sem, 1)
                        if 0 <= n - 2 < NU:
                            exponents(n - 2)
                        if n < NU:
                            scores(n)
                        if n == 0:
                            for h in range(2):
                                pe.wait_ge(s_vf.sem, s_vf.at(l, 2 * hp + h + 1))
                                for t in range(4):
                                    ins = pe.transpose(psum[6 + h][:, t * P:(t + 1) * P], vf[:, (4 * h + t) * P:(4 * h + t + 1) * P], ident[:])
                                ins.then_inc(s_vt.sem, 1)
                        if 0 <= n - 3 < NU:
                            values(n - 3)

                with pe.Fori(0, NPAIR - 1) as hp:
                    stick_pair(hp, True)
                stick_pair(NPAIR - 1, False)
                phase_end(pe, "pe")
                phase_start(pe, l, 4, "act", "dve")
                for t in range(TT):
                    turn(l, TT + t)
                for s in range(SLOTS):
                    pe.wait_ge(lo_done[s], use(l, s, use_out[s]) + 3)
                pe.wait_ge(turned_lo.sem, turned_lo.at(l, 4 * TT))
                for t in range(TT):
                    for h in range(2):
                        if t >= 2:
                            pe.wait_ge(resid_new.sem, resid_new.at(l, t - 1))
                        bank = psum[4 + 2 * (t % 2) + h]
                        for k in range(KT):
                            w = spl if k < SLOTS else wo_more
                            for i, (a, b) in enumerate(PASSES):
                                ins = pe.matmul(bank[:], act_t[:, a, k, t * P:(t + 1) * P],
                                                w[:, k % SLOTS, b, h * HALF:(h + 1) * HALF],
                                                start=(k == 0 and i == 0), stop=(k == KT - 1 and i == 2))
                        ins.then_inc(out_psum.sem, 1)
                    if t >= 1:
                        turn(l, 2 * TT + t - 1)
                turn(l, 3 * TT - 1)
                phase_end(pe, "pe")
                phase_start(pe, l, 5, "act", "dve")
                up(l, 0, first=True)
                up(l, 1)
                down(l, 0, 0, first=True)
                with pe.Fori(0, NG // 2 - 1) as m:
                    up(l, 2 * m + 2)
                    down(l, 2 * m + 1, 1)
                    up(l, 2 * m + 3)
                    down(l, 2 * m + 2, 0)
                down(l, NG - 1, 1)
                phase_end(pe, "pe")

        @block.scalar
        def _(act):
            def hi(s, l, n, dst):
                act.wait_ge(raw_loaded[s], (use(l, s, n) + 1) * 16)
                act.activation(dst, raw[:, s], ACT.Copy).then_inc(hi_done[s], 1)

            def turn_hi(l, n):
                t = n % TT
                for b in range(2):
                    act.wait_ge(tile_turned.sem, tile_turned.at(l, 2 * n + b + 1))
                    act.activation(act_t[:, 0, 4 * b:4 * b + 4, t * P:(t + 1) * P],
                                   psum[(2 * n + b) % 4][:].rearrange("p (k n) -> p k n", k=4), ACT.Copy).then_inc(turned_hi.sem, 1)

            def tile_scale(l, n, t):
                if n >= 2:
                    act.wait_ge(tile_turned.sem, tile_turned.at(l, 2 * (n - 1)))
                act.activation(turned[:, n % 2], resid[:, t], ACT.Square, accum_out=ssq[:, n % 2:n % 2 + 1])
                act.drain()
                act.activation(ssq[:, n % 2:n % 2 + 1], ssq[:, n % 2:n % 2 + 1], ACT.Ln, bias=eps_c[:, 0:1], scale=1.0 / D)
                act.drain()
                act.activation(rst[:, n % 2:n % 2 + 1], ssq[:, n % 2:n % 2 + 1], ACT.Exp, scale=-0.5).then_inc(scale_ready.sem, 1)

            act.preload_act_table_set("natural_log_exp_and_others")
            act.wait_ge(const_done, 1)
            with act.Fori(0, DEPTH) as l:
                phase_start(act, l, 0, "pe", "dve")
                act.dma_start(gain[:], attn_norm_g[l].unsqueeze(0).to_broadcast([P, D])).then_inc(gain_loaded, 16)
                act.dma_start(small_rows[ROW_W:ROW_B, :], conv_w[l].rearrange("j (t p) -> (j t) p", p=P)).then_inc(small_loaded, 16)
                act.dma_start(small_rows[ROW_B:ROW_Q, :], conv_b[l].rearrange("(t p) -> t p", p=P)).then_inc(small_loaded, 16)
                for r, g in ((ROW_Q, q_norm_g), (ROW_K, k_norm_g)):
                    for j in range(2):
                        act.dma_start(small_rows[r:r + 1, j * HD:(j + 1) * HD], g[l].unsqueeze(0)).then_inc(small_loaded, 16)
                act.dma_start(gate_bias[:, 0:NH], b_igate[l].unsqueeze(0).to_broadcast([P, NH])).then_inc(small_loaded, 16)
                act.dma_start(gate_bias[:, NH:2 * NH], b_fgate[l].unsqueeze(0).to_broadcast([P, NH])).then_inc(small_loaded, 16)
                act.dma_start(wg_raw[:], w_in[l].rearrange("(k p) n -> p k n", p=P)[:, :, 4 * DH:4 * DH + P]).then_inc(wg_loaded, 16)
                for t in range(TT + 1):
                    if t < TT:
                        act.wait_ge(x_loaded[t], 16)
                        tile_scale(l, t, t)
                    if t >= 1:
                        turn_hi(l, t - 1)
                    if 2 <= t < 4:
                        hi(t - 2, l, use_m[t - 2], spl[:, t - 2, 0])
                    if t == 4:
                        act.wait_ge(wg_loaded, 16 * (l + 1))
                        act.activation(wg[:, 0], wg_raw[:], ACT.Copy).then_inc(wg_hi.sem, 1)
                act.dma_start(resid_v, resid[:]).then_inc(resid_stored, 16)
                phase_end(act, "act")
                phase_start(act, l, 1, "dve")
                act.dma_start(gain[:], out_norm_g[l].unsqueeze(0).to_broadcast([P, D])).then_inc(gain_loaded, 16)
                act.wait_ge(gate_dve.sem, gate_dve.at(l, 3))
                act.activation(gabs[:], gabs[:], ACT.Exp, scale=-1.0)
                act.drain()
                act.activation(gabs[:], gabs[:], ACT.Ln, bias=1.0).then_inc(gate_act.sem, 1)
                for s in range(2, SLOTS):
                    hi(s, l, use_m[s], spl[:, s, 0])
                act.wait_ge(gate_dve.sem, gate_dve.at(l, 7))
                act.dma_start(rows_d, nrow[:]).then_inc(rows_stored, 16)
                act.wait_ge(gate_pe.sem, gate_pe.at(l, 7))
                act.activation(floor_col[:], psum[5][:, CH:2 * CH], ACT.Exp).then_inc(gate_act.sem, 1)
                act.wait_ge(rows_stored, (l + 1) * 16)
                phase_end(act, "act")
                phase_start(act, l, 2, "pe", "dve")
                with act.Fori(0, NPAIR) as hp:
                    act.wait_ge(m_num.sem, m_num.at(l, 3 * hp))
                    act.dma_start(nm[:], rows_d.rearrange("(c h) t -> c h t", c=TT)[:, bass.ds(2 * hp, 2), :].unsqueeze(0)
                                  .to_broadcast([P, TT, 2, P + 1])).then_inc(nm_loaded, 16)

                    def log_part(w):
                        act.wait_ge(m_abs.sem, m_abs.at(l, 3 * hp + w + 1))
                        act.activation(sig[:], sig[:], ACT.Exp, scale=-1.0)
                        act.drain()
                        act.activation(sig[:], sig[:], ACT.Ln, bias=1.0).then_inc(m_ln.sem, 1)

                    def sigmoid(w, buf):
                        act.wait_ge(m_log.sem, m_log.at(l, 3 * hp + w + 1))
                        act.activation(buf[:], buf[:], ACT.Exp).then_inc(m_sig.sem, 1)

                    for h in range(2):
                        act.wait_ge(q_proj.sem, q_proj.at(l, 2 * hp + h + 1))
                        if h == 0:
                            act.wait_ge(m_yms.sem, m_yms.at(l, hp))
                        act.activation(pre[:, CW - 1 + h * HALF:CW - 1 + (h + 1) * HALF], psum[h][:], ACT.Copy).then_inc(m_evac.sem, 1)
                    log_part(0)
                    act.wait_ge(m_args.sem, m_args.at(l, hp + 1))
                    act.activation(qs[:], qs[:], ACT.Exp)
                    act.activation(dec[:], dec[:], ACT.Exp).then_inc(m_exp.sem, 1)
                    sigmoid(0, sig)
                    act.wait_ge(m_conv.sem, m_conv.at(l, 2 * hp + 1))
                    for h in range(2):
                        act.wait_ge(m_proj.sem, m_proj.at(l, 6 * hp + h + 1))
                        act.activation(pre[:, CW - 1 + h * HALF:CW - 1 + (h + 1) * HALF], psum[2 + h][:], ACT.Copy).then_inc(m_evac.sem, 1)
                    act.wait_ge(m_masked.sem, m_masked.at(l, hp + 1))
                    act.activation(nm[:, :, :, 0:P], nm[:, :, :, 0:P], ACT.Exp).then_inc(m_exp.sem, 1)
                    for s in range(2):
                        hi(s, l, use_m[s] + hp + 1, spl[:, s, 0])
                    log_part(1)
                    sigmoid(1, sig)
                    act.wait_ge(m_gated.sem, m_gated.at(l, hp))
                    for b in range(4):
                        act.wait_ge(m_proj.sem, m_proj.at(l, 6 * hp + 3 + b))
                        src = psum[4 + b][:].rearrange("p (t s n) -> p t s n", t=2, s=2)
                        for t in range(2):
                            act.activation(vm[:, 2 * b + t, :, 0:HD], src[:, t, 0].rearrange("p (j d) -> p j d", j=2), ACT.Copy)
                        act.activation(og[:, 2 * b:2 * b + 2], src[:, :, 1], ACT.Copy).then_inc(m_evac.sem, 1)
                    for s in range(2, SLOTS):
                        hi(s, l, use_m[s] + hp + 1, spl[:, s, 0])
                    log_part(2)
                    sigmoid(2, og)
                    act.wait_ge(m_y.sem, m_y.at(l, 3 * (hp + 1)))
                    act.activation(pre[:, CW - 1:].rearrange("p (t n) -> p t n", t=TT), resid[:, :, bass.ds(hp * P, P)],
                                   ACT.Square).then_inc(m_ysq.sem, 1)
                    act.wait_ge(m_yms.sem, m_yms.at(l, hp + 1))
                    act.activation(mss[:], mss[:], ACT.Ln, bias=eps_c[:, 0:1], scale=1.0 / HD)
                    act.drain()
                    act.activation(mss[:], mss[:], ACT.Exp, scale=-0.5).then_inc(m_yrs.sem, 1)
                phase_end(act, "act")
                phase_start(act, l, 3, "pe", "dve")
                with act.Fori(0, NPAIR) as hp:
                    for n in range(4):
                        if n < 2:
                            act.wait_ge(q_proj.sem, q_proj.at(l, 2 * NPAIR + 2 * hp + n + 1))
                        else:
                            act.wait_ge(s_proj.sem, s_proj.at(l, 4 * hp + n - 1))
                        act.wait_ge(s_sum.sem, s_sum.at(l, 4 * hp + max(n - 1, 0)))
                        act.activation(sq[:, n % 2], psum[n][:], ACT.Square).then_inc(s_sq.sem, 1)
                        act.wait_ge(s_sum.sem, s_sum.at(l, 4 * hp + n + 1))
                        act.wait_ge(s_qk.sem, s_qk.at(l, 4 * hp + max(n - 1, 0)))
                        is_q = n < 2
                        act.activation(rs[:, n % 2], psum[6 + n % 2][:], ACT.Ln, scale=1.0 if is_q else 1.0 / HD,
                                       bias=eps_c[:, 1:2] if is_q else eps_c[:, 0:1])
                        act.drain()
                        act.activation(rs[:, n % 2], rs[:, n % 2], ACT.Exp, scale=-0.5).then_inc(s_rs.sem, 1)
                    for h in range(2):
                        act.wait_ge(s_proj.sem, s_proj.at(l, 4 * hp + 3 + h))
                        act.activation(vf[:, h * HALF:(h + 1) * HALF], psum[4 + h][:], ACT.Copy).then_inc(s_vf.sem, 1)

                    def log_part(n):
                        u = sp_[:, n % 2, :, span(n)[0]:HALF]
                        act.wait_ge(u_abs.sem, u_abs.at(l, NU * hp + n + 1))
                        act.activation(u, u, ACT.Exp, scale=-1.0)
                        act.drain()
                        act.activation(u, u, ACT.Ln, bias=1.0).then_inc(u_ln.sem, 1)

                    def hi_part(n):
                        c0, _, _ = span(n)
                        act.wait_ge(u_sp.sem, u_sp.at(l, NU * hp + n + 1))
                        act.wait_ge(u_e.sem, u_e.at(l, NU * hp + max(n - 1, 0)))
                        act.activation(sph[:, n % 2, 0, :, c0:HALF], sp_[:, n % 2, :, c0:HALF], ACT.Copy).then_inc(u_hi.sem, 1)

                    def weights(n):
                        c0, _, _ = span(n)
                        act.wait_ge(u_e.sem, u_e.at(l, NU * hp + n + 1))
                        act.wait_ge(u_av.sem, u_av.at(l, NU * hp + max(n - 1, 0)))
                        act.activation(prob[:, n % 2, :, c0:HALF], logits(n), ACT.Exp).then_inc(u_prob.sem, 1)

                    def square_out(n):
                        b, k = units[n]
                        if k == 0:
                            act.wait_ge(y_out.sem, y_out.at(l, 2 * hp + b + 1))
                            act.activation(ysq[:].rearrange("p j (t d) -> p j t d", d=HD), y_store(b, hp), ACT.Square).then_inc(y_sq.sem, 1)

                    def root(n):
                        b, k = units[n]
                        if k == 0:
                            act.wait_ge(y_ms.sem, y_ms.at(l, 2 * hp + b + 1))
                            act.activation(yss[:], yss[:], ACT.Ln, bias=eps_c[:, 0:1], scale=1.0 / HD)
                            act.drain()
                            act.activation(yss[:], yss[:], ACT.Exp, scale=-0.5).then_inc(y_rs.sem, 1)

                    for n in range(NU + 5):
                        if 0 <= n - 1 < NU:
                            hi_part(n - 1)
                        if 0 <= n - 2 < NU:
                            weights(n - 2)
                        if n < NU:
                            log_part(n)
                        if n == 0:
                            for h in range(2):
                                act.wait_ge(s_vt.sem, s_vt.at(l, 2 * hp + h + 1))
                                act.activation(vs[:, 4 * h:4 * h + 4], psum[6 + h][:].rearrange("p (t n) -> p t n", t=4), ACT.Copy).then_inc(s_v.sem, 1)
                        if 3 <= n < 3 + STICK_SLOTS:
                            hi(n - 3, l, use_s[n - 3] + hp + 1, spl[:, n - 3, 0])
                        if 0 <= n - 4 < NU:
                            square_out(n - 4)
                        if 0 <= n - 5 < NU:
                            root(n - 5)
                phase_end(act, "act")
                phase_start(act, l, 4, "pe", "dve", "pool")
                for s in range(SLOTS):
                    hi(s, l, use_out[s] + 1, wo_more[:, s, 0])
                for t in range(TT):
                    turn_hi(l, TT + t)
                act.dma_start(gain[:], mlp_norm_g[l].unsqueeze(0).to_broadcast([P, D])).then_inc(gain_loaded, 16)
                for t in range(TT + 1):
                    if t < TT:
                        act.wait_ge(resid_new.sem, resid_new.at(l, t + 1))
                        tile_scale(l, 2 * TT + t, t)
                    if t >= 1:
                        turn_hi(l, 2 * TT + t - 1)
                act.wait_ge(out_psum.sem, out_psum.at(l, 2 * TT))
                for s in range(SLOTS):
                    hi(s, l, use_mlp[s], spl[:, s, 0])
                phase_end(act, "act")
                phase_start(act, l, 5, "pe", "dve")

                def hidden(l, g, buf, more):
                    for i in range(UPS + 1):
                        if i < UPS:
                            act.wait_ge(up_psum.sem, up_psum.at(l, UPS * g + i + 1))
                            if not (more == "first" and i < 2):
                                act.wait_ge(squared.sem, squared.at(l, UPS * g + i - 1))
                            act.activation(h1[:, i % 2], psum[i][:], ACT.Relu).then_inc(relu.sem, 1)
                        if i >= 1:
                            q = i - 1
                            act.wait_ge(squared.sem, squared.at(l, UPS * g + q + 1))
                            act.activation(hid[:, buf, 0, q // 2, (q % 2) * HALF:(q % 2 + 1) * HALF], h2[:, q % 2], ACT.Copy).then_inc(hid_hi_done.sem, 1)
                    if more:
                        for s in range(GROUP):
                            hi(s, l, use_mlp[s] + g + 1, spl[:, s, 0])

                def next_down(l, g):
                    act.wait_ge(down_psum.sem, down_psum.at(l, 2 * TT * (g + 1)))
                    for s in range(GROUP, SLOTS):
                        hi(s, l, use_mlp[s] + g + 1, spl[:, s, 0])

                hidden(l, 0, 0, "first")
                hidden(l, 1, 1, "yes")
                next_down(l, 0)
                with act.Fori(0, NG // 2 - 2) as m:
                    hidden(l, 2 * m + 2, 0, "yes")
                    next_down(l, 2 * m + 1)
                    hidden(l, 2 * m + 3, 1, "yes")
                    next_down(l, 2 * m + 2)
                hidden(l, NG - 2, 0, "yes")
                next_down(l, NG - 3)
                hidden(l, NG - 1, 1, None)
                next_down(l, NG - 2)
                phase_end(act, "act")

        @block.gpsimd
        def _(pool):
            def lo(s, l, n, dst):
                pool.wait_ge(hi_done[s], use(l, s, n) + 1)
                pool.tensor_tensor(dst[:, 1], raw[:, s], dst[:, 0].bitcast(F32), ALU.subtract).then_inc(lo_done[s], 1)

            for s in from_one:
                pool.sem_inc(s, 1)

            def select(dst, value, op, step):
                pool.memset(dst, value)
                pool.drain()
                pool.affine_select(out=dst, in_=dst, compare_op=op, fill=0.0, base=0, pattern=[[step, P]],
                                   channel_multiplier=-step)
                pool.drain()

            select(ident[:], 1.0, ALU.is_equal, 1)
            select(tri_f[:], 1.0, ALU.is_ge, 1)
            select(minus_ones[:], -1.0, ALU.is_ge, -1)
            pool.tensor_copy(suffix[:], minus_ones[:])
            pool.drain()
            select(minus_ones[:], MASKED, ALU.is_ge, -1)
            pool.tensor_copy(after_mask[:], minus_ones[:])
            pool.tensor_copy(ident_b[:], ident[:])
            pool.drain()
            pool.memset(minus_ones[:], -1.0)
            pool.memset(head_ones[:], 0.0)
            pool.memset(eps_c[:, 0:1], EPS)
            pool.memset(eps_c[:, 1:2], HD * EPS)
            pool.drain()
            for j in range(2):
                pool.memset(head_ones[j * HD:(j + 1) * HD, j * HD:(j + 1) * HD], 1.0)
            pool.drain().then_inc(const_done, 1)
            with pool.Fori(0, DEPTH) as l:
                for s in range(2):
                    lo(s, l, use_m[s], spl[:, s])
                pool.wait_ge(wg_hi.sem, wg_hi.at(l, 1))
                pool.tensor_tensor(wg[:, 1], wg_raw[:], wg[:, 0].bitcast(F32), ALU.subtract).then_inc(wg_lo.sem, 1)
                phase_end(pool, "pool")
                for s in range(2, SLOTS):
                    lo(s, l, use_m[s], spl[:, s])
                phase_end(pool, "pool")
                with pool.Fori(0, NPAIR) as hp:
                    pool.wait_ge(nm_loaded, (l * NPAIR + hp + 1) * 16)
                    pool.wait_ge(m_args.sem, m_args.at(l, hp + 1))
                    part(pool)
                    acol = a_col[:].rearrange("p (c h) -> p c h", c=TT)[:, :, bass.ds(2 * hp, 2)]
                    pool.tensor_tensor(nm[:, :, :, 0:P], nm[:, :, :, 0:P], acol.unsqueeze(3).to_broadcast([P, TT, 2, P]), ALU.add)
                    pool.drain()
                    view = nm[:].rearrange("p c j t -> p (c j) t")[:, :, 0:P]
                    pool.affine_select(out=view, in_=view, compare_op=ALU.is_ge, fill=MASKED, base=0,
                                       pattern=[[0, 2 * TT], [1, P]], channel_multiplier=-1).then_inc(m_masked.sem, 1)
                    for s in range(SLOTS):
                        lo(s, l, use_m[s] + hp + 1, spl[:, s])
                    pool.wait_ge(m_yrs.sem, m_yrs.at(l, hp + 1))
                    part(pool)
                    yv = resid[:, :, bass.ds(hp * P, P)].rearrange("p t (j d) -> p t j d", j=2)
                    pool.tensor_tensor(yv, yv, mss[:].rearrange("p (t j) -> p t j", j=2).unsqueeze(3).to_broadcast([P, TT, 2, HD]), ALU.mult)
                    pool.drain()
                    yw = resid[:, :, bass.ds(hp * P, P)]
                    pool.tensor_tensor(yw, yw, og[:], ALU.mult).then_inc(m_gated.sem, 1)
                phase_end(pool, "pool")
                phase_start(pool, l, 3, "pe", "dve", "act")
                with pool.Fori(0, NPAIR) as hp:
                    for n in range(NU):
                        _, k = units[n]
                        c0, c1, diag = span(n)
                        if k:
                            pool.wait_ge(u_sp.sem, u_sp.at(l, NU * hp + n + 1))
                            pool.wait_ge(u_carry.sem, u_carry.at(l, NC * hp + carries(n)))
                            pool.wait_ge(u_e.sem, u_e.at(l, NU * hp + n))
                            part(pool)
                            dst, src = carry[:, (n + 1) % 2], carry[:, n % 2]
                            if diag:
                                ins = pool.tensor_copy(dst[:, :, c0:c1], sp_[:, n % 2, :, c0:c1])
                            if c1 < HALF:
                                ins = pool.tensor_tensor(dst[:, :, c1:HALF], src[:, :, c1:HALF], sp_[:, n % 2, :, c1:HALF], ALU.add)
                            ins.then_inc(u_carry.sem, 1)
                        if 3 <= n < 3 + STICK_SLOTS:
                            lo(n - 3, l, use_s[n - 3] + hp + 1, spl[:, n - 3])
                phase_end(pool, "pool")
                for s in range(SLOTS):
                    lo(s, l, use_out[s] + 1, wo_more[:, s])
                for s in range(SLOTS):
                    lo(s, l, use_mlp[s], spl[:, s])
                phase_end(pool, "pool")
                def hid_lo(l, g, buf, more):
                    for q in range(UPS):
                        pool.wait_ge(hid_hi_done.sem, hid_hi_done.at(l, UPS * g + q + 1))
                        cols = slice((q % 2) * HALF, (q % 2 + 1) * HALF)
                        pool.tensor_tensor(hid[:, buf, 1, q // 2, cols], h2[:, q % 2], hid[:, buf, 0, q // 2, cols].bitcast(F32),
                                           ALU.subtract).then_inc(hid_lo_done.sem, 1)
                    if more:
                        for s in range(GROUP):
                            lo(s, l, use_mlp[s] + g + 1, spl[:, s])

                def next_down(l, g):
                    for s in range(GROUP, SLOTS):
                        lo(s, l, use_mlp[s] + g + 1, spl[:, s])

                hid_lo(l, 0, 0, True)
                hid_lo(l, 1, 1, True)
                next_down(l, 0)
                with pool.Fori(0, NG // 2 - 2) as m:
                    hid_lo(l, 2 * m + 2, 0, True)
                    next_down(l, 2 * m + 1)
                    hid_lo(l, 2 * m + 3, 1, True)
                    next_down(l, 2 * m + 2)
                hid_lo(l, NG - 2, 0, True)
                next_down(l, NG - 3)
                hid_lo(l, NG - 1, 1, False)
                next_down(l, NG - 2)
                phase_end(pool, "pool")

        @block.vector
        def _(dve):
            def turn_lo(l, n):
                t = n % TT
                for b in range(2):
                    dve.wait_ge(turned_hi.sem, turned_hi.at(l, 2 * n + b + 1))
                    cells = (slice(None), slice(4 * b, 4 * b + 4), slice(t * P, (t + 1) * P))
                    dve.tensor_tensor(act_t[:, 1][cells], psum[(2 * n + b) % 4][:].rearrange("p (k n) -> p k n", k=4),
                                      act_t[:, 0][cells].bitcast(F32), ALU.subtract).then_inc(turned_lo.sem, 1)

            def normed_tile(l, n, t, scale_no):
                dve.wait_ge(scale_ready.sem, scale_ready.at(l, scale_no))
                dve.scalar_tensor_tensor(out=turned[:, n % 2], in0=resid[:, t], scalar=rst[:, n % 2:n % 2 + 1],
                                         in1=gain[:], op0=ALU.mult, op1=ALU.mult).then_inc(tile_ready.sem, 1)

            dve.wait_ge(const_done, 1)
            with dve.Fori(0, DEPTH) as l:
                phase_start(dve, l, 0, "pe", "act")
                dve.wait_ge(gain_loaded, (l * 3 + 1) * 16)
                for t in range(TT + 1):
                    if t < TT:
                        normed_tile(l, t, t, t + 1)
                    if t >= 1:
                        turn_lo(l, t - 1)
                dve.wait_ge(small_pe.sem, small_pe.at(l, 1))
                dve.tensor_copy(small_cols[:, 0:N_SMALL], psum[7][:, 0:N_SMALL])
                phase_end(dve, "dve")
                phase_start(dve, l, 1, "act")
                dve.wait_ge(small_loaded, (l + 1) * (16 * SMALL_DMAS))
                for b in range(2):
                    dve.memset(cmax[:, b, 0:64], MASKED)
                for h in range(2):
                    dve.wait_ge(gate_pe.sem, gate_pe.at(l, h + 1))
                    dve.tensor_copy(gt[:, h * HALF:(h + 1) * HALF], psum[6 + h][0:2 * NH, :]).then_inc(gate_dve.sem, 1)
                dve.wait_ge(gate_pe.sem, gate_pe.at(l, 3))
                dve.tensor_tensor(gsb[:], psum[4][:, 0:TT * 2 * NH].rearrange("p (t g) -> p t g", t=TT),
                                  gate_bias[:].unsqueeze(1).to_broadcast([P, TT, 2 * NH]), ALU.add)
                dve.drain()
                gf = gsb[:, :, NH:2 * NH]
                dve.tensor_scalar(gabs[:].bitcast(I32), gf.bitcast(I32), NO_SIGN, None, ALU.bitwise_and).then_inc(gate_dve.sem, 1)
                dve.tensor_copy(gi[:], gsb[:, :, 0:NH])
                dve.wait_ge(gate_act.sem, gate_act.at(l, 1))
                dve.scalar_tensor_tensor(out=glog[:], in0=gf, scalar=0.0, in1=gabs[:], op0=ALU.min, op1=ALU.subtract).then_inc(gate_dve.sem, 1)
                dve.wait_ge(gate_pe.sem, gate_pe.at(l, 4))
                dve.tensor_copy(brow[:], psum[5][0:CH, 0:P])
                dve.drain()
                dve.tensor_tensor(arow[:], psum[6][0:CH, 0:P], brow[:], ALU.subtract)
                dve.drain()
                dve.tensor_copy(cmax[:, 0, 64:], arow[:])
                dve.drain()
                for n in range(7):
                    a, b = cmax[:, n % 2], cmax[:, 1 - n % 2]
                    ins = dve.tensor_tensor(b[:, 64:], a[:, 64:], a[:, 64 - 2 ** n:64 + P - 2 ** n], ALU.max)
                    if n < 6:
                        dve.drain()
                ins.then_inc(gate_dve.sem, 1)
                dve.wait_ge(gate_pe.sem, gate_pe.at(l, 5))
                dve.tensor_copy(lastv[:].rearrange("p a n -> p (a n)"), psum[7][0:1, 0:2 * CH])
                dve.memset(mprev[:, 0:NH], 0.0)
                dve.drain()
                for c in range(TT - 1):
                    cur, nxt = mprev[:, c * NH:(c + 1) * NH], mprev[:, (c + 1) * NH:(c + 2) * NH]
                    dve.tensor_tensor(nxt, cur, lastv[:, 1, c * NH:(c + 1) * NH], ALU.max)
                    dve.drain()
                    ins = dve.tensor_tensor(nxt, nxt, lastv[:, 0, c * NH:(c + 1) * NH], ALU.add)
                    if c < TT - 2:
                        dve.drain()
                ins.then_inc(gate_dve.sem, 1)
                dve.wait_ge(gate_pe.sem, gate_pe.at(l, 6))
                dve.tensor_copy(mpcol[:], psum[4][0:CH, 0:1])
                dve.drain()
                dve.tensor_scalar(nrow[:, 0:P], cmax[:, 1, 64:], mpcol[:, 0:1], -1.0, ALU.max, ALU.mult)
                dve.tensor_copy(nrow[:, P:P + 1], mpcol[:])
                dve.drain()
                dve.tensor_tensor(frow[:], nrow[:, 0:P], brow[:], ALU.subtract).then_inc(gate_dve.sem, 1)
                dve.wait_ge(gate_pe.sem, gate_pe.at(l, 7))
                dve.wait_ge(gate_act.sem, gate_act.at(l, 2))
                dve.tensor_copy(a_col[:], psum[5][:, 0:CH])
                phase_end(dve, "dve")
                phase_start(dve, l, 2, "pe", "act")
                dve.wait_ge(resid_stored, (l + 1) * 16)
                dve.memset(pre[:, 0:CW - 1], 0.0)
                dve.memset(vm[:, :, :, HD:VW], 1.0)
                dve.memset(state[:], 0.0)
                dve.drain()
                with dve.Fori(0, NPAIR) as hp:
                    def absolute(src):
                        dve.tensor_scalar(sig[:].bitcast(I32), src.bitcast(I32), NO_SIGN, None, ALU.bitwise_and).then_inc(m_abs.sem, 1)

                    def log_sigmoid(w, dst, u):
                        dve.wait_ge(m_ln.sem, m_ln.at(l, 3 * hp + w + 1))
                        dve.scalar_tensor_tensor(out=dst, in0=u, scalar=0.0, in1=sig[:], op0=ALU.min, op1=ALU.subtract).then_inc(m_log.sem, 1)

                    for w, dst in ((0, qm), (1, km)):
                        dve.wait_ge(m_evac.sem, m_evac.at(l, 8 * hp + 2 * w + 2))

                        def tap(j):
                            return small_cols[:, bass.ds(ROW_W + j * KT + w * NPAIR + hp, 1)]

                        dve.tensor_scalar(dst[:], pre[:, 0:SEQ], tap(0), small_cols[:, bass.ds(ROW_B + w * NPAIR + hp, 1)],
                                          ALU.mult, ALU.add)
                        for j in range(1, CW):
                            dve.drain()
                            ins = dve.scalar_tensor_tensor(out=dst[:], in0=pre[:, j:j + SEQ], scalar=tap(j), in1=dst[:],
                                                           op0=ALU.mult, op1=ALU.add)
                        ins.then_inc(m_conv.sem, 1)
                        dve.drain()
                        absolute(dst[:])
                        if w == 0:
                            dve.wait_ge(nm_loaded, (l * NPAIR + hp + 1) * 16)
                            for j in range(2):
                                hs = slice(j * HD, (j + 1) * HD)
                                dve.tensor_tensor(qs[hs], nm[hs, :, j, 0:P], nm[hs, :, j, P:P + 1].to_broadcast([HD, TT, P]), ALU.add)
                            dve.tensor_tensor(dec[:], nm[:, :, :, P - 1], nm[:, :, :, P], ALU.add).then_inc(m_args.sem, 1)
                        log_sigmoid(w, sig[:], dst[:])
                        dve.wait_ge(m_sig.sem, m_sig.at(l, 3 * hp + w + 1))
                        dve.scalar_tensor_tensor(out=dst[:], in0=dst[:], scalar=QSC if w == 0 else 1.0, in1=sig[:],
                                                 op0=ALU.mult, op1=ALU.mult).then_inc(m_qk.sem, 1)
                    dve.drain()
                    dve.wait_ge(m_exp.sem, m_exp.at(l, 2 * hp + 2))
                    dve.tensor_tensor(qs[:], qs[:], qm[:].rearrange("p (c t) -> p c t", c=TT), ALU.mult).then_inc(m_qs.sem, 1)
                    for b in range(2):
                        dve.wait_ge(m_kt.sem, m_kt.at(l, 2 * hp + b + 1))
                        for j in range(2):
                            ins = dve.tensor_tensor(kw[:, 4 * b:4 * b + 4, j * HD:(j + 1) * HD],
                                                    psum[b][:].rearrange("p (c n) -> p c n", c=4)[:, :, j * HD:(j + 1) * HD],
                                                    nm[:, 4 * b:4 * b + 4, j, P - 1:P].to_broadcast([P, 4, HD]), ALU.mult)
                    ins.then_inc(m_kw.sem, 1)
                    dve.drain()

                    def weigh(b):
                        dve.wait_ge(m_s.sem, m_s.at(l, 2 * hp + b + 1))
                        d = nm[:, 4 * b:4 * b + 4, :, 0:P]
                        dve.tensor_tensor(d, banks[:, 2:4].rearrange("p j (c t) -> p c j t", c=4), d, ALU.mult).then_inc(m_w.sem, 1)

                    weigh(0)
                    dve.wait_ge(m_evac.sem, m_evac.at(l, 8 * hp + 8))
                    absolute(og[:].rearrange("p t n -> p (t n)"))
                    for c in range(1, TT):
                        a, bank = UPD_BANK[c - 1]
                        if c == TT - 1:
                            weigh(1)
                        if c - 1 == a:
                            dve.wait_ge(m_u.sem, m_u.at(l, 3 * hp + a // 3 + 1))
                        for j in range(2):
                            hs = slice(j * HD, (j + 1) * HD)
                            upd = psum[bank][hs, ((c - 1 - a) * 2 + j) * VW:((c - 1 - a) * 2 + j + 1) * VW]
                            new = state[hs, c - 1, j * VW:(j + 1) * VW]
                            if c == 1:
                                ins = dve.tensor_copy(new, upd)
                            else:
                                ins = dve.scalar_tensor_tensor(out=new, in0=state[hs, c - 2, j * VW:(j + 1) * VW],
                                                               scalar=dec[hs, c - 1, j:j + 1], in1=upd, op0=ALU.mult, op1=ALU.add)
                        ins.then_inc(m_state.sem, 1)
                        dve.drain()
                    log_sigmoid(2, og[:].rearrange("p t n -> p (t n)"), og[:].rearrange("p t n -> p (t n)"))
                    floors = floor_col[:].rearrange("p (c h) -> p c h", c=TT)
                    for i, (a, e, bank) in enumerate(NUM_BANKS):
                        dve.wait_ge(m_num.sem, m_num.at(l, 3 * hp + i + 1))
                        num = psum[bank][:, 0:(e - a) * 2 * VW].rearrange("p (c j v) -> p c j v", j=2, v=VW)
                        dve.tensor_scalar(dd[:, a:e].bitcast(I32), num[:, :, :, HD].bitcast(I32), NO_SIGN, None, ALU.bitwise_and)
                        dve.drain()
                        dve.tensor_tensor(dd[:, a:e], dd[:, a:e], floors[:, a:e, bass.ds(2 * hp, 2)], ALU.max)
                        dve.drain()
                        dve.reciprocal(dd[:, a:e], dd[:, a:e])
                        dve.drain()
                        dve.tensor_tensor(resid[:, a:e, bass.ds(hp * P, P)].rearrange("p c (j d) -> p c j d", j=2), num[:, :, :, 0:HD],
                                          dd[:, a:e].unsqueeze(3).to_broadcast([P, e - a, 2, HD]), ALU.mult).then_inc(m_y.sem, 1)
                    dve.wait_ge(m_ysq.sem, m_ysq.at(l, hp + 1))
                    dve.wait_ge(m_gated.sem, m_gated.at(l, hp))
                    dve.tensor_reduce(mss[:], pre[:, CW - 1:].rearrange("p (n d) -> p n d", d=HD), AX.X, ALU.add).then_inc(m_yms.sem, 1)
                phase_end(dve, "dve")
                phase_start(dve, l, 3, "pe", "act", "pool")
                with dve.Fori(0, NPAIR) as hp:
                    for n in range(4):
                        dve.wait_ge(s_rs.sem, s_rs.at(l, 4 * hp + n + 1))
                        row = ROW_Q if n < 2 else ROW_K
                        dve.scalar_tensor_tensor(out=qkt[:, n // 2, (n % 2) * HALF:(n % 2 + 1) * HALF], in0=psum[n][:],
                                                 scalar=small_cols[:, row:row + 1], in1=rs[:, n % 2], op0=ALU.mult, op1=ALU.mult).then_inc(s_qk.sem, 1)

                    def absolute(n):
                        dve.wait_ge(u_z.sem, u_z.at(l, NU * hp + n + 1))
                        if n == 1:
                            dve.wait_ge(s_vt.sem, s_vt.at(l, 2 * hp + 2))
                        dve.wait_ge(u_carry.sem, u_carry.at(l, NC * hp + carries(n - 1)))
                        dve.tensor_scalar(sp_[:, n % 2, :, span(n)[0]:HALF].bitcast(I32), logits(n).bitcast(I32), NO_SIGN, None,
                                          ALU.bitwise_and).then_inc(u_abs.sem, 1)

                    def softplus(n):
                        dve.wait_ge(u_ln.sem, u_ln.at(l, NU * hp + n + 1))
                        u = sp_[:, n % 2, :, span(n)[0]:HALF]
                        dve.scalar_tensor_tensor(out=u, in0=logits(n), scalar=0.0, in1=u, op0=ALU.max, op1=ALU.add).then_inc(u_sp.sem, 1)

                    def lo_part(n):
                        c0, _, _ = span(n)
                        dve.wait_ge(u_hi.sem, u_hi.at(l, NU * hp + n + 1))
                        dve.tensor_tensor(sph[:, n % 2, 1, :, c0:HALF], sp_[:, n % 2, :, c0:HALF],
                                          sph[:, n % 2, 0, :, c0:HALF].bitcast(F32), ALU.subtract).then_inc(u_lo.sem, 1)

                    def store(n):
                        b, k = units[n]
                        if k == 0:
                            dve.wait_ge(u_av.sem, u_av.at(l, NU * hp + n + 1))
                            dve.tensor_copy(y_store(b, hp), banks[:, 4:6, 0:SBLK * HD].rearrange("p j (t d) -> p j t d", d=HD)).then_inc(y_out.sem, 1)

                    def mean(n):
                        b, k = units[n]
                        if k == 0:
                            dve.wait_ge(y_sq.sem, y_sq.at(l, 2 * hp + b + 1))
                            dve.tensor_reduce(yss[:], ysq[:].rearrange("p j (t d) -> p (j t) d", d=HD), AX.X, ALU.add).then_inc(y_ms.sem, 1)

                    def norm(n):
                        b, k = units[n]
                        if k == 0:
                            dve.wait_ge(y_rs.sem, y_rs.at(l, 2 * hp + b + 1))
                            dve.tensor_tensor(y_store(b, hp), y_store(b, hp),
                                              yss[:].rearrange("p (j t) -> p j t", j=2).unsqueeze(3).to_broadcast([P, 2, SBLK, HD]), ALU.mult)

                    for n in range(NU + 6):
                        if 0 <= n - 1 < NU:
                            lo_part(n - 1)
                        if n < NU:
                            absolute(n)
                            softplus(n)
                        if 0 <= n - 3 < NU:
                            store(n - 3)
                        if 0 <= n - 4 < NU:
                            mean(n - 4)
                        if 0 <= n - 6 < NU:
                            norm(n - 6)
                phase_end(dve, "dve")
                phase_start(dve, l, 4, "pe", "act", "pool")
                dve.wait_ge(gain_loaded, (l * 3 + 2) * 16)
                for t in range(TT + 1):
                    if t < TT:
                        if t >= 2:
                            dve.wait_ge(tile_turned.sem, tile_turned.at(l, 2 * (TT + t - 1)))
                        dve.tensor_tensor(turned[:, t % 2], resid[:, t], gain[:], ALU.mult).then_inc(tile_ready.sem, 1)
                    if t >= 1:
                        turn_lo(l, TT + t - 1)
                for t in range(TT + 1):
                    if t < TT:
                        dve.wait_ge(rt_loaded[t % 2], (l * (TT // 2) + t // 2 + 1) * 16)
                        for h in range(2):
                            dve.wait_ge(out_psum.sem, out_psum.at(l, 2 * t + h + 1))
                            cols = slice(h * HALF, (h + 1) * HALF)
                            ins = dve.tensor_tensor(resid[:, t, cols], psum[4 + 2 * (t % 2) + h][:], rtile[:, t % 2, cols], ALU.add)
                        ins.then_inc(resid_new.sem, 1)
                        if t == 0:
                            dve.wait_ge(gain_loaded, (l * 3 + 3) * 16)
                        normed_tile(l, 2 * TT + t, t, TT + t + 1)
                    if t >= 1:
                        turn_lo(l, 2 * TT + t - 1)
                phase_end(dve, "dve")
                phase_start(dve, l, 5, "pe", "act", "pool")

                def square(l, g, first):
                    for i in range(UPS):
                        dve.wait_ge(relu.sem, relu.at(l, UPS * g + i + 1))
                        if not (first and i < 2):
                            dve.wait_ge(hid_lo_done.sem, hid_lo_done.at(l, UPS * g + i - 1))
                        dve.scalar_tensor_tensor(out=h2[:, i % 2], in0=psum[i][:], scalar=0.0, in1=h1[:, i % 2],
                                                 op0=ALU.max, op1=ALU.mult).then_inc(squared.sem, 1)

                def add(l, g):
                    for i in range(2 * TT):
                        dve.wait_ge(down_psum.sem, down_psum.at(l, 2 * TT * g + i + 1))
                        r = resid[:, i // 2, (i % 2) * HALF:(i % 2 + 1) * HALF]
                        dve.tensor_tensor(r, psum[4 + i % 4][:], r, ALU.add).then_inc(down_add.sem, 1)

                square(l, 0, True)
                square(l, 1, False)
                add(l, 0)
                with dve.Fori(0, NG // 2 - 1) as m:
                    square(l, 2 * m + 2, False)
                    add(l, 2 * m + 1)
                    square(l, 2 * m + 3, False)
                    add(l, 2 * m + 2)
                add(l, NG - 1)
                phase_end(dve, "dve")


_INS = ["x", "attn_norm_g", "w_in", "conv_w", "conv_b", "b_igate", "b_fgate", "q_norm_g", "k_norm_g", "out_norm_g",
        "w_out", "mlp_norm_g", "w_up", "w_down"]


def kernel(**inputs):
    import numpy as np
    import concourse.bacc as bacc
    from concourse.bass_utils import run_bass_kernel_spmd

    nc = bacc.Bacc("TRN2", target_bir_lowering=False, num_devices=1)
    arrays, args = {}, []
    for name in _INS:
        a = np.ascontiguousarray(inputs[name])
        arrays[f"in_{name}"] = a
        args.append(nc.dram_tensor(f"in_{name}", a.shape, mybir.dt.from_np(a.dtype), kind="ExternalInput").ap())
    out = nc.dram_tensor("out_x", inputs["x"].shape, F32, kind="ExternalOutput").ap()
    trunk(nc, *args, out)
    r = run_bass_kernel_spmd(nc, [arrays], core_ids=[0])
    return r.results[0]["out_x"]
```

```python
from contextlib import ExitStack

import concourse.bass as bass
from concourse import mybir

F32 = mybir.dt.float32
F32R = mybir.dt.float32r
BF16 = mybir.dt.bfloat16
I32 = mybir.dt.int32
ALU = mybir.AluOpType
ACT = mybir.ActivationFunctionType
AX = mybir.AxisListType

P = 128
EPS = 1e-6
NO_SIGN = 0x7FFFFFFF
MASKED = -float(2 ** 100)


def trunk(nc, x, attn_norm_g, w_in, conv_w, conv_b, b_igate, b_fgate, q_norm_g, k_norm_g,
          out_norm_g, w_out, mlp_norm_g, w_up, w_down, out):
    _, SEQ, D = x.shape
    DEPTH = w_in.shape[0]
    HD = q_norm_g.shape[1]
    NH = b_igate.shape[1]
    DH = NH * HD
    FF = w_up.shape[2]
    CW = conv_w.shape[1]
    TT = SEQ // P
    KT = D // P
    NPAIR = NH // 2
    HALF = 512
    SLOTS = 4
    GROUP = 2
    NG = FF // (GROUP * P)
    O_SB = 4 * DH + 2 * NH
    CH = NH * TT
    VW = HD + 1
    QSC = float(HD) ** -0.5
    SBLK = HALF // P
    assert SEQ == 2 * HALF and KT == 8 and TT == 8 and CH == 64 and HD == 64

    OUT_USES = KT // SLOTS
    STICK_SLOTS = 3
    uses_m = [NPAIR] * SLOTS
    uses_s = [NPAIR if s < STICK_SLOTS else 0 for s in range(SLOTS)]
    uses_layer = [uses_m[s] + uses_s[s] + OUT_USES + NG for s in range(SLOTS)]

    resid_d = nc.dram_tensor("resid_scratch", (SEQ, D), F32, kind="Internal").ap()
    rows_d = nc.dram_tensor("rows_scratch", (CH, P + 1), F32, kind="Internal").ap()
    xin_v = x[0].rearrange("(t p) f -> p t f", p=P)
    out_v = out[0].rearrange("(t p) f -> p t f", p=P)
    resid_v = resid_d.rearrange("(t p) f -> p t f", p=P)

    ctx = ExitStack()
    with ctx:
        def sb(stack, name, shape, dt=F32):
            return stack.enter_context(nc.sbuf_tensor(name, shape, dt))

        def sem(name):
            return ctx.enter_context(nc.semaphore(name))

        ident = sb(ctx, "ident", [P, P])
        ident_b = sb(ctx, "ident_b", [P, P], BF16)
        after_mask = sb(ctx, "after_mask", [P, P], BF16)
        tri_f = sb(ctx, "tri_f", [P, P])
        suffix = sb(ctx, "suffix", [P, P], F32R)
        minus_ones = sb(ctx, "minus_ones", [P, P])
        head_ones = sb(ctx, "head_ones", [P, P])
        eps_c = sb(ctx, "eps_c", [P, 2])
        small_rows = sb(ctx, "small_rows", [P, P])
        small_cols = sb(ctx, "small_cols", [P, P])
        gate_bias = sb(ctx, "gate_bias", [P, 2 * NH])
        a_col = sb(ctx, "a_col", [P, CH])
        floor_col = sb(ctx, "floor_col", [P, CH])
        act_t = sb(ctx, "act_t", [P, 2, KT, SEQ], F32R)
        resid = sb(ctx, "resid", [P, TT, D])
        raw = sb(ctx, "raw", [P, SLOTS, KT * P])
        spl = sb(ctx, "spl", [P, SLOTS, 2, KT * P], F32R)
        gain = sb(ctx, "gain", [P, D])
        turned = sb(ctx, "turned", [P, 2, D])
        ssq = sb(ctx, "ssq", [P, 2])
        rst = sb(ctx, "rst", [P, 2])
        banks = ctx.enter_context(nc.psum_tensor("banks", [P, 8, 512], F32))
        psum = [banks[:, i] for i in range(8)]

        with ExitStack() as s:
            wg_raw = sb(s, "wg_raw", [P, KT, P])
            wg = sb(s, "wg", [P, 2, KT, P], F32R)
            gt = sb(s, "gt", [2 * NH, SEQ])
            gsb = sb(s, "gsb", [P, TT, 2 * NH])
            glog = sb(s, "glog", [P, TT, NH])
            gabs = sb(s, "gabs", [P, TT, NH])
            gi = sb(s, "gi", [P, TT, NH])
            brow = sb(s, "brow", [CH, P])
            arow = sb(s, "arow", [CH, P])
            cmax = sb(s, "cmax", [CH, 2, P + 64])
            lastv = sb(s, "lastv", [1, 2, CH])
            mprev = sb(s, "mprev", [1, CH])
            mpcol = sb(s, "mpcol", [CH, 1])
            nrow = sb(s, "nrow", [CH, P + 1])
            frow = sb(s, "frow", [CH, P])
        with ExitStack() as s:
            pre = sb(s, "pre", [P, CW - 1 + SEQ])
            qm = sb(s, "qm", [P, SEQ])
            km = sb(s, "km", [P, SEQ])
            sig = sb(s, "sig", [P, SEQ])
            qs = sb(s, "qs", [P, TT, P])
            vm = sb(s, "vm", [P, TT, 2, VW])
            og = sb(s, "og", [P, TT, P])
            nm = sb(s, "nm", [P, TT, 2, P + 1])
            kw = sb(s, "kw", [P, TT, P])
            state = sb(s, "state", [P, TT - 1, 2 * VW])
            dec = sb(s, "dec", [P, TT, 2])
            dd = sb(s, "dd", [P, TT, 2])
            mss = sb(s, "mss", [P, 2 * TT])
        with ExitStack() as s:
            qkt = sb(s, "qkt", [P, 2, SEQ])
            vs = sb(s, "vs", [P, TT, P])
            sp_ = sb(s, "sp", [P, 2, 2, HALF])
            sph = sb(s, "sph", [P, 2, 2, 2, HALF], F32R)
            carry = sb(s, "carry", [P, 2, 2, HALF])
            prob = turned[:].rearrange("p i (j t) -> p i j t", j=2)
            sq = carry[:, 0]
            rs = carry[:, 1]
            vf = sp_[:, 1].rearrange("p j t -> p (j t)")
            ysq = sb(s, "ysq", [P, 2, SBLK * HD])
            yss = sb(s, "yss", [P, 2 * SBLK])
        with ExitStack() as s:
            wo_more = sb(s, "wo_more", [P, SLOTS, 2, KT * P], F32R)
            rtile = sb(s, "rtile", [P, 2, D])
            mlp_gain = sb(s, "mlp_gain", [P, D])
        with ExitStack() as s:
            hid = sb(s, "hid", [P, 2, 2, GROUP, SEQ], F32R)
            h1 = sb(s, "h1", [P, 2, HALF])
            h2 = sb(s, "h2", [P, 2, HALF])

        started = sem("started")
        const_done = sem("const_done")
        x_loaded = [sem(f"x_loaded{t}") for t in range(TT)]
        raw_loaded = [sem(f"raw_loaded{s}") for s in range(SLOTS)]
        hi_done = [sem(f"hi_done{s}") for s in range(SLOTS)]
        lo_done = [sem(f"lo_done{s}") for s in range(SLOTS)]
        phase_done = {e: sem(f"phase_done_{e}") for e in ("pe", "act", "dve", "pool", "sp")}
        small_loaded = sem("small_loaded")
        gain_loaded = sem("gain_loaded")
        resid_stored = sem("resid_stored")
        out_stored = sem("out_stored")
        rows_stored = sem("rows_stored")
        nm_loaded = sem("nm_loaded")
        wg_loaded = sem("wg_loaded")
        rt_loaded = [sem(f"rt_loaded{i}") for i in range(2)]
        steps = {e.engine: sem(f"steps_{i}") for i, e in enumerate((nc.tensor, nc.scalar, nc.vector, nc.gpsimd, nc.sync))}

        from_one = [*lo_done, *phase_done.values()]

        class Flag:

            def __init__(self, name, per_layer, start=1):
                self.sem, self.per_layer, self.start = sem(name), per_layer, start
                from_one.extend([self.sem] * start)

            def at(self, l, n):
                return l * self.per_layer + n + self.start

        NT = 3 * TT
        NU = SBLK + 2 * SBLK
        NC = NU - 2
        tile_ready = Flag("tile_ready", NT)
        scale_ready = Flag("scale_ready", 2 * TT)
        tile_turned = Flag("tile_turned", 2 * NT)
        turned_hi = Flag("turned_hi", 2 * NT)
        turned_lo = Flag("turned_lo", 2 * NT)
        out_psum = Flag("out_psum", TT)
        wo_used = Flag("wo_used", 1)
        resid_new = Flag("resid_new", TT)
        small_pe = Flag("small_pe", 1)
        wg_hi = Flag("wg_hi", 1)
        wg_lo = Flag("wg_lo", 1)
        gate_pe = Flag("gate_pe", 7)
        gate_dve = Flag("gate_dve", 7)
        gate_act = Flag("gate_act", 2)
        m_gated = Flag("m_gated", NPAIR)
        q_proj = Flag("q_proj", 2 * 2 * NPAIR)
        m_proj = Flag("m_proj", 6 * NPAIR)
        m_evac = Flag("m_evac", 8 * NPAIR)
        m_conv = Flag("m_conv", 2 * NPAIR)
        m_abs = Flag("m_abs", 3 * NPAIR)
        m_ln = Flag("m_ln", 3 * NPAIR)
        m_log = Flag("m_log", 3 * NPAIR)
        m_sig = Flag("m_sig", 3 * NPAIR)
        m_qk = Flag("m_qk", 2 * NPAIR)
        m_args = Flag("m_args", NPAIR)
        m_masked = Flag("m_masked", NPAIR)
        m_exp = Flag("m_exp", 2 * NPAIR)
        m_kt = Flag("m_kt", 2 * NPAIR)
        m_kw = Flag("m_kw", NPAIR)
        m_qs = Flag("m_qs", NPAIR)
        m_s = Flag("m_s", 2 * NPAIR)
        m_w = Flag("m_w", 2 * NPAIR)
        m_u = Flag("m_u", 3 * NPAIR)
        m_state = Flag("m_state", (TT - 1) * NPAIR)
        m_num = Flag("m_num", 3 * NPAIR)
        m_y = Flag("m_y", 3 * NPAIR)
        m_ysq = Flag("m_ysq", NPAIR)
        m_yms = Flag("m_yms", NPAIR)
        m_yrs = Flag("m_yrs", NPAIR)
        s_proj = Flag("s_proj", 4 * NPAIR)
        s_sq = Flag("s_sq", 4 * NPAIR)
        s_sum = Flag("s_sum", 4 * NPAIR)
        s_rs = Flag("s_rs", 4 * NPAIR)
        s_qk = Flag("s_qk", 4 * NPAIR)
        s_vf = Flag("s_vf", 2 * NPAIR)
        s_vt = Flag("s_vt", 2 * NPAIR)
        s_v = Flag("s_v", 2 * NPAIR)
        u_z = Flag("u_z", NU * NPAIR)
        u_abs = Flag("u_abs", 2 * NU * NPAIR)
        u_ln = Flag("u_ln", 2 * NU * NPAIR)
        u_sp = Flag("u_sp", 2 * NU * NPAIR)
        u_hi = Flag("u_hi", 2 * NU * NPAIR)
        u_lo = Flag("u_lo", 2 * NU * NPAIR)
        u_carry = Flag("u_carry", NC * NPAIR)
        u_e = Flag("u_e", 2 * NU * NPAIR)
        u_prob = Flag("u_prob", 2 * NU * NPAIR)
        u_av = Flag("u_av", NU * NPAIR)
        y_out = Flag("y_out", 2 * NPAIR)
        y_sq = Flag("y_sq", 2 * NPAIR)
        y_ms = Flag("y_ms", 2 * NPAIR)
        y_rs = Flag("y_rs", 2 * NPAIR)
        UPS = 2 * GROUP
        up_psum = Flag("up_psum", UPS * NG)
        relu = Flag("relu", UPS * NG)
        squared = Flag("squared", UPS * NG)
        hid_hi_done = Flag("hid_hi_done", UPS * NG)
        hid_lo_done = Flag("hid_lo_done", UPS * NG)
        down_psum = Flag("down_psum", 2 * TT * NG)
        down_add = Flag("down_add", 2 * TT * NG, 2 * TT + 1)

        PHASES = 6

        def part(eng):
            eng.sem_inc(steps[eng.engine], 1)

        def phase_end(eng, name):
            part(eng)
            eng.drain().then_inc(phase_done[name], 1)

        def phase_start(eng, l, n, *others):
            for o in others:
                eng.wait_ge(phase_done[o], l * PHASES + n + 1)
            part(eng)

        def raw_k(s):
            return raw[:, s].rearrange("p (k n) -> p k n", k=KT)

        def spl_k(s, h):
            return spl[:, s, h].rearrange("p (k n) -> p k n", k=KT)

        def use(l, s, n):
            return l * uses_layer[s] + n

        use_m = [0] * SLOTS
        use_s = uses_m
        use_out = [uses_m[s] + uses_s[s] for s in range(SLOTS)]
        use_mlp = [use_out[s] + OUT_USES for s in range(SLOTS)]

        OUT_SEQ = [("y", 0), ("y", 1)]
        for t in range(TT):
            OUT_SEQ += [("n", t - 1)] if t >= 1 else []
            OUT_SEQ += [("y", t + 2)] if t + 2 < TT else []
        OUT_SEQ.append(("n", TT - 1))

        def place(kind, t):
            return TT + OUT_SEQ.index((kind, t))

        NUM_BANKS = ((0, 3, 4), (3, 6, 5), (6, 8, 6))
        UPD_BANKS = ((0, 3, 6), (3, 6, 7), (6, 7, 2))
        UPD_BANK = {c: (a, bank) for a, e, bank in UPD_BANKS for c in range(a, e)}

        units = [(b, k) for b in range(2) for k in reversed(range(SBLK * (b + 1)))]
        assert len(units) == NU and NU % 3 == 0
        E_BANKS = (0, 2, 6)

        def span(n):
            b, k = units[n]
            diag = k >= SBLK * b
            c0 = (k - SBLK * b) * P if diag else 0
            return c0, c0 + P if diag else 0, diag

        def top(n):
            b, k = units[n]
            return k == SBLK * (b + 1) - 1

        def carries(n):
            return sum(1 for _, k in units[:max(n, 0)] if k)

        def logits(n):
            e = E_BANKS[n % 3]
            return banks[:, e:e + 2, span(n)[0]:HALF]

        def y_store(b, hp):
            return resid[:, b * SBLK:(b + 1) * SBLK, bass.ds(DH + hp * P, P)].rearrange("p t (j d) -> p j t d", j=2)

        PASSES = ((0, 0), (0, 1), (1, 0))
        ROW_W, ROW_B, ROW_Q, ROW_K = 0, CW * KT, (CW + 1) * KT, (CW + 1) * KT + 1
        N_SMALL = ROW_K + 1
        SMALL_DMAS = 8

        block = ctx.enter_context(nc.Block())

        @block.sync
        def _(sp):
            def load_x(tiles):
                for t in tiles:
                    sp.dma_start(resid[:, t], xin_v[:, t]).then_inc(x_loaded[t], 16)

            load_x(range(3))
            sp.wait_ge(started, 1)
            load_x(range(3, TT))

            def load(s, l, n, dst, src):
                sp.wait_ge(lo_done[s], use(l, s, n) + 1)
                part(sp)
                sp.dma_start(dst, src).then_inc(raw_loaded[s], 16)

            with sp.Fori(0, DEPTH) as l:
                w_in_v = w_in[l].rearrange("(k p) n -> p k n", p=P)
                w_up_v = w_up[l].rearrange("(k p) n -> p k n", p=P)

                sp.wait_ge(small_pe.sem, small_pe.at(l, 0))
                sp.wait_ge(gate_dve.sem, gate_dve.at(l, 0))
                part(sp)
                sp.dma_start(small_rows[ROW_W:ROW_B, :], conv_w[l].rearrange("j (t p) -> (j t) p", p=P)).then_inc(small_loaded, 16)
                sp.dma_start(small_rows[ROW_B:ROW_Q, :], conv_b[l].rearrange("(t p) -> t p", p=P)).then_inc(small_loaded, 16)
                for r, g in ((ROW_Q, q_norm_g), (ROW_K, k_norm_g)):
                    for j in range(2):
                        sp.dma_start(small_rows[r:r + 1, j * HD:(j + 1) * HD], g[l].unsqueeze(0)).then_inc(small_loaded, 16)
                sp.dma_start(gate_bias[:, 0:NH], b_igate[l].unsqueeze(0).to_broadcast([P, NH])).then_inc(small_loaded, 16)
                sp.dma_start(gate_bias[:, NH:2 * NH], b_fgate[l].unsqueeze(0).to_broadcast([P, NH])).then_inc(small_loaded, 16)

                with sp.Fori(0, NPAIR) as hp:
                    for s in range(SLOTS):
                        load(s, l, use_m[s] + hp, raw_k(s), w_in_v[:, :, bass.ds(s * DH + hp * P, P)])
                load(3, l, use_out[3], raw[:, 3], w_out[l, 3 * P:4 * P, :])
                with sp.Fori(0, NPAIR) as hp:
                    for s in range(STICK_SLOTS):
                        load(s, l, use_s[s] + hp, raw_k(s), w_in_v[:, :, bass.ds(O_SB + s * DH + hp * P, P)])
                for s in range(STICK_SLOTS):
                    load(s, l, use_out[s], raw[:, s], w_out[l, s * P:(s + 1) * P, :])
                for s in range(SLOTS):
                    load(s, l, use_out[s] + 1, raw[:, s], w_out[l, (SLOTS + s) * P:(SLOTS + s + 1) * P, :])
                phase_start(sp, l, 4, "pe", "act", "dve", "pool")
                sp.wait_ge(resid_stored, l * 16 + 16)
                for t in range(TT):
                    if t >= 2:
                        sp.wait_ge(resid_new.sem, resid_new.at(l, t - 1))
                    sp.dma_start(rtile[:, t % 2], resid_v[:, t]).then_inc(rt_loaded[t % 2], 16)
                with sp.Fori(0, NG) as g:
                    for s in range(GROUP):
                        load(s, l, use_mlp[s] + g, raw_k(s), w_up_v[:, :, bass.ds((g * GROUP + s) * P, P)])
                    for s in range(GROUP):
                        load(GROUP + s, l, use_mlp[GROUP + s] + g, raw[:, GROUP + s],
                             w_down[l, bass.ds((g * GROUP + s) * P, P), :])
            phase_start(sp, DEPTH - 1, PHASES, "dve")
            sp.dma_start(out_v, resid[:]).then_inc(out_stored, 16)
            sp.wait_ge(out_stored, 16)

        @block.tensor
        def _(pe):
            def turn(l, n):
                pe.wait_ge(tile_ready.sem, tile_ready.at(l, n + 1))
                for b in range(2):
                    i = 2 * n + b
                    if i >= 4:
                        pe.wait_ge(turned_lo.sem, turned_lo.at(l, i - 3))
                    for k in range(4):
                        ins = pe.transpose(psum[i % 4][:, k * P:(k + 1) * P],
                                           turned[:, n % 2, (4 * b + k) * P:(4 * b + k + 1) * P], ident[:])
                    ins.then_inc(tile_turned.sem, 1)

            def project(s, h, bank):
                for k in range(KT):
                    for i, (a, b) in enumerate(PASSES):
                        ins = pe.matmul(psum[bank][:], spl_k(s, a)[:, k, :], act_t[:, b, k, h * HALF:(h + 1) * HALF],
                                        start=(k == 0 and i == 0), stop=(k == KT - 1 and i == 2))
                return ins

            def project_half(l, s, n, h, bank):
                pe.wait_ge(lo_done[s], use(l, s, n) + 2)
                return project(s, h, bank)

            def project_t(l, n):
                for s in (2, 3):
                    pe.wait_ge(lo_done[s], use(l, s, n) + 2)
                for t in range(TT):
                    dst = psum[4 + t // 2][:, (t % 2) * 2 * P:(t % 2 + 1) * 2 * P].rearrange("p (s n) -> p s n", s=2)
                    for k in range(KT):
                        for i, (a, b) in enumerate(PASSES):
                            ins = pe.matmul(dst, act_t[:, a, k, t * P:(t + 1) * P], spl[:, 2:4, b, k * P:(k + 1) * P],
                                            start=(k == 0 and i == 0), stop=(k == KT - 1 and i == 2))
                    if t % 2:
                        ins.then_inc(m_proj.sem, 1)

            def up_half(l, g, i, first=False):
                s, h = i // 2, i % 2
                if h == 0:
                    pe.wait_ge(lo_done[s], use(l, s, use_mlp[s] + g) + 2)
                if not first:
                    pe.wait_ge(squared.sem, squared.at(l, UPS * g + i + 1 - UPS))
                project(s, h, i).then_inc(up_psum.sem, 1)

            def up(l, g):
                for i in range(UPS):
                    up_half(l, g, i)

            def down(l, g, buf, first=False, base=GROUP):
                for s in range(GROUP):
                    pe.wait_ge(lo_done[GROUP + s], use(l, GROUP + s, use_mlp[GROUP + s] + g) + 2)
                for i in range(2 * TT):
                    t, h = i // 2, i % 2
                    if i == 0:
                        pe.wait_ge(hid_lo_done.sem, hid_lo_done.at(l, UPS * g + UPS))
                    if not (first and i < 4):
                        pe.wait_ge(down_add.sem, down_add.at(l, 2 * TT * g + i - 3))
                    for k in range(GROUP):
                        for q, (a, b) in enumerate(PASSES):
                            ins = pe.matmul(psum[4 + i % 4][:], hid[:, buf, a, k, t * P:(t + 1) * P],
                                            spl[:, base + k, b, h * HALF:(h + 1) * HALF],
                                            start=(k == 0 and q == 0), stop=(k == GROUP - 1 and q == 2))
                    ins.then_inc(down_psum.sem, 1)

            pe.wait_ge(const_done, 1)
            with pe.Fori(0, DEPTH) as l:
                phase_start(pe, l, 0, "act", "dve")
                for t in range(TT):
                    turn(l, t)
                pe.wait_ge(small_loaded, (l + 1) * (16 * SMALL_DMAS))
                part(pe)
                pe.transpose(psum[7][:, 0:N_SMALL], small_rows[0:N_SMALL, :], ident[0:N_SMALL, 0:N_SMALL]).then_inc(small_pe.sem, 1)
                phase_end(pe, "pe")
                phase_start(pe, l, 1, "act", "dve")
                pe.wait_ge(wg_lo.sem, wg_lo.at(l, 1))
                for h in range(2):
                    for k in range(KT):
                        for i, (a, b) in enumerate(PASSES):
                            ins = pe.matmul(psum[6 + h][:], wg[:, a, k, :], act_t[:, b, k, h * HALF:(h + 1) * HALF],
                                            start=(k == 0 and i == 0), stop=(k == KT - 1 and i == 2))
                    ins.then_inc(gate_pe.sem, 1)
                pe.wait_ge(gate_dve.sem, gate_dve.at(l, 2))
                part(pe)
                for t in range(TT):
                    ins = pe.transpose(psum[4][:, t * 2 * NH:(t + 1) * 2 * NH], gt[:, t * P:(t + 1) * P], ident[0:2 * NH, 0:2 * NH])
                ins.then_inc(gate_pe.sem, 1)
                project_half(l, 0, use_m[0], 0, 0).then_inc(q_proj.sem, 1)
                pe.wait_ge(gate_dve.sem, gate_dve.at(l, 4))
                pe.matmul(psum[5][0:CH, 0:P], glog[:].rearrange("p t h -> p (t h)"), tri_f[:], start=True, stop=True)
                pe.matmul(psum[6][0:CH, 0:P], gi[:].rearrange("p t h -> p (t h)"), ident[:],
                          start=True, stop=True).then_inc(gate_pe.sem, 1)
                project_half(l, 0, use_m[0], 1, 1).then_inc(q_proj.sem, 1)
                pe.wait_ge(gate_dve.sem, gate_dve.at(l, 5))
                part(pe)
                pe.matmul(psum[7][0:1, 0:CH], brow[:, P - 1:P], ident[0:CH, 0:CH], start=True, stop=True)
                pe.matmul(psum[7][0:1, CH:2 * CH], cmax[:, 1, 64 + P - 1:64 + P], ident[0:CH, 0:CH],
                          start=True, stop=True).then_inc(gate_pe.sem, 1)
                pe.wait_ge(gate_dve.sem, gate_dve.at(l, 6))
                part(pe)
                pe.matmul(psum[4][0:CH, 0:1], mprev[:, :], ident[0:1, 0:1], start=True, stop=True).then_inc(gate_pe.sem, 1)
                pe.wait_ge(gate_dve.sem, gate_dve.at(l, 7))
                part(pe)
                pe.transpose(psum[5][:, 0:CH], arow[:], ident[0:CH, 0:CH])
                pe.transpose(psum[5][:, CH:2 * CH], frow[:], ident[0:CH, 0:CH]).then_inc(gate_pe.sem, 1)
                phase_end(pe, "pe")
                with pe.Fori(0, NPAIR) as hp:
                    for h in range(2):
                        project_half(l, 1, use_m[1] + hp, h, 2 + h).then_inc(m_proj.sem, 1)
                    pe.wait_ge(m_y.sem, m_y.at(l, 3 * hp))
                    phase_start(pe, l, 2, "act", "dve")
                    project_t(l, use_m[2] + hp)
                    pe.wait_ge(m_qk.sem, m_qk.at(l, 2 * hp + 2))

                    def scores(b):
                        for c in range(4 * b, 4 * b + 4):
                            for j in range(2):
                                cc, hs = slice(c * P, (c + 1) * P), slice(j * HD, (j + 1) * HD)
                                ins = pe.matmul(psum[2 + j][:, (c % 4) * P:(c % 4 + 1) * P], km[hs, cc], qm[hs, cc],
                                                start=True, stop=True)
                        ins.then_inc(m_s.sem, 1)

                    for b in range(2):
                        for c in range(4):
                            ins = pe.transpose(psum[b][:, c * P:(c + 1) * P], km[:, (4 * b + c) * P:(4 * b + c + 1) * P], ident[:])
                        ins.then_inc(m_kt.sem, 1)
                    scores(0)
                    pe.wait_ge(m_kw.sem, m_kw.at(l, hp + 1))
                    project_half(l, 0, use_m[0] + hp + 1, 0, 0).then_inc(q_proj.sem, 1)
                    pe.wait_ge(m_evac.sem, m_evac.at(l, 8 * hp + 8))

                    def updates(a, e, bank):
                        for c in range(a, e):
                            o = (c - a) * 2 * VW
                            ins = pe.matmul(psum[bank][:, o:o + 2 * VW], kw[:, c], vm[:, c].rearrange("p j v -> p (j v)"),
                                            start=True, stop=True)
                        ins.then_inc(m_u.sem, 1)

                    updates(*UPD_BANKS[0])
                    updates(*UPD_BANKS[1])
                    pe.wait_ge(m_w.sem, m_w.at(l, 2 * hp + 1))
                    scores(1)
                    project_half(l, 0, use_m[0] + hp + 1, 1, 1).then_inc(q_proj.sem, 1)
                    pe.wait_ge(m_w.sem, m_w.at(l, 2 * hp + 2))
                    updates(*UPD_BANKS[2])
                    pe.wait_ge(m_qs.sem, m_qs.at(l, hp + 1))
                    for a, e, bank in NUM_BANKS:
                        for c in range(a, e):
                            o = (c - a) * 2 * VW
                            if c:
                                pe.wait_ge(m_state.sem, m_state.at(l, (TT - 1) * hp + c))
                                pe.matmul(psum[bank][:, o:o + 2 * VW], qs[:, c], state[:, c - 1], start=True, stop=False,
                                          skip_group_check=True)
                            for j in range(2):
                                ins = pe.matmul(psum[bank][:, o + j * VW:o + (j + 1) * VW], nm[:, c, j, 0:P], vm[:, c, j],
                                                start=(c == 0), stop=(j == 1 or c == 0), skip_group_check=True)
                        ins.then_inc(m_num.sem, 1)
                phase_end(pe, "pe")
                def stick_pair(hp, more):
                    def norm_sum(n):
                        pe.wait_ge(s_sq.sem, s_sq.at(l, 4 * hp + n + 1))
                        pe.wait_ge(s_rs.sem, s_rs.at(l, 4 * hp + max(n - 1, 0)))
                        pe.matmul(psum[6 + n % 2][:], head_ones[:], sq[:, n % 2], start=True, stop=True).then_inc(s_sum.sem, 1)

                    pe.wait_ge(u_prob.sem, u_prob.at(l, 2 * NU * hp))
                    project_half(l, 1, use_s[1] + hp, 0, 2).then_inc(s_proj.sem, 1)
                    pe.wait_ge(m_y.sem, m_y.at(l, 3 * NPAIR))
                    norm_sum(0)
                    project_half(l, 1, use_s[1] + hp, 1, 3).then_inc(s_proj.sem, 1)
                    norm_sum(1)
                    norm_sum(2)
                    pe.wait_ge(y_out.sem, y_out.at(l, 2 * hp))
                    project_half(l, 2, use_s[2] + hp, 0, 4).then_inc(s_proj.sem, 1)
                    norm_sum(3)

                    def scores(n):
                        b, k = units[n]
                        c0, c1, diag = span(n)
                        if n < 2:
                            pe.wait_ge(s_qk.sem, s_qk.at(l, 4 * hp + 3 + n))
                        if n == 2:
                            pe.wait_ge(s_v.sem, s_v.at(l, 2 * hp + 2))
                        pe.wait_ge(u_prob.sem, u_prob.at(l, 2 * (NU * hp + max(n - 2, 0))))
                        e = E_BANKS[n % 3]
                        for j in range(2):
                            hs = slice(j * HD, (j + 1) * HD)
                            ins = pe.matmul(psum[e + j][:, c0:HALF], qkt[hs, 1, k * P:(k + 1) * P],
                                            qkt[hs, 0, b * HALF + c0:(b + 1) * HALF],
                                            start=True, stop=False, skip_group_check=True)
                        if diag:
                            for j in range(2):
                                ins = pe.matmul(psum[e + j][:, c0:c1], ident_b[:], after_mask[:], start=False, stop=False,
                                                skip_group_check=True)
                        ins.then_inc(u_z.sem, 1)

                    def exponents(n):
                        c0, c1, diag = span(n)
                        e = E_BANKS[n % 3]
                        for j in range(2):
                            pe.wait_ge(u_lo.sem, u_lo.at(l, 2 * (NU * hp + n) + j + 1))
                            for h in range(2):
                                ins = pe.matmul(psum[e + j][:, c0:HALF], suffix[:], sph[:, n % 2, h, j, c0:HALF], start=False,
                                                stop=(h == 1 and c1 == HALF), skip_group_check=True)
                            if c1 < HALF:
                                pe.wait_ge(u_carry.sem, u_carry.at(l, NC * hp + carries(n)))
                                ins = pe.matmul(psum[e + j][:, c1:HALF], minus_ones[:], carry[:, n % 2, j, c1:HALF], start=False,
                                                stop=True, skip_group_check=True)
                            ins.then_inc(u_e.sem, 1)

                    def values(n):
                        b, k = units[n]
                        c0, _, _ = span(n)
                        if top(n) and b == 1:
                            pe.wait_ge(y_out.sem, y_out.at(l, 2 * hp + 1))
                        for j in range(2):
                            pe.wait_ge(u_prob.sem, u_prob.at(l, 2 * (NU * hp + n) + j + 1))
                            for q in range(c0 // P, SBLK):
                                ins = pe.matmul(psum[4 + j][:, q * HD:(q + 1) * HD], prob[:, n % 2, j, q * P:(q + 1) * P],
                                                vs[:, k, j * HD:(j + 1) * HD], start=top(n), stop=(k == 0), skip_group_check=True)
                        ins.then_inc(u_av.sem, 1)

                    for n in range(NU + 3):
                        if more and n > NU:
                            pe.wait_ge(u_prob.sem, u_prob.at(l, 2 * (NU * hp + NU - 2)))
                            h = n - NU - 1
                            project_half(l, 0, use_s[0] + hp + 1, h, h).then_inc(q_proj.sem, 1)
                        if n < NU:
                            scores(n)
                        if 0 <= n - 2 < NU:
                            exponents(n - 2)
                        if n < 2:
                            pe.wait_ge(s_vf.sem, s_vf.at(l, 2 * hp + n + 1))
                            pe.wait_ge(s_v.sem, s_v.at(l, 2 * hp + n))
                            for q in range(4):
                                ins = pe.transpose(psum[6][:, q * P:(q + 1) * P], vf[:, (4 * n + q) * P:(4 * n + q + 1) * P], ident[:])
                            ins.then_inc(s_vt.sem, 1)
                        if n == 0:
                            pe.wait_ge(s_rs.sem, s_rs.at(l, 4 * hp + 4))
                            project_half(l, 2, use_s[2] + hp, 1, 7).then_inc(s_proj.sem, 1)
                        if 0 <= n - 3 < NU:
                            values(n - 3)

                with pe.Fori(0, NPAIR - 1) as hp:
                    stick_pair(hp, True)
                stick_pair(NPAIR - 1, False)
                phase_end(pe, "pe")
                phase_start(pe, l, 4, "act", "dve")
                for t in range(2):
                    turn(l, place("y", t))
                for t in range(TT):
                    pe.wait_ge(turned_lo.sem, turned_lo.at(l, 2 * place("y", t) + 2))
                    if t >= 2:
                        pe.wait_ge(resid_new.sem, resid_new.at(l, t - 1))
                    for k in range(KT):
                        if t == 0:
                            s = k % SLOTS
                            pe.wait_ge(lo_done[s], use(l, s, use_out[s]) + (2 if k < SLOTS else 3))
                        if t >= 1 and k == KT // 2:
                            turn(l, place("n", t - 1))
                        w = spl if k < SLOTS else wo_more
                        for h in range(2):
                            for i, (a, b) in enumerate(PASSES):
                                ins = pe.matmul(psum[4 + 2 * (t % 2) + h][:], act_t[:, a, k, t * P:(t + 1) * P],
                                                w[:, k % SLOTS, b, h * HALF:(h + 1) * HALF],
                                                start=(k == 0 and i == 0), stop=(k == KT - 1 and i == 2))
                        if t == TT - 1 and k == GROUP - 1:
                            ins.then_inc(wo_used.sem, 1)
                    ins.then_inc(out_psum.sem, 1)
                    if t + 2 < TT:
                        turn(l, place("y", t + 2))
                pe.wait_ge(turned_lo.sem, turned_lo.at(l, 2 * place("n", TT - 2) + 2))
                up_half(l, 0, 0, first=True)
                turn(l, place("n", TT - 1))
                phase_end(pe, "pe")
                pe.wait_ge(turned_lo.sem, turned_lo.at(l, 2 * NT))
                for i in range(1, UPS):
                    up_half(l, 0, i, first=True)
                up(l, 1)
                down(l, 0, 0, first=True)
                with pe.Fori(0, NG // 2 - 1) as m:
                    up(l, 2 * m + 2)
                    down(l, 2 * m + 1, 1)
                    up(l, 2 * m + 3)
                    down(l, 2 * m + 2, 0)
                down(l, NG - 1, 1, base=0)
                phase_end(pe, "pe")

        @block.scalar
        def _(act):
            def hi(s, l, n, dst):
                act.wait_ge(raw_loaded[s], (use(l, s, n) + 1) * 16)
                act.activation(dst, raw[:, s], ACT.Copy).then_inc(hi_done[s], 1)

            def turn_hi(l, n, t):
                for b in range(2):
                    act.wait_ge(tile_turned.sem, tile_turned.at(l, 2 * n + b + 1))
                    act.activation(act_t[:, 0, 4 * b:4 * b + 4, t * P:(t + 1) * P],
                                   psum[(2 * n + b) % 4][:].rearrange("p (k n) -> p k n", k=4), ACT.Copy).then_inc(turned_hi.sem, 1)

            def tile_scale(l, n, t):
                if n >= 2:
                    act.wait_ge(tile_turned.sem, tile_turned.at(l, 2 * (n - 1)))
                act.activation(turned[:, n % 2], resid[:, t], ACT.Square, accum_out=ssq[:, n % 2:n % 2 + 1])
                act.drain()
                act.activation(ssq[:, n % 2:n % 2 + 1], ssq[:, n % 2:n % 2 + 1], ACT.Ln, bias=eps_c[:, 0:1], scale=1.0 / D)
                act.drain()
                act.activation(rst[:, n % 2:n % 2 + 1], ssq[:, n % 2:n % 2 + 1], ACT.Exp, scale=-0.5).then_inc(scale_ready.sem, 1)

            act.preload_act_table_set("natural_log_exp_and_others")
            act.wait_ge(started, 1)
            with act.Fori(0, DEPTH) as l:
                act.dma_start(gain[:], attn_norm_g[l].unsqueeze(0).to_broadcast([P, D])).then_inc(gain_loaded, 16)

                def scale_in(t):
                    act.wait_ge(x_loaded[t], 16)
                    act.wait_ge(down_add.sem, down_add.at(l, 2 * (t + 1) - 2 * TT))
                    tile_scale(l, t, t)

                for t in range(2):
                    scale_in(t)
                phase_start(act, l, 0, "pe", "dve")
                act.dma_start(wg_raw[:], w_in[l].rearrange("(k p) n -> p k n", p=P)[:, :, 4 * DH:4 * DH + P]).then_inc(wg_loaded, 16)
                for t in range(TT + 1):
                    if 2 <= t < TT:
                        scale_in(t)
                    if t >= 1:
                        turn_hi(l, t - 1, t - 1)
                    if 2 <= t < 4:
                        hi(t - 2, l, use_m[t - 2], spl[:, t - 2, 0])
                    if t == 4:
                        act.wait_ge(wg_loaded, 16 * (l + 1))
                        act.activation(wg[:, 0], wg_raw[:], ACT.Copy).then_inc(wg_hi.sem, 1)
                act.dma_start(resid_v, resid[:]).then_inc(resid_stored, 16)
                phase_end(act, "act")
                phase_start(act, l, 1, "dve")
                act.dma_start(gain[:], out_norm_g[l].unsqueeze(0).to_broadcast([P, D])).then_inc(gain_loaded, 16)
                act.wait_ge(gate_dve.sem, gate_dve.at(l, 3))
                act.activation(gabs[:], gabs[:], ACT.Exp, scale=-1.0)
                act.drain()
                act.activation(gabs[:], gabs[:], ACT.Ln, bias=1.0).then_inc(gate_act.sem, 1)
                for s in range(2, SLOTS):
                    hi(s, l, use_m[s], spl[:, s, 0])
                act.wait_ge(gate_dve.sem, gate_dve.at(l, 7))
                act.dma_start(rows_d, nrow[:]).then_inc(rows_stored, 16)
                act.wait_ge(gate_pe.sem, gate_pe.at(l, 7))
                act.activation(floor_col[:], psum[5][:, CH:2 * CH], ACT.Exp).then_inc(gate_act.sem, 1)
                act.wait_ge(rows_stored, (l + 1) * 16)
                phase_end(act, "act")
                phase_start(act, l, 2, "pe", "dve")
                with act.Fori(0, NPAIR) as hp:
                    act.wait_ge(m_num.sem, m_num.at(l, 3 * hp))
                    act.dma_start(nm[:], rows_d.rearrange("(c h) t -> c h t", c=TT)[:, bass.ds(2 * hp, 2), :].unsqueeze(0)
                                  .to_broadcast([P, TT, 2, P + 1])).then_inc(nm_loaded, 16)

                    def log_part(w):
                        act.wait_ge(m_abs.sem, m_abs.at(l, 3 * hp + w + 1))
                        act.activation(sig[:], sig[:], ACT.Exp, scale=-1.0)
                        act.drain()
                        act.activation(sig[:], sig[:], ACT.Ln, bias=1.0).then_inc(m_ln.sem, 1)

                    def sigmoid(w, buf):
                        act.wait_ge(m_log.sem, m_log.at(l, 3 * hp + w + 1))
                        act.activation(buf[:], buf[:], ACT.Exp).then_inc(m_sig.sem, 1)

                    for h in range(2):
                        act.wait_ge(q_proj.sem, q_proj.at(l, 2 * hp + h + 1))
                        if h == 0:
                            act.wait_ge(m_yms.sem, m_yms.at(l, hp))
                        act.activation(pre[:, CW - 1 + h * HALF:CW - 1 + (h + 1) * HALF], psum[h][:], ACT.Copy).then_inc(m_evac.sem, 1)
                    log_part(0)
                    act.wait_ge(m_args.sem, m_args.at(l, hp + 1))
                    act.activation(qs[:], qs[:], ACT.Exp)
                    act.activation(dec[:], dec[:], ACT.Exp).then_inc(m_exp.sem, 1)
                    sigmoid(0, sig)
                    act.wait_ge(m_conv.sem, m_conv.at(l, 2 * hp + 1))
                    for h in range(2):
                        act.wait_ge(m_proj.sem, m_proj.at(l, 6 * hp + h + 1))
                        act.activation(pre[:, CW - 1 + h * HALF:CW - 1 + (h + 1) * HALF], psum[2 + h][:], ACT.Copy).then_inc(m_evac.sem, 1)
                    act.wait_ge(m_masked.sem, m_masked.at(l, hp + 1))
                    act.activation(nm[:, :, :, 0:P], nm[:, :, :, 0:P], ACT.Exp).then_inc(m_exp.sem, 1)
                    for s in range(2):
                        hi(s, l, use_m[s] + hp + 1, spl[:, s, 0])
                    log_part(1)
                    sigmoid(1, sig)
                    act.wait_ge(m_gated.sem, m_gated.at(l, hp))
                    for b in range(4):
                        act.wait_ge(m_proj.sem, m_proj.at(l, 6 * hp + 3 + b))
                        src = psum[4 + b][:].rearrange("p (t s n) -> p t s n", t=2, s=2)
                        for t in range(2):
                            act.activation(vm[:, 2 * b + t, :, 0:HD], src[:, t, 0].rearrange("p (j d) -> p j d", j=2), ACT.Copy)
                        act.activation(og[:, 2 * b:2 * b + 2], src[:, :, 1], ACT.Copy).then_inc(m_evac.sem, 1)
                    for s in range(2, SLOTS):
                        hi(s, l, use_m[s] + hp + 1, spl[:, s, 0])
                    log_part(2)
                    sigmoid(2, og)
                    act.wait_ge(m_y.sem, m_y.at(l, 3 * (hp + 1)))
                    act.activation(pre[:, CW - 1:].rearrange("p (t n) -> p t n", t=TT), resid[:, :, bass.ds(hp * P, P)],
                                   ACT.Square).then_inc(m_ysq.sem, 1)
                    act.wait_ge(m_yms.sem, m_yms.at(l, hp + 1))
                    act.activation(mss[:], mss[:], ACT.Ln, bias=eps_c[:, 0:1], scale=1.0 / HD)
                    act.drain()
                    act.activation(mss[:], mss[:], ACT.Exp, scale=-0.5).then_inc(m_yrs.sem, 1)
                phase_end(act, "act")
                phase_start(act, l, 3, "pe", "dve", "pool")
                with act.Fori(0, NPAIR) as hp:
                    def square_in(n):
                        if n < 2:
                            act.wait_ge(q_proj.sem, q_proj.at(l, 2 * NPAIR + 2 * hp + n + 1))
                        else:
                            act.wait_ge(s_proj.sem, s_proj.at(l, 4 * hp + n - 1))
                        act.wait_ge(s_sum.sem, s_sum.at(l, 4 * hp + max(n - 1, 0)))
                        act.activation(sq[:, n % 2], psum[n][:], ACT.Square).then_inc(s_sq.sem, 1)

                    def values_out(h, bank):
                        act.wait_ge(s_proj.sem, s_proj.at(l, 4 * hp + 3 + h))
                        act.activation(vf[:, h * HALF:(h + 1) * HALF], psum[bank][:], ACT.Copy).then_inc(s_vf.sem, 1)

                    square_in(0)
                    for n in range(4):
                        if n < 3:
                            square_in(n + 1)
                        if n == 3:
                            values_out(0, 4)
                        act.wait_ge(s_sum.sem, s_sum.at(l, 4 * hp + n + 1))
                        act.wait_ge(s_qk.sem, s_qk.at(l, 4 * hp + max(n - 1, 0)))
                        is_q = n < 2
                        act.activation(rs[:, n % 2], psum[6 + n % 2][:], ACT.Ln, scale=1.0 if is_q else 1.0 / HD,
                                       bias=eps_c[:, 1:2] if is_q else eps_c[:, 0:1])
                        act.drain()
                        act.activation(rs[:, n % 2], rs[:, n % 2], ACT.Exp, scale=-0.5).then_inc(s_rs.sem, 1)

                    def values_turned(h):
                        act.wait_ge(s_vt.sem, s_vt.at(l, 2 * hp + h + 1))
                        act.activation(vs[:, 4 * h:4 * h + 4], psum[6][:].rearrange("p (t n) -> p t n", t=4), ACT.Copy).then_inc(s_v.sem, 1)

                    def log_part(n):
                        u = sp_[:, n % 2, :, span(n)[0]:HALF]
                        for j in range(2):
                            act.wait_ge(u_abs.sem, u_abs.at(l, 2 * (NU * hp + n) + j + 1))
                            act.activation(u[:, j], u[:, j], ACT.Exp, scale=-1.0)
                        act.drain()
                        for j in range(2):
                            act.activation(u[:, j], u[:, j], ACT.Ln, bias=1.0).then_inc(u_ln.sem, 1)

                    def hi_part(n):
                        c0, _, _ = span(n)
                        act.wait_ge(u_e.sem, u_e.at(l, 2 * (NU * hp + max(n - 1, 0))))
                        for j in range(2):
                            act.wait_ge(u_sp.sem, u_sp.at(l, 2 * (NU * hp + n) + j + 1))
                            act.activation(sph[:, n % 2, 0, j, c0:HALF], sp_[:, n % 2, j, c0:HALF], ACT.Copy).then_inc(u_hi.sem, 1)

                    def weights(n):
                        c0, _, _ = span(n)
                        act.wait_ge(u_av.sem, u_av.at(l, NU * hp + max(n - 1, 0)))
                        for j in range(2):
                            act.wait_ge(u_e.sem, u_e.at(l, 2 * (NU * hp + n) + j + 1))
                            act.activation(prob[:, n % 2, j, c0:HALF], logits(n)[:, j], ACT.Exp).then_inc(u_prob.sem, 1)

                    def square_out(n):
                        b, k = units[n]
                        if k == 0:
                            act.wait_ge(y_out.sem, y_out.at(l, 2 * hp + b + 1))
                            act.activation(ysq[:].rearrange("p j (t d) -> p j t d", d=HD), y_store(b, hp), ACT.Square).then_inc(y_sq.sem, 1)

                    def root(n):
                        b, k = units[n]
                        if k == 0:
                            act.wait_ge(y_ms.sem, y_ms.at(l, 2 * hp + b + 1))
                            act.activation(yss[:], yss[:], ACT.Ln, bias=eps_c[:, 0:1], scale=1.0 / HD)
                            act.drain()
                            act.activation(yss[:], yss[:], ACT.Exp, scale=-0.5).then_inc(y_rs.sem, 1)

                    for n in range(NU + 5):
                        if 1 < n <= NU:
                            hi_part(n - 1)
                        if 0 <= n - 2 < NU:
                            weights(n - 2)
                        if n == 1:
                            values_turned(1)
                        if n < NU:
                            log_part(n)
                        if n == 0:
                            values_turned(0)
                        if n == 0:
                            hi_part(0)
                            values_out(1, 7)
                        if 0 <= n - 7 < STICK_SLOTS:
                            hi(n - 7, l, use_s[n - 7] + hp + 1, spl[:, n - 7, 0])
                        if 0 <= n - 4 < NU:
                            square_out(n - 4)
                        if 0 <= n - 5 < NU:
                            root(n - 5)
                phase_end(act, "act")
                phase_start(act, l, 4, "pe", "dve", "pool")
                act.dma_start(mlp_gain[:], mlp_norm_g[l].unsqueeze(0).to_broadcast([P, D])).then_inc(gain_loaded, 16)
                for m in range(2 * TT + 1):
                    if m == 2 * TT - 1:
                        act.wait_ge(wo_used.sem, wo_used.at(l, 1))
                        for s in range(GROUP):
                            hi(s, l, use_mlp[s], spl[:, s, 0])
                        turn_hi(l, TT + m - 1, OUT_SEQ[m - 1][1])
                    if m < 2 * TT and OUT_SEQ[m][0] == "n":
                        t = OUT_SEQ[m][1]
                        act.wait_ge(resid_new.sem, resid_new.at(l, t + 1))
                        tile_scale(l, TT + m, t)
                    if m < 2:
                        for s in (2 * m, 2 * m + 1):
                            hi(s, l, use_out[s] + 1, wo_more[:, s, 0])
                    if m >= 1 and m != 2 * TT - 1:
                        turn_hi(l, TT + m - 1, OUT_SEQ[m - 1][1])
                act.wait_ge(out_psum.sem, out_psum.at(l, TT))
                for s in range(GROUP, SLOTS):
                    hi(s, l, use_mlp[s], spl[:, s, 0])
                phase_end(act, "act")
                phase_start(act, l, 5, "pe", "dve")

                def hidden(l, g, buf, more):
                    for i in range(UPS + 1):
                        if i < UPS:
                            act.wait_ge(up_psum.sem, up_psum.at(l, UPS * g + i + 1))
                            if not (more == "first" and i < 2):
                                act.wait_ge(squared.sem, squared.at(l, UPS * g + i - 1))
                            act.activation(h1[:, i % 2], psum[i][:], ACT.Relu).then_inc(relu.sem, 1)
                        if i >= 1:
                            q = i - 1
                            act.wait_ge(squared.sem, squared.at(l, UPS * g + q + 1))
                            act.activation(hid[:, buf, 0, q // 2, (q % 2) * HALF:(q % 2 + 1) * HALF], h2[:, q % 2], ACT.Copy).then_inc(hid_hi_done.sem, 1)
                            if more and q % 2:
                                hi(q // 2, l, use_mlp[q // 2] + g + 1, spl[:, q // 2, 0])

                def next_down(l, g):
                    act.wait_ge(down_psum.sem, down_psum.at(l, 2 * TT * (g + 1)))
                    for s in range(GROUP, SLOTS):
                        hi(s, l, use_mlp[s] + g + 1, spl[:, s, 0])

                hidden(l, 0, 0, "first")
                hidden(l, 1, 1, "yes")
                next_down(l, 0)
                with act.Fori(0, NG // 2 - 2) as m:
                    hidden(l, 2 * m + 2, 0, "yes")
                    next_down(l, 2 * m + 1)
                    hidden(l, 2 * m + 3, 1, "yes")
                    next_down(l, 2 * m + 2)
                hidden(l, NG - 2, 0, "yes")
                next_down(l, NG - 3)
                hidden(l, NG - 1, 1, None)
                for s in range(GROUP, SLOTS):
                    hi(s, l, use_mlp[s] + NG - 1, spl[:, s - GROUP, 0])
                phase_end(act, "act")

        @block.gpsimd
        def _(pool):
            def lo(s, l, n, dst):
                pool.wait_ge(hi_done[s], use(l, s, n) + 1)
                pool.tensor_tensor(dst[:, 1], raw[:, s], dst[:, 0].bitcast(F32), ALU.subtract).then_inc(lo_done[s], 1)

            pool.memset(eps_c[:, 0:1], EPS)
            pool.memset(eps_c[:, 1:2], HD * EPS)
            for s in from_one:
                pool.sem_inc(s, 1)
            pool.drain().then_inc(started, 1)

            def select(dst, value, op, step):
                pool.memset(dst, value)
                pool.drain()
                pool.affine_select(out=dst, in_=dst, compare_op=op, fill=0.0, base=0, pattern=[[step, P]],
                                   channel_multiplier=-step)
                pool.drain()

            select(ident[:], 1.0, ALU.is_equal, 1)
            select(tri_f[:], 1.0, ALU.is_ge, 1)
            select(minus_ones[:], -1.0, ALU.is_ge, -1)
            pool.tensor_copy(suffix[:], minus_ones[:])
            pool.drain()
            select(minus_ones[:], MASKED, ALU.is_ge, -1)
            pool.tensor_copy(after_mask[:], minus_ones[:])
            pool.tensor_copy(ident_b[:], ident[:])
            pool.drain()
            pool.memset(minus_ones[:], -1.0)
            pool.memset(head_ones[:], 0.0)
            pool.drain()
            for j in range(2):
                pool.memset(head_ones[j * HD:(j + 1) * HD, j * HD:(j + 1) * HD], 1.0)
            pool.drain().then_inc(const_done, 1)
            with pool.Fori(0, DEPTH) as l:
                for s in range(2):
                    lo(s, l, use_m[s], spl[:, s])
                pool.wait_ge(wg_hi.sem, wg_hi.at(l, 1))
                pool.tensor_tensor(wg[:, 1], wg_raw[:], wg[:, 0].bitcast(F32), ALU.subtract).then_inc(wg_lo.sem, 1)
                phase_end(pool, "pool")
                for s in range(2, SLOTS):
                    lo(s, l, use_m[s], spl[:, s])
                phase_end(pool, "pool")
                with pool.Fori(0, NPAIR) as hp:
                    pool.wait_ge(nm_loaded, (l * NPAIR + hp + 1) * 16)
                    pool.wait_ge(m_args.sem, m_args.at(l, hp + 1))
                    part(pool)
                    acol = a_col[:].rearrange("p (c h) -> p c h", c=TT)[:, :, bass.ds(2 * hp, 2)]
                    pool.tensor_tensor(nm[:, :, :, 0:P], nm[:, :, :, 0:P], acol.unsqueeze(3).to_broadcast([P, TT, 2, P]), ALU.add)
                    pool.drain()
                    view = nm[:].rearrange("p c j t -> p (c j) t")[:, :, 0:P]
                    pool.affine_select(out=view, in_=view, compare_op=ALU.is_ge, fill=MASKED, base=0,
                                       pattern=[[0, 2 * TT], [1, P]], channel_multiplier=-1).then_inc(m_masked.sem, 1)
                    for s in range(SLOTS):
                        lo(s, l, use_m[s] + hp + 1, spl[:, s])
                    pool.wait_ge(m_yrs.sem, m_yrs.at(l, hp + 1))
                    part(pool)
                    yv = resid[:, :, bass.ds(hp * P, P)].rearrange("p t (j d) -> p t j d", j=2)
                    pool.tensor_tensor(yv, yv, mss[:].rearrange("p (t j) -> p t j", j=2).unsqueeze(3).to_broadcast([P, TT, 2, HD]), ALU.mult)
                    pool.drain()
                    yw = resid[:, :, bass.ds(hp * P, P)]
                    pool.tensor_tensor(yw, yw, og[:], ALU.mult).then_inc(m_gated.sem, 1)
                phase_end(pool, "pool")
                phase_start(pool, l, 3, "pe", "dve", "act")
                with pool.Fori(0, NPAIR) as hp:
                    for n in range(NU):
                        _, k = units[n]
                        c0, c1, diag = span(n)
                        if k:
                            pool.wait_ge(u_sp.sem, u_sp.at(l, 2 * (NU * hp + n + 1)))
                            pool.wait_ge(u_carry.sem, u_carry.at(l, NC * hp + carries(n)))
                            pool.wait_ge(u_e.sem, u_e.at(l, 2 * (NU * hp + n)))
                            part(pool)
                            dst, src = carry[:, (n + 1) % 2], carry[:, n % 2]
                            if diag:
                                ins = pool.tensor_copy(dst[:, :, c0:c1], sp_[:, n % 2, :, c0:c1])
                            if c1 < HALF:
                                ins = pool.tensor_tensor(dst[:, :, c1:HALF], src[:, :, c1:HALF], sp_[:, n % 2, :, c1:HALF], ALU.add)
                            ins.then_inc(u_carry.sem, 1)
                        if 0 <= n - 7 < STICK_SLOTS:
                            lo(n - 7, l, use_s[n - 7] + hp + 1, spl[:, n - 7])
                phase_end(pool, "pool")
                for s in range(SLOTS):
                    lo(s, l, use_out[s] + 1, wo_more[:, s])
                for s in range(SLOTS):
                    lo(s, l, use_mlp[s], spl[:, s])
                phase_end(pool, "pool")
                def hid_lo(l, g, buf, more):
                    for q in range(UPS):
                        pool.wait_ge(hid_hi_done.sem, hid_hi_done.at(l, UPS * g + q + 1))
                        cols = slice((q % 2) * HALF, (q % 2 + 1) * HALF)
                        pool.tensor_tensor(hid[:, buf, 1, q // 2, cols], h2[:, q % 2], hid[:, buf, 0, q // 2, cols].bitcast(F32),
                                           ALU.subtract).then_inc(hid_lo_done.sem, 1)
                        if more and q % 2:
                            lo(q // 2, l, use_mlp[q // 2] + g + 1, spl[:, q // 2])

                def next_down(l, g):
                    for s in range(GROUP, SLOTS):
                        lo(s, l, use_mlp[s] + g + 1, spl[:, s])

                hid_lo(l, 0, 0, True)
                hid_lo(l, 1, 1, True)
                next_down(l, 0)
                with pool.Fori(0, NG // 2 - 2) as m:
                    hid_lo(l, 2 * m + 2, 0, True)
                    next_down(l, 2 * m + 1)
                    hid_lo(l, 2 * m + 3, 1, True)
                    next_down(l, 2 * m + 2)
                hid_lo(l, NG - 2, 0, True)
                next_down(l, NG - 3)
                hid_lo(l, NG - 1, 1, False)
                for s in range(GROUP, SLOTS):
                    lo(s, l, use_mlp[s] + NG - 1, spl[:, s - GROUP])
                phase_end(pool, "pool")

        @block.vector
        def _(dve):
            def turn_lo(l, n, t):
                for b in range(2):
                    dve.wait_ge(turned_hi.sem, turned_hi.at(l, 2 * n + b + 1))
                    cells = (slice(None), slice(4 * b, 4 * b + 4), slice(t * P, (t + 1) * P))
                    dve.tensor_tensor(act_t[:, 1][cells], psum[(2 * n + b) % 4][:].rearrange("p (k n) -> p k n", k=4),
                                      act_t[:, 0][cells].bitcast(F32), ALU.subtract).then_inc(turned_lo.sem, 1)

            def normed_tile(l, n, t, scale_no, gain):
                dve.wait_ge(scale_ready.sem, scale_ready.at(l, scale_no))
                dve.scalar_tensor_tensor(out=turned[:, n % 2], in0=resid[:, t], scalar=rst[:, n % 2:n % 2 + 1],
                                         in1=gain[:], op0=ALU.mult, op1=ALU.mult).then_inc(tile_ready.sem, 1)

            dve.wait_ge(const_done, 1)
            with dve.Fori(0, DEPTH) as l:
                phase_start(dve, l, 0, "pe", "act")
                dve.wait_ge(gain_loaded, (l * 3 + 1) * 16)
                for t in range(TT + 1):
                    if t < TT:
                        normed_tile(l, t, t, t + 1, gain)
                    if t >= 1:
                        turn_lo(l, t - 1, t - 1)
                dve.wait_ge(small_pe.sem, small_pe.at(l, 1))
                dve.tensor_copy(small_cols[:, 0:N_SMALL], psum[7][:, 0:N_SMALL])
                phase_end(dve, "dve")
                phase_start(dve, l, 1, "act")
                dve.wait_ge(small_loaded, (l + 1) * (16 * SMALL_DMAS))
                for b in range(2):
                    dve.memset(cmax[:, b, 0:64], MASKED)
                for h in range(2):
                    dve.wait_ge(gate_pe.sem, gate_pe.at(l, h + 1))
                    dve.tensor_copy(gt[:, h * HALF:(h + 1) * HALF], psum[6 + h][0:2 * NH, :]).then_inc(gate_dve.sem, 1)
                dve.wait_ge(gate_pe.sem, gate_pe.at(l, 3))
                dve.tensor_tensor(gsb[:], psum[4][:, 0:TT * 2 * NH].rearrange("p (t g) -> p t g", t=TT),
                                  gate_bias[:].unsqueeze(1).to_broadcast([P, TT, 2 * NH]), ALU.add)
                dve.drain()
                gf = gsb[:, :, NH:2 * NH]
                dve.tensor_scalar(gabs[:].bitcast(I32), gf.bitcast(I32), NO_SIGN, None, ALU.bitwise_and).then_inc(gate_dve.sem, 1)
                dve.tensor_copy(gi[:], gsb[:, :, 0:NH])
                dve.wait_ge(gate_act.sem, gate_act.at(l, 1))
                dve.scalar_tensor_tensor(out=glog[:], in0=gf, scalar=0.0, in1=gabs[:], op0=ALU.min, op1=ALU.subtract).then_inc(gate_dve.sem, 1)
                dve.wait_ge(gate_pe.sem, gate_pe.at(l, 4))
                dve.tensor_copy(brow[:], psum[5][0:CH, 0:P])
                dve.drain()
                dve.tensor_tensor(arow[:], psum[6][0:CH, 0:P], brow[:], ALU.subtract)
                dve.drain()
                dve.tensor_copy(cmax[:, 0, 64:], arow[:])
                dve.drain()
                for n in range(7):
                    a, b = cmax[:, n % 2], cmax[:, 1 - n % 2]
                    ins = dve.tensor_tensor(b[:, 64:], a[:, 64:], a[:, 64 - 2 ** n:64 + P - 2 ** n], ALU.max)
                    if n < 6:
                        dve.drain()
                ins.then_inc(gate_dve.sem, 1)
                dve.wait_ge(gate_pe.sem, gate_pe.at(l, 5))
                dve.tensor_copy(lastv[:].rearrange("p a n -> p (a n)"), psum[7][0:1, 0:2 * CH])
                dve.memset(mprev[:, 0:NH], 0.0)
                dve.drain()
                for c in range(TT - 1):
                    cur, nxt = mprev[:, c * NH:(c + 1) * NH], mprev[:, (c + 1) * NH:(c + 2) * NH]
                    dve.tensor_tensor(nxt, cur, lastv[:, 1, c * NH:(c + 1) * NH], ALU.max)
                    dve.drain()
                    ins = dve.tensor_tensor(nxt, nxt, lastv[:, 0, c * NH:(c + 1) * NH], ALU.add)
                    if c < TT - 2:
                        dve.drain()
                ins.then_inc(gate_dve.sem, 1)
                dve.wait_ge(gate_pe.sem, gate_pe.at(l, 6))
                dve.tensor_copy(mpcol[:], psum[4][0:CH, 0:1])
                dve.drain()
                dve.tensor_scalar(nrow[:, 0:P], cmax[:, 1, 64:], mpcol[:, 0:1], -1.0, ALU.max, ALU.mult)
                dve.tensor_copy(nrow[:, P:P + 1], mpcol[:])
                dve.drain()
                dve.tensor_tensor(frow[:], nrow[:, 0:P], brow[:], ALU.subtract).then_inc(gate_dve.sem, 1)
                dve.wait_ge(gate_pe.sem, gate_pe.at(l, 7))
                dve.wait_ge(gate_act.sem, gate_act.at(l, 2))
                dve.tensor_copy(a_col[:], psum[5][:, 0:CH])
                phase_end(dve, "dve")
                phase_start(dve, l, 2, "pe", "act")
                dve.wait_ge(resid_stored, (l + 1) * 16)
                dve.memset(pre[:, 0:CW - 1], 0.0)
                dve.memset(vm[:, :, :, HD:VW], 1.0)
                dve.memset(state[:], 0.0)
                dve.drain()
                with dve.Fori(0, NPAIR) as hp:
                    def absolute(src):
                        dve.tensor_scalar(sig[:].bitcast(I32), src.bitcast(I32), NO_SIGN, None, ALU.bitwise_and).then_inc(m_abs.sem, 1)

                    def log_sigmoid(w, dst, u):
                        dve.wait_ge(m_ln.sem, m_ln.at(l, 3 * hp + w + 1))
                        dve.scalar_tensor_tensor(out=dst, in0=u, scalar=0.0, in1=sig[:], op0=ALU.min, op1=ALU.subtract).then_inc(m_log.sem, 1)

                    for w, dst in ((0, qm), (1, km)):
                        dve.wait_ge(m_evac.sem, m_evac.at(l, 8 * hp + 2 * w + 2))

                        def tap(j):
                            return small_cols[:, bass.ds(ROW_W + j * KT + w * NPAIR + hp, 1)]

                        dve.tensor_scalar(dst[:], pre[:, 0:SEQ], tap(0), small_cols[:, bass.ds(ROW_B + w * NPAIR + hp, 1)],
                                          ALU.mult, ALU.add)
                        for j in range(1, CW):
                            dve.drain()
                            ins = dve.scalar_tensor_tensor(out=dst[:], in0=pre[:, j:j + SEQ], scalar=tap(j), in1=dst[:],
                                                           op0=ALU.mult, op1=ALU.add)
                        ins.then_inc(m_conv.sem, 1)
                        dve.drain()
                        absolute(dst[:])
                        if w == 0:
                            dve.wait_ge(nm_loaded, (l * NPAIR + hp + 1) * 16)
                            for j in range(2):
                                hs = slice(j * HD, (j + 1) * HD)
                                dve.tensor_tensor(qs[hs], nm[hs, :, j, 0:P], nm[hs, :, j, P:P + 1].to_broadcast([HD, TT, P]), ALU.add)
                            dve.tensor_tensor(dec[:], nm[:, :, :, P - 1], nm[:, :, :, P], ALU.add).then_inc(m_args.sem, 1)
                        log_sigmoid(w, sig[:], dst[:])
                        dve.wait_ge(m_sig.sem, m_sig.at(l, 3 * hp + w + 1))
                        dve.scalar_tensor_tensor(out=dst[:], in0=dst[:], scalar=QSC if w == 0 else 1.0, in1=sig[:],
                                                 op0=ALU.mult, op1=ALU.mult).then_inc(m_qk.sem, 1)
                    dve.drain()
                    dve.wait_ge(m_exp.sem, m_exp.at(l, 2 * hp + 2))
                    dve.tensor_tensor(qs[:], qs[:], qm[:].rearrange("p (c t) -> p c t", c=TT), ALU.mult).then_inc(m_qs.sem, 1)
                    for b in range(2):
                        dve.wait_ge(m_kt.sem, m_kt.at(l, 2 * hp + b + 1))
                        for j in range(2):
                            ins = dve.tensor_tensor(kw[:, 4 * b:4 * b + 4, j * HD:(j + 1) * HD],
                                                    psum[b][:].rearrange("p (c n) -> p c n", c=4)[:, :, j * HD:(j + 1) * HD],
                                                    nm[:, 4 * b:4 * b + 4, j, P - 1:P].to_broadcast([P, 4, HD]), ALU.mult)
                    ins.then_inc(m_kw.sem, 1)
                    dve.drain()

                    def weigh(b):
                        dve.wait_ge(m_s.sem, m_s.at(l, 2 * hp + b + 1))
                        d = nm[:, 4 * b:4 * b + 4, :, 0:P]
                        dve.tensor_tensor(d, banks[:, 2:4].rearrange("p j (c t) -> p c j t", c=4), d, ALU.mult).then_inc(m_w.sem, 1)

                    weigh(0)
                    dve.wait_ge(m_evac.sem, m_evac.at(l, 8 * hp + 8))
                    absolute(og[:].rearrange("p t n -> p (t n)"))
                    for c in range(1, TT):
                        a, bank = UPD_BANK[c - 1]
                        if c == TT - 1:
                            weigh(1)
                        if c - 1 == a:
                            dve.wait_ge(m_u.sem, m_u.at(l, 3 * hp + a // 3 + 1))
                        for j in range(2):
                            hs = slice(j * HD, (j + 1) * HD)
                            upd = psum[bank][hs, ((c - 1 - a) * 2 + j) * VW:((c - 1 - a) * 2 + j + 1) * VW]
                            new = state[hs, c - 1, j * VW:(j + 1) * VW]
                            if c == 1:
                                ins = dve.tensor_copy(new, upd)
                            else:
                                ins = dve.scalar_tensor_tensor(out=new, in0=state[hs, c - 2, j * VW:(j + 1) * VW],
                                                               scalar=dec[hs, c - 1, j:j + 1], in1=upd, op0=ALU.mult, op1=ALU.add)
                        ins.then_inc(m_state.sem, 1)
                        dve.drain()
                    log_sigmoid(2, og[:].rearrange("p t n -> p (t n)"), og[:].rearrange("p t n -> p (t n)"))
                    floors = floor_col[:].rearrange("p (c h) -> p c h", c=TT)
                    for i, (a, e, bank) in enumerate(NUM_BANKS):
                        dve.wait_ge(m_num.sem, m_num.at(l, 3 * hp + i + 1))
                        num = psum[bank][:, 0:(e - a) * 2 * VW].rearrange("p (c j v) -> p c j v", j=2, v=VW)
                        dve.tensor_scalar(dd[:, a:e].bitcast(I32), num[:, :, :, HD].bitcast(I32), NO_SIGN, None, ALU.bitwise_and)
                        dve.drain()
                        dve.tensor_tensor(dd[:, a:e], dd[:, a:e], floors[:, a:e, bass.ds(2 * hp, 2)], ALU.max)
                        dve.drain()
                        dve.reciprocal(dd[:, a:e], dd[:, a:e])
                        dve.drain()
                        dve.tensor_tensor(resid[:, a:e, bass.ds(hp * P, P)].rearrange("p c (j d) -> p c j d", j=2), num[:, :, :, 0:HD],
                                          dd[:, a:e].unsqueeze(3).to_broadcast([P, e - a, 2, HD]), ALU.mult).then_inc(m_y.sem, 1)
                    dve.wait_ge(m_ysq.sem, m_ysq.at(l, hp + 1))
                    dve.wait_ge(m_gated.sem, m_gated.at(l, hp))
                    dve.tensor_reduce(mss[:], pre[:, CW - 1:].rearrange("p (n d) -> p n d", d=HD), AX.X, ALU.add).then_inc(m_yms.sem, 1)
                phase_end(dve, "dve")
                phase_start(dve, l, 3, "pe", "act", "pool")
                with dve.Fori(0, NPAIR) as hp:
                    for n in range(4):
                        dve.wait_ge(s_rs.sem, s_rs.at(l, 4 * hp + n + 1))
                        row = ROW_Q if n < 2 else ROW_K
                        dve.scalar_tensor_tensor(out=qkt[:, n // 2, (n % 2) * HALF:(n % 2 + 1) * HALF], in0=psum[n][:],
                                                 scalar=small_cols[:, row:row + 1], in1=rs[:, n % 2], op0=ALU.mult, op1=ALU.mult).then_inc(s_qk.sem, 1)

                    def absolute(n):
                        dve.wait_ge(u_z.sem, u_z.at(l, NU * hp + n + 1))
                        if n == 1:
                            dve.wait_ge(s_vt.sem, s_vt.at(l, 2 * hp + 2))
                        dve.wait_ge(u_carry.sem, u_carry.at(l, NC * hp + carries(n - 1)))
                        for j in range(2):
                            dve.tensor_scalar(sp_[:, n % 2, j, span(n)[0]:HALF].bitcast(I32), logits(n)[:, j].bitcast(I32), NO_SIGN, None,
                                              ALU.bitwise_and).then_inc(u_abs.sem, 1)

                    def softplus(n):
                        for j in range(2):
                            dve.wait_ge(u_ln.sem, u_ln.at(l, 2 * (NU * hp + n) + j + 1))
                            u = sp_[:, n % 2, j, span(n)[0]:HALF]
                            dve.scalar_tensor_tensor(out=u, in0=logits(n)[:, j], scalar=0.0, in1=u, op0=ALU.max,
                                                     op1=ALU.add).then_inc(u_sp.sem, 1)

                    def lo_part(n):
                        c0, _, _ = span(n)
                        for j in range(2):
                            dve.wait_ge(u_hi.sem, u_hi.at(l, 2 * (NU * hp + n) + j + 1))
                            dve.tensor_tensor(sph[:, n % 2, 1, j, c0:HALF], sp_[:, n % 2, j, c0:HALF],
                                              sph[:, n % 2, 0, j, c0:HALF].bitcast(F32), ALU.subtract).then_inc(u_lo.sem, 1)

                    def store(n):
                        b, k = units[n]
                        if k == 0:
                            dve.wait_ge(u_av.sem, u_av.at(l, NU * hp + n + 1))
                            dve.tensor_copy(y_store(b, hp), banks[:, 4:6, 0:SBLK * HD].rearrange("p j (t d) -> p j t d", d=HD)).then_inc(y_out.sem, 1)

                    def mean(n):
                        b, k = units[n]
                        if k == 0:
                            dve.wait_ge(y_sq.sem, y_sq.at(l, 2 * hp + b + 1))
                            dve.tensor_reduce(yss[:], ysq[:].rearrange("p j (t d) -> p (j t) d", d=HD), AX.X, ALU.add).then_inc(y_ms.sem, 1)

                    def norm(n):
                        b, k = units[n]
                        if k == 0:
                            dve.wait_ge(y_rs.sem, y_rs.at(l, 2 * hp + b + 1))
                            dve.tensor_tensor(y_store(b, hp), y_store(b, hp),
                                              yss[:].rearrange("p (j t) -> p j t", j=2).unsqueeze(3).to_broadcast([P, 2, SBLK, HD]), ALU.mult)

                    for n in range(NU + 6):
                        if 0 <= n - 1 < NU:
                            lo_part(n - 1)
                        if n < NU:
                            absolute(n)
                            softplus(n)
                        if 0 <= n - 3 < NU:
                            store(n - 3)
                        if 0 <= n - 4 < NU:
                            mean(n - 4)
                        if 0 <= n - 6 < NU:
                            norm(n - 6)
                phase_end(dve, "dve")
                phase_start(dve, l, 4, "pe", "act", "pool")
                dve.wait_ge(gain_loaded, (l * 3 + 2) * 16)
                for m in range(2 * TT + 1):
                    if m == 2 * TT - 1:
                        turn_lo(l, TT + m - 1, OUT_SEQ[m - 1][1])
                    if m < 2 * TT:
                        kind, t = OUT_SEQ[m]
                        if kind == "y":
                            if m >= 2:
                                dve.wait_ge(tile_turned.sem, tile_turned.at(l, 2 * (TT + m - 1)))
                            dve.tensor_tensor(turned[:, m % 2], resid[:, t], gain[:], ALU.mult).then_inc(tile_ready.sem, 1)
                        else:
                            dve.wait_ge(rt_loaded[t % 2], (l * (TT // 2) + t // 2 + 1) * 16)
                            dve.wait_ge(out_psum.sem, out_psum.at(l, t + 1))
                            b = 4 + 2 * (t % 2)
                            dve.tensor_tensor(resid[:, t].rearrange("p (h n) -> p h n", h=2), banks[:, b:b + 2],
                                              rtile[:, t % 2].rearrange("p (h n) -> p h n", h=2), ALU.add).then_inc(resid_new.sem, 1)
                            if t == 0:
                                dve.wait_ge(gain_loaded, (l * 3 + 3) * 16)
                            normed_tile(l, TT + m, t, TT + t + 1, mlp_gain)
                    if m >= 1 and m != 2 * TT - 1:
                        turn_lo(l, TT + m - 1, OUT_SEQ[m - 1][1])
                phase_end(dve, "dve")
                phase_start(dve, l, 5, "pe", "act", "pool")

                def square(l, g, first):
                    for i in range(UPS):
                        dve.wait_ge(relu.sem, relu.at(l, UPS * g + i + 1))
                        if not (first and i < 2):
                            dve.wait_ge(hid_lo_done.sem, hid_lo_done.at(l, UPS * g + i - 1))
                        dve.scalar_tensor_tensor(out=h2[:, i % 2], in0=psum[i][:], scalar=0.0, in1=h1[:, i % 2],
                                                 op0=ALU.max, op1=ALU.mult).then_inc(squared.sem, 1)

                def add(l, g):
                    for i in range(2 * TT):
                        dve.wait_ge(down_psum.sem, down_psum.at(l, 2 * TT * g + i + 1))
                        r = resid[:, i // 2, (i % 2) * HALF:(i % 2 + 1) * HALF]
                        dve.tensor_tensor(r, psum[4 + i % 4][:], r, ALU.add).then_inc(down_add.sem, 1)

                square(l, 0, True)
                square(l, 1, False)
                add(l, 0)
                with dve.Fori(0, NG // 2 - 1) as m:
                    square(l, 2 * m + 2, False)
                    add(l, 2 * m + 1)
                    square(l, 2 * m + 3, False)
                    add(l, 2 * m + 2)
                add(l, NG - 1)
                phase_end(dve, "dve")


_INS = ["x", "attn_norm_g", "w_in", "conv_w", "conv_b", "b_igate", "b_fgate", "q_norm_g", "k_norm_g", "out_norm_g",
        "w_out", "mlp_norm_g", "w_up", "w_down"]


def kernel(**inputs):
    import numpy as np
    import concourse.bacc as bacc
    from concourse.bass_utils import run_bass_kernel_spmd

    nc = bacc.Bacc("TRN2", target_bir_lowering=False, num_devices=1)
    arrays, args = {}, []
    for name in _INS:
        a = np.ascontiguousarray(inputs[name])
        arrays[f"in_{name}"] = a
        args.append(nc.dram_tensor(f"in_{name}", a.shape, mybir.dt.from_np(a.dtype), kind="ExternalInput").ap())
    out = nc.dram_tensor("out_x", inputs["x"].shape, F32, kind="ExternalOutput").ap()
    trunk(nc, *args, out)
    r = run_bass_kernel_spmd(nc, [arrays], core_ids=[0])
    return r.results[0]["out_x"]
```
